# Optimizing a Trainium2 kernel written in Bass

```python
import math
import jax, jax.numpy as jnp
from jax import lax
import numpy as np

D_MODEL = 1024
BATCH = 1
SEQ = 256
DEPTH = 4

CHUNK = 64
N_MIXERS = 3
D_FF = 4 * D_MODEL
NORM_EPS = 1e-6
GDN_HEADS = 8
GDN_DK = D_MODEL // GDN_HEADS
GDN_DV = D_MODEL // GDN_HEADS
GDN_CONV = 4
GDN_QKV = GDN_HEADS * (2 * GDN_DK + GDN_DV)
GDN_IN = GDN_QKV + GDN_HEADS * GDN_DV + 2 * GDN_HEADS
MLSTM_HEADS = 8
MLSTM_DV = D_MODEL // MLSTM_HEADS
MLSTM_DK = MLSTM_DV // 2
GATE_CAP = 15.0
MLSTM_IN = MLSTM_HEADS * (2 * MLSTM_DK + 2 * MLSTM_DV) + 2 * MLSTM_HEADS
DIFF_HEADS = 8
DIFF_D = D_MODEL // (2 * DIFF_HEADS)
ROPE_THETA = 500000.0
ROT_DIMS = DIFF_D // 4
Q_BLOCK = 128
N_GDN = (DEPTH + 2) // 3
N_MLSTM = (DEPTH + 1) // 3
N_DIFF = DEPTH // 3


def rms_norm(x, g):
    xf = x.astype(jnp.float32)
    y = xf * lax.rsqrt(jnp.mean(xf * xf, axis=-1, keepdims=True) + NORM_EPS)
    return (y * g.astype(jnp.float32)).astype(x.dtype)

def l2_norm(x):
    xf = x.astype(jnp.float32)
    return xf * lax.rsqrt(jnp.sum(xf * xf, axis=-1, keepdims=True) + NORM_EPS)

def soft_cap(x):
    return GATE_CAP * jnp.tanh(x / GATE_CAP)

def to_chunks(x):
    b, t, h = x.shape[:3]
    x = x.reshape((b, t // CHUNK, CHUNK, h) + x.shape[3:])
    return jnp.swapaxes(jnp.moveaxis(x, 1, 0), 2, 3)

def from_chunks(x):
    n, b, h, c, d = x.shape
    return jnp.moveaxis(jnp.swapaxes(x, 2, 3), 0, 1).reshape(b, n * c, h, d)

def causal_conv(x, w):
    width, t = w.shape[0], x.shape[1]
    xp = jnp.pad(x, ((0, 0), (width - 1, 0), (0, 0)))
    return sum(xp[:, j:j + t] * w[j] for j in range(width))

def partial_rope(x, cos, sin):
    shp = (1, x.shape[1]) + (1,) * (x.ndim - 3) + (ROT_DIMS // 2,)
    c, s = cos.reshape(shp), sin.reshape(shp)
    x1, x2, rest = x[..., :ROT_DIMS // 2], x[..., ROT_DIMS // 2:ROT_DIMS], x[..., ROT_DIMS:]
    return jnp.concatenate([x1 * c - x2 * s, x1 * s + x2 * c, rest], axis=-1)

def gated_delta_rule(q, k, v, g, beta):
    dk, dv = q.shape[-1], v.shape[-1]
    qc = to_chunks(q * dk ** -0.5)
    kc = to_chunks(k)
    vc = to_chunks(v.astype(jnp.float32))
    gc = jnp.cumsum(to_chunks(g.astype(jnp.float32)), axis=-1)
    bc = to_chunks(beta.astype(jnp.float32))
    tril = jnp.tril(jnp.ones((CHUNK, CHUNK), bool))
    strict = jnp.tril(jnp.ones((CHUNK, CHUNK), bool), -1)
    diff = gc[..., :, None] - gc[..., None, :]
    decay = jnp.where(tril, jnp.exp(jnp.where(tril, diff, 0.0)), 0.0)
    kb = kc * bc[..., None]
    a_mat = jnp.where(strict, jnp.einsum('nbhid,nbhjd->nbhij', kb, kc) * decay, 0.0)
    t_mat = a_mat + jnp.eye(CHUNK, dtype=jnp.float32)
    rhs = jnp.concatenate([vc * bc[..., None], kb * jnp.exp(gc)[..., None]], axis=-1)
    sol = lax.linalg.triangular_solve(t_mat, rhs, left_side=True, lower=True, unit_diagonal=True)
    value, kcd = sol[..., :dv], sol[..., dv:]
    attn = jnp.einsum('nbhid,nbhjd->nbhij', qc, kc) * decay
    q_inter = qc * jnp.exp(gc)[..., None]
    g_last = gc[..., -1]
    k_state = kc * jnp.exp(g_last[..., None] - gc)[..., None]

    def step(s_st, xs):
        qi, kcd_i, val_i, attn_i, kst_i, gl_i = xs
        v_new = val_i - jnp.einsum('bhck,bhkv->bhcv', kcd_i, s_st)
        o = jnp.einsum('bhck,bhkv->bhcv', qi, s_st) + jnp.einsum('bhcs,bhsv->bhcv', attn_i, v_new)
        s_st = s_st * jnp.exp(gl_i)[..., None, None] + jnp.einsum('bhck,bhcv->bhkv', kst_i, v_new)
        return s_st, o

    s0 = jnp.zeros(qc.shape[1:3] + (dk, dv), jnp.float32)
    _, o = lax.scan(step, s0, (q_inter, kcd, value, attn, k_state, g_last))
    return from_chunks(o)

def gdn_mixer(h, w_in, conv_w, a_log, dt_bias, norm_g, w_out):
    b, t, _ = h.shape
    proj = h @ w_in
    qkv = jax.nn.silu(causal_conv(proj[..., :GDN_QKV], conv_w))
    z = proj[..., GDN_QKV:GDN_QKV + GDN_HEADS * GDN_DV].reshape(b, t, GDN_HEADS, GDN_DV)
    a = proj[..., GDN_QKV + GDN_HEADS * GDN_DV:GDN_IN - GDN_HEADS]
    bt = proj[..., GDN_IN - GDN_HEADS:]
    hk = GDN_HEADS * GDN_DK
    q = l2_norm(qkv[..., :hk].reshape(b, t, GDN_HEADS, GDN_DK))
    k = l2_norm(qkv[..., hk:2 * hk].reshape(b, t, GDN_HEADS, GDN_DK))
    v = qkv[..., 2 * hk:].reshape(b, t, GDN_HEADS, GDN_DV)
    g = -jnp.exp(a_log.astype(jnp.float32)) * jax.nn.softplus((a + dt_bias).astype(jnp.float32))
    beta = jax.nn.sigmoid(bt.astype(jnp.float32))
    o = gated_delta_rule(q, k, v, g, beta)
    o = rms_norm(o, norm_g) * jax.nn.silu(z.astype(jnp.float32))
    return o.reshape(b, t, GDN_HEADS * GDN_DV).astype(h.dtype) @ w_out

def mlstm_chunkwise(q, k, v, i_pre, f_pre):
    dk, dv = q.shape[-1], v.shape[-1]
    qc = to_chunks(q.astype(jnp.float32) * dk ** -0.5)
    kc = to_chunks(k.astype(jnp.float32))
    vc = to_chunks(v.astype(jnp.float32))
    lfc = to_chunks(jax.nn.log_sigmoid(f_pre.astype(jnp.float32)))
    ic = to_chunks(i_pre.astype(jnp.float32))
    tril = jnp.tril(jnp.ones((CHUNK, CHUNK), bool))

    def step(carry, xs):
        c_st, n_st, m_st = carry
        q_, k_, v_, lf, ig = xs
        bcum = jnp.cumsum(lf, axis=-1)
        g = bcum[..., -1]
        dlog = jnp.where(tril, bcum[..., :, None] - bcum[..., None, :] + ig[..., None, :], -jnp.inf)
        m_inter = bcum + m_st[..., None]
        m_out = jnp.maximum(m_inter, jnp.max(dlog, axis=-1))
        w_inter = jnp.exp(m_inter - m_out)
        s = jnp.einsum('bhtd,bhsd->bhts', q_, k_) * jnp.exp(dlog - m_out[..., None])
        num = w_inter[..., None] * jnp.einsum('bhtd,bhde->bhte', q_, c_st) + jnp.einsum('bhts,bhse->bhte', s, v_)
        den = w_inter * jnp.einsum('bhtd,bhd->bht', q_, n_st) + jnp.sum(s, axis=-1)
        h_ = num / jnp.maximum(jnp.abs(den), jnp.exp(-m_out))[..., None]
        a = g[..., None] - bcum + ig
        m_new = jnp.maximum(g + m_st, jnp.max(a, axis=-1))
        w_old = jnp.exp(g + m_st - m_new)
        kw = k_ * jnp.exp(a - m_new[..., None])[..., None]
        c_new = w_old[..., None, None] * c_st + jnp.einsum('bhsd,bhse->bhde', kw, v_)
        n_new = w_old[..., None] * n_st + jnp.sum(kw, axis=-2)
        return (c_new, n_new, m_new), h_

    bh = qc.shape[1:3]
    init = (jnp.zeros(bh + (dk, dv), jnp.float32), jnp.zeros(bh + (dk,), jnp.float32),
            jnp.zeros(bh, jnp.float32))
    _, hs = lax.scan(step, init, (qc, kc, vc, lfc, ic))
    return from_chunks(hs)

def mlstm_mixer(h, w_in, gate_b, norm_g, w_out):
    b, t, _ = h.shape
    proj = h @ w_in
    hk, hv = MLSTM_HEADS * MLSTM_DK, MLSTM_HEADS * MLSTM_DV
    q = proj[..., :hk].reshape(b, t, MLSTM_HEADS, MLSTM_DK)
    k = proj[..., hk:2 * hk].reshape(b, t, MLSTM_HEADS, MLSTM_DK)
    v = proj[..., 2 * hk:2 * hk + hv].reshape(b, t, MLSTM_HEADS, MLSTM_DV)
    o_gate = proj[..., 2 * hk + hv:2 * hk + 2 * hv]
    i_pre = soft_cap(proj[..., MLSTM_IN - 2 * MLSTM_HEADS:MLSTM_IN - MLSTM_HEADS] + gate_b[0])
    f_pre = soft_cap(proj[..., MLSTM_IN - MLSTM_HEADS:] + gate_b[1])
    hc = mlstm_chunkwise(q, k, v, i_pre, f_pre)
    hn = rms_norm(hc, norm_g.reshape(MLSTM_HEADS, MLSTM_DV)).reshape(b, t, hv)
    return (jax.nn.sigmoid(o_gate.astype(jnp.float32)) * hn).astype(h.dtype) @ w_out

def diff_attention(q, k, v, lam):
    b, t, h, _, d = q.shape
    nq = t // Q_BLOCK
    qf = jnp.moveaxis((q.astype(jnp.float32) * d ** -0.5).reshape(b, nq, Q_BLOCK, h, 2, d), 1, 0)
    kf, vf = k.astype(jnp.float32), v.astype(jnp.float32)
    key_chunk = jnp.arange(t) // CHUNK

    def one_block(args):
        qb, idx = args
        q_chunk = (idx * Q_BLOCK + jnp.arange(Q_BLOCK)) // CHUNK
        s = jnp.einsum('bqhcd,bkhcd->bhcqk', qb, kf)
        mask = key_chunk[None, :] <= q_chunk[:, None]
        p = jax.nn.softmax(jnp.where(mask, s, -jnp.inf), axis=-1)
        attn = p[:, :, 0] - lam * p[:, :, 1]
        return jnp.einsum('bhqk,bkhe->bqhe', attn, vf)

    o = lax.map(one_block, (qf, jnp.arange(nq)))
    return jnp.moveaxis(o, 0, 1).reshape(b, t, h, 2 * d)

def diff_mixer(h, w_in, lam_p, norm_g, w_out, lambda_init, cos, sin):
    b, t, _ = h.shape
    proj = h @ w_in
    hq = DIFF_HEADS * 2 * DIFF_D
    q = partial_rope(proj[..., :hq].reshape(b, t, DIFF_HEADS, 2, DIFF_D), cos, sin)
    k = partial_rope(proj[..., hq:2 * hq].reshape(b, t, DIFF_HEADS, 2, DIFF_D), cos, sin)
    v = proj[..., 2 * hq:].reshape(b, t, DIFF_HEADS, 2 * DIFF_D)
    lp = lam_p.astype(jnp.float32)
    lam = jnp.exp(jnp.sum(lp[0] * lp[1])) - jnp.exp(jnp.sum(lp[2] * lp[3])) + lambda_init
    o = diff_attention(q, k, v, lam)
    o = rms_norm(o, norm_g) * (1.0 - lambda_init)
    return o.reshape(b, t, hq).astype(h.dtype) @ w_out

def sq_relu_mlp(h, w1, w2):
    return jnp.square(jax.nn.relu(h @ w1)) @ w2

def first_inputs(seed: int = 0) -> dict:
    key = jax.random.key(seed)
    ks = jax.random.split(key, 18)
    nrm = lambda k, shape, scale: jax.random.normal(k, shape, jnp.float32) * scale
    return {
        "x": nrm(ks[0], (BATCH, SEQ, D_MODEL), 1.0),
        "norm_g": 1.0 + nrm(ks[1], (DEPTH, 4, D_MODEL), 0.05),
        "mlp_w1": nrm(ks[2], (DEPTH, D_MODEL, D_FF), D_MODEL ** -0.5),
        "mlp_w2": nrm(ks[3], (DEPTH, D_FF, D_MODEL), D_FF ** -0.5),
        "gdn_w_in": nrm(ks[4], (N_GDN, D_MODEL, GDN_IN), D_MODEL ** -0.5),
        "gdn_conv": nrm(ks[5], (N_GDN, GDN_CONV, GDN_QKV), GDN_CONV ** -0.5),
        "gdn_a_log": jnp.log(jax.random.uniform(ks[6], (N_GDN, GDN_HEADS), jnp.float32, 1.0, 16.0)),
        "gdn_dt_bias": -4.0 + nrm(ks[7], (N_GDN, GDN_HEADS), 0.5),
        "gdn_norm_g": 1.0 + nrm(ks[8], (N_GDN, GDN_DV), 0.05),
        "gdn_w_out": nrm(ks[9], (N_GDN, GDN_HEADS * GDN_DV, D_MODEL), (GDN_HEADS * GDN_DV) ** -0.5),
        "mlstm_w_in": nrm(ks[10], (N_MLSTM, D_MODEL, MLSTM_IN), D_MODEL ** -0.5),
        "mlstm_gate_b": jnp.array([[-1.0], [3.0]], jnp.float32) + nrm(ks[11], (N_MLSTM, 2, MLSTM_HEADS), 0.1),
        "mlstm_norm_g": 1.0 + nrm(ks[12], (N_MLSTM, MLSTM_HEADS * MLSTM_DV), 0.05),
        "mlstm_w_out": nrm(ks[13], (N_MLSTM, MLSTM_HEADS * MLSTM_DV, D_MODEL), (MLSTM_HEADS * MLSTM_DV) ** -0.5),
        "diff_w_in": nrm(ks[14], (N_DIFF, D_MODEL, 3 * DIFF_HEADS * 2 * DIFF_D), D_MODEL ** -0.5),
        "diff_lambda": nrm(ks[15], (N_DIFF, 4, DIFF_D), 0.1),
        "diff_norm_g": 1.0 + nrm(ks[16], (N_DIFF, 2 * DIFF_D), 0.05),
        "diff_w_out": nrm(ks[17], (N_DIFF, DIFF_HEADS * 2 * DIFF_D, D_MODEL), (DIFF_HEADS * 2 * DIFF_D) ** -0.5),
    }

def first_block(x, norm_g, mlp_w1, mlp_w2, gdn_w_in, gdn_conv, gdn_a_log, gdn_dt_bias, gdn_norm_g,
              gdn_w_out, mlstm_w_in, mlstm_gate_b, mlstm_norm_g, mlstm_w_out, diff_w_in,
              diff_lambda, diff_norm_g, diff_w_out):
    t = x.shape[1]
    inv_freq = ROPE_THETA ** (-jnp.arange(0, ROT_DIMS, 2, dtype=jnp.float32) / ROT_DIMS)
    ang = jnp.arange(t, dtype=jnp.float32)[:, None] * inv_freq[None, :]
    cos, sin = jnp.cos(ang).astype(x.dtype), jnp.sin(ang).astype(x.dtype)
    for i in range(DEPTH):
        kind, j = i % N_MIXERS, i // N_MIXERS
        h = rms_norm(x, norm_g[i, 0])
        if kind == 0:
            m = gdn_mixer(h, gdn_w_in[j], gdn_conv[j], gdn_a_log[j], gdn_dt_bias[j], gdn_norm_g[j], gdn_w_out[j])
        elif kind == 1:
            m = mlstm_mixer(h, mlstm_w_in[j], mlstm_gate_b[j], mlstm_norm_g[j], mlstm_w_out[j])
        else:
            lambda_init = 0.8 - 0.6 * math.exp(-0.3 * i)
            m = diff_mixer(h, diff_w_in[j], diff_lambda[j], diff_norm_g[j], diff_w_out[j], lambda_init, cos, sin)
        x = x + rms_norm(m, norm_g[i, 1])
        h = rms_norm(x, norm_g[i, 2])
        x = x + rms_norm(sq_relu_mlp(h, mlp_w1[i], mlp_w2[i]), norm_g[i, 3])
    return x


DEPTH_2 = 2

N_MEM = 256
D_MIX = D_MODEL
HGRN_DK = 128
HGRN_DV = 128
HGRN_WIDTH = D_MIX // 2
HGRN_HEADS = HGRN_WIDTH // HGRN_DV
HGRN_KW = HGRN_HEADS * HGRN_DK
FOX_DH = 64
FOX_WIDTH = D_MIX - HGRN_WIDTH
FOX_HEADS = FOX_WIDTH // FOX_DH
D_FF_2 = 2816
CROSS_HEADS = 4
CROSS_DH = D_MODEL // CROSS_HEADS
EPS = 1e-6
N_IN = 2 * HGRN_KW + 2 * HGRN_WIDTH + 3 * FOX_WIDTH + FOX_HEADS


def rms_norm_2(x, w):
    x32 = x.astype(jnp.float32)
    y = x32 * lax.rsqrt(jnp.mean(x32 * x32, axis=-1, keepdims=True) + EPS)
    return (y * w.astype(jnp.float32)).astype(x.dtype)

def swiglu(h, w_gate, w_up, w_down):
    return (jax.nn.silu(h @ w_gate) * (h @ w_up)) @ w_down

def hgrn2_chunk_scan(q, k, v, logf):
    B, H, S, DK = q.shape
    DV = v.shape[-1]
    nc = S // CHUNK

    def to_chunks(t):
        return t.reshape(B, H, nc, CHUNK, t.shape[-1]).transpose(2, 0, 1, 3, 4)

    qc, kc, vc = to_chunks(q), to_chunks(k), to_chunks(v)
    gc = jnp.cumsum(to_chunks(logf), axis=-2)
    mask = jnp.tril(jnp.ones((CHUNK, CHUNK), dtype=bool))[None, None, :, :, None]

    def step(state, inp):
        q_, k_, v_, g_ = inp
        o_inter = jnp.einsum('bhtk,bhkv->bhtv', q_ * jnp.exp(g_), state)
        diff = g_[:, :, :, None, :] - g_[:, :, None, :, :]
        decay = jnp.exp(jnp.where(mask, diff, -jnp.inf))
        a = jnp.einsum('bhtk,bhsk,bhtsk->bhts', q_, k_, decay)
        o = o_inter + jnp.einsum('bhts,bhsv->bhtv', a, v_)
        g_last = g_[:, :, -1:, :]
        new_state = jnp.exp(g_last[:, :, 0, :])[..., None] * state + jnp.einsum(
            'bhsk,bhsv->bhkv', k_ * jnp.exp(g_last - g_), v_)
        return new_state, o

    s0 = jnp.zeros((B, H, DK, DV), jnp.float32)
    _, oc = lax.scan(step, s0, (qc, kc, vc, gc))
    return oc.transpose(1, 2, 0, 3, 4).reshape(B, H, S, DV)

def forgetting_attention(q, k, v, logf):
    B, H, S, dh = q.shape
    nb = S // Q_BLOCK
    c = jnp.cumsum(logf, axis=-1)
    qb = q.reshape(B, H, nb, Q_BLOCK, dh).transpose(2, 0, 1, 3, 4)
    cb = c.reshape(B, H, nb, Q_BLOCK).transpose(2, 0, 1, 3)
    kpos = jnp.arange(S)
    scale = dh ** -0.5

    def block(args):
        q_blk, c_blk, i = args
        s = jnp.einsum('bhqd,bhkd->bhqk', q_blk, k).astype(jnp.float32) * scale
        s = s + (c_blk[..., :, None] - c[:, :, None, :])
        qpos = i * Q_BLOCK + jnp.arange(Q_BLOCK)
        s = jnp.where(kpos[None, :] <= qpos[:, None], s, -jnp.inf)
        p = jax.nn.softmax(s, axis=-1)
        return jnp.einsum('bhqk,bhkd->bhqd', p.astype(v.dtype), v)

    ob = lax.map(block, (qb, cb, jnp.arange(nb)))
    return ob.transpose(1, 2, 0, 3, 4).reshape(B, H, S, dh)

def hybrid_mixer(h, w_in, lb, out_norm_w, fox_bf, w_out):
    B, S, _ = h.shape
    sizes = [HGRN_KW, HGRN_KW, HGRN_WIDTH, HGRN_WIDTH, FOX_WIDTH, FOX_WIDTH, FOX_WIDTH]
    offsets = [int(o) for o in np.cumsum(sizes)]
    z = h @ w_in
    hq, hf, hi, hg, fq, fk, fv, ff = jnp.split(z, offsets, axis=-1)

    def heads(t, n):
        return t.reshape(B, S, n, -1).transpose(0, 2, 1, 3)

    zf = hf.astype(jnp.float32)
    lb32 = lb.astype(jnp.float32)
    logf_h = jnp.logaddexp(jnp.log(lb32), jnp.log1p(-lb32) + jax.nn.log_sigmoid(zf))
    k_h = (1.0 - lb32) * jax.nn.sigmoid(-zf)
    q_h = jax.nn.silu(hq.astype(jnp.float32))
    o_h = hgrn2_chunk_scan(heads(q_h, HGRN_HEADS), heads(k_h, HGRN_HEADS),
                           heads(hi.astype(jnp.float32), HGRN_HEADS),
                           heads(logf_h, HGRN_HEADS))
    o_h = rms_norm_2(o_h.transpose(0, 2, 1, 3), out_norm_w).reshape(B, S, HGRN_WIDTH)
    o_h = o_h * jax.nn.silu(hg.astype(jnp.float32))

    logf_f = jax.nn.log_sigmoid(ff.astype(jnp.float32) + fox_bf.astype(jnp.float32))
    o_f = forgetting_attention(heads(fq, FOX_HEADS), heads(fk, FOX_HEADS),
                               heads(fv, FOX_HEADS), logf_f.transpose(0, 2, 1))
    o_f = o_f.transpose(0, 2, 1, 3).reshape(B, S, FOX_WIDTH)

    o = jnp.concatenate([o_h.astype(h.dtype), o_f.astype(h.dtype)], axis=-1)
    return o @ w_out

def memory_cross_attention(h, m, wq, wk, wv, wo):
    B, S, _ = h.shape
    M = m.shape[1]
    q = (h @ wq).reshape(B, S, CROSS_HEADS, CROSS_DH)
    k = (m @ wk).reshape(B, M, CROSS_HEADS, CROSS_DH)
    v = (m @ wv).reshape(B, M, CROSS_HEADS, CROSS_DH)
    s = jnp.einsum('bshd,bmhd->bhsm', q, k).astype(jnp.float32) * (CROSS_DH ** -0.5)
    p = jax.nn.softmax(s, axis=-1).astype(h.dtype)
    o = jnp.einsum('bhsm,bmhd->bshd', p, v).reshape(B, S, D_MODEL)
    return o @ wo

def second_inputs(seed: int = 0) -> dict:
    key = jax.random.key(seed)
    ks = jax.random.split(key, 24)
    n = jax.random.normal
    f32 = jnp.float32

    def w(k, shape, fan_in):
        return n(k, shape, f32) * fan_in ** -0.5

    def gain(k, shape):
        return 1.0 + 0.05 * n(k, shape, f32)

    return {
        "x": n(ks[0], (BATCH, SEQ, D_MODEL), f32),
        "mem": n(ks[1], (BATCH, N_MEM, D_MODEL), f32),
        "ffn1_norm": gain(ks[2], (DEPTH_2, D_MODEL)),
        "ffn1_w_gate": w(ks[3], (DEPTH_2, D_MODEL, D_FF_2), D_MODEL),
        "ffn1_w_up": w(ks[4], (DEPTH_2, D_MODEL, D_FF_2), D_MODEL),
        "ffn1_w_down": w(ks[5], (DEPTH_2, D_FF_2, D_MODEL), D_FF_2),
        "mix_norm": gain(ks[6], (DEPTH_2, D_MODEL)),
        "w_in": w(ks[7], (DEPTH_2, D_MODEL, N_IN), D_MODEL),
        "hgrn_lb": n(ks[8], (DEPTH_2, HGRN_KW), f32),
        "hgrn_out_norm": gain(ks[9], (DEPTH_2, HGRN_DV)),
        "fox_f_bias": 2.0 + 0.5 * n(ks[10], (DEPTH_2, FOX_HEADS), f32),
        "w_out": w(ks[11], (DEPTH_2, D_MIX, D_MODEL), D_MIX),
        "cross_norm": gain(ks[12], (DEPTH_2, D_MODEL)),
        "mem_norm": gain(ks[13], (DEPTH_2, D_MODEL)),
        "cross_wq": w(ks[14], (DEPTH_2, D_MODEL, D_MODEL), D_MODEL),
        "cross_wk": w(ks[15], (DEPTH_2, D_MODEL, D_MODEL), D_MODEL),
        "cross_wv": w(ks[16], (DEPTH_2, D_MODEL, D_MODEL), D_MODEL),
        "cross_wo": w(ks[17], (DEPTH_2, D_MODEL, D_MODEL), D_MODEL),
        "ffn2_norm": gain(ks[18], (DEPTH_2, D_MODEL)),
        "ffn2_w_gate": w(ks[19], (DEPTH_2, D_MODEL, D_FF_2), D_MODEL),
        "ffn2_w_up": w(ks[20], (DEPTH_2, D_MODEL, D_FF_2), D_MODEL),
        "ffn2_w_down": w(ks[21], (DEPTH_2, D_FF_2, D_MODEL), D_FF_2),
        "final_norm": gain(ks[22], (D_MODEL,)),
    }

def second_block(x, mem, ffn1_norm, ffn1_w_gate, ffn1_w_up, ffn1_w_down, mix_norm, w_in,
              hgrn_lb, hgrn_out_norm, fox_f_bias, w_out, cross_norm, mem_norm,
              cross_wq, cross_wk, cross_wv, cross_wo, ffn2_norm, ffn2_w_gate,
              ffn2_w_up, ffn2_w_down, final_norm):
    lb_cum = jnp.cumsum(jax.nn.softmax(hgrn_lb.astype(jnp.float32), axis=0), axis=0)
    lb_all = lb_cum - lb_cum[0:1]
    for l in range(DEPTH_2):
        x = x + 0.5 * swiglu(rms_norm_2(x, ffn1_norm[l]), ffn1_w_gate[l], ffn1_w_up[l], ffn1_w_down[l])
        x = x + hybrid_mixer(rms_norm_2(x, mix_norm[l]), w_in[l], lb_all[l], hgrn_out_norm[l],
                             fox_f_bias[l], w_out[l])
        x = x + memory_cross_attention(rms_norm_2(x, cross_norm[l]), rms_norm_2(mem, mem_norm[l]),
                                       cross_wq[l], cross_wk[l], cross_wv[l], cross_wo[l])
        x = x + 0.5 * swiglu(rms_norm_2(x, ffn2_norm[l]), ffn2_w_gate[l], ffn2_w_up[l], ffn2_w_down[l])
    return rms_norm_2(x, final_norm)


def setup_inputs(seed=0):
    out = dict(first_inputs(seed))
    for name, value in second_inputs(seed + 1).items():
        if name != "x":
            out[name + "_2"] = value
    return out


def reference(
    x, norm_g, mlp_w1, mlp_w2, gdn_w_in, gdn_conv, gdn_a_log, gdn_dt_bias, gdn_norm_g,
    gdn_w_out, mlstm_w_in, mlstm_gate_b, mlstm_norm_g, mlstm_w_out, diff_w_in, diff_lambda,
    diff_norm_g, diff_w_out, mem_2, ffn1_norm_2, ffn1_w_gate_2, ffn1_w_up_2, ffn1_w_down_2,
    mix_norm_2, w_in_2, hgrn_lb_2, hgrn_out_norm_2, fox_f_bias_2, w_out_2, cross_norm_2,
    mem_norm_2, cross_wq_2, cross_wk_2, cross_wv_2, cross_wo_2, ffn2_norm_2, ffn2_w_gate_2,
    ffn2_w_up_2, ffn2_w_down_2, final_norm_2,
):
    x = first_block(
        x, norm_g, mlp_w1, mlp_w2, gdn_w_in, gdn_conv, gdn_a_log, gdn_dt_bias, gdn_norm_g,
        gdn_w_out, mlstm_w_in, mlstm_gate_b, mlstm_norm_g, mlstm_w_out, diff_w_in, diff_lambda,
        diff_norm_g, diff_w_out,
    )
    return second_block(
        x, mem_2, ffn1_norm_2, ffn1_w_gate_2, ffn1_w_up_2, ffn1_w_down_2, mix_norm_2, w_in_2,
        hgrn_lb_2, hgrn_out_norm_2, fox_f_bias_2, w_out_2, cross_norm_2, mem_norm_2, cross_wq_2,
        cross_wk_2, cross_wv_2, cross_wo_2, ffn2_norm_2, ffn2_w_gate_2, ffn2_w_up_2,
        ffn2_w_down_2, final_norm_2,
    )


_drawn_inputs = setup_inputs


def setup_inputs(seed=0):
    import zlib

    import numpy as np

    out = dict(_drawn_inputs(seed))
    spreads = {}
    factors = {'ffn1_norm_2': 5.7,
     'mix_norm_2': 3.143,
     'hgrn_lb_2': 5.548,
     'hgrn_out_norm_2': 5.738,
     'cross_norm_2': 8.0,
     'mem_norm_2': 8.0,
     'ffn2_norm_2': 5.712}
    for name, (base, spread) in spreads.items():
        noise = np.random.default_rng([zlib.crc32(name.encode()), seed]).standard_normal(out[name].shape)
        drawn = base * np.exp(spread * noise) if base else spread * noise
        out[name] = __import__('jax').numpy.asarray(drawn.astype(out[name].dtype))
    for name, factor in factors.items():
        out[name] = (out[name] * factor).astype(out[name].dtype)
    return out
```

```python
import math
from contextlib import ExitStack

import numpy as np

import concourse.bass as bass
from concourse import mybir

F32 = mybir.dt.float32
I32 = mybir.dt.int32
ALU = mybir.AluOpType
ACT = mybir.ActivationFunctionType
AX = mybir.AxisListType.X

P = 128
T = 256
TT = T // P
D = 1024
DC = D // P
EPS = 1e-6
RING = 4
SLAB = 4096
NEG = -1e30
TREE = [1, 2, 4, 8, 16, 32, 64]
ED = 384

CONST = {}
_at = 0
for _name, _n in (("ident", P), ("after", P), ("upto", T), ("neg_causal", P), ("neg_block", P),
                  ("rotate", P), ("cos", T), ("sin", T), ("tree_ts", 7 * P), ("tree_st", 7 * P)):
    CONST[_name] = (_at, _at + _n)
    _at += _n
NCONST = _at


def shape_constants():
    c = np.zeros((P, NCONST), np.float32)
    row, col = np.arange(P)[:, None], np.arange(P)[None, :]

    def put(name, value):
        c[:, CONST[name][0]:CONST[name][1]] = value

    put("ident", row == col)
    put("after", row > col)
    put("upto", row <= np.arange(T)[None, :])
    put("neg_causal", np.where(col > row, NEG, 0.0))
    put("neg_block", np.where(col // 64 > row // 64, NEG, 0.0))
    rot = np.zeros((P, P), np.float32)
    cos, sin = np.ones((P, T), np.float32), np.zeros((P, T), np.float32)
    inv = (np.float32(500000.0) ** (-np.arange(0, 16, 2, dtype=np.float32) / np.float32(16))).astype(np.float32)
    ang = (np.arange(T, dtype=np.float32)[None, :] * inv[:, None]).astype(np.float32)
    for base in (0, 64):
        for j in range(8):
            rot[base + 8 + j, base + j] = -1.0
            rot[base + j, base + 8 + j] = 1.0
            for k in (j, 8 + j):
                cos[base + k] = np.cos(ang[j])
                sin[base + k] = np.sin(ang[j])
    put("rotate", rot)
    put("cos", cos)
    put("sin", sin)
    ts = []
    for m in TREE:
        same = row // (2 * m) == col // (2 * m)
        ts.append((same & (row % (2 * m) >= m) & (col % (2 * m) < m)).astype(np.float32))
    put("tree_ts", np.concatenate(ts, 1))
    put("tree_st", np.concatenate([m.T for m in ts], 1))
    return c


VROWS = [("norm_g", 128), ("ffn1_norm_2", 16), ("mix_norm_2", 16), ("cross_norm_2", 16), ("mem_norm_2", 16),
         ("ffn2_norm_2", 16), ("final_norm_2", 8), ("mlstm_norm_g", 8), ("hgrn_lb_2", 8),
         ("hgrn_out_norm_2", 2), ("gdn_norm_g", 2), ("diff_norm_g", 1)]
VCOL = {}
_at = 0
for _name, _n in VROWS:
    VCOL[_name] = _at
    _at += _n
NVEC = _at

DEPTH = 4
LAYERS2 = 2


def schedule():
    parts = []
    for i in range(DEPTH):
        parts += [(("gdn", "mlstm", "diff")[i % 3], i), ("mlp", i)]
    for l in range(LAYERS2):
        parts += [("ffn1", l), ("hybrid", l), ("cross", l), ("ffn2", l)]
    return parts


def slabs_of(kind, i):
    def cols(name, layer, n, first=0):
        return [(name, layer, "cols", j, 2) for j in range(first, first + n)]

    if kind == "gdn":
        return cols("gdn_w_in", i // 3, 8) + cols("gdn_w_out", i // 3, 2)
    if kind == "mlstm":
        return cols("mlstm_w_in", i // 3, 6) + cols("mlstm_w_out", i // 3, 2)
    if kind == "diff":
        return cols("diff_w_in", i // 3, 6) + cols("diff_w_out", i // 3, 2)
    if kind == "mlp":
        return cols("mlp_w1", i, 8) + [("mlp_w2", i, "rows", j, 4 if j == 7 else 1) for j in range(8)]
    if kind in ("ffn1", "ffn2"):
        return ([(kind, i, "gate_up", j, 2) for j in range(11)]
                + [(f"{kind}_w_down_2", i, "rows", j, 4 if j == 5 else 1) for j in range(6)])
    if kind == "hybrid":
        return cols("w_in_2", i, 7) + cols("w_out_2", i, 2)
    assert kind == "cross"
    return (cols("cross_wq_2", i, 2) + cols("cross_wk_2", i, 2) + cols("cross_wv_2", i, 2)
            + cols("cross_wo_2", i, 2))


SHARED = ("x_ready", "sq_ready", "ss_ready", "rs_ready", "h_ready", "products_done", "slab_in", "stored", "out_",
          "pe_step", "act_step", "dve_step", "pool_step", "gates_in")

LAMBDA_INIT = 0.8 - 0.6 * math.exp(-0.3 * 2)


def program(nc, io, out, parts=None):
    parts = schedule() if parts is None else parts

    slabs, slab_no, groups_before = [], {}, {}
    count = 0
    for kind, i in parts:
        for s in slabs_of(kind, i):
            key = (s[0], s[1], s[3])
            slab_no[key] = len(slabs)
            groups_before[key] = count
            count += s[4]
            slabs.append(s + (count,))
    filled, landed = [0] * RING, []
    for n, s in enumerate(slabs):
        filled[n % RING] += 16 * (2 if s[2] == "gate_up" else 1)
        landed.append(filled[n % RING])
    x_at = {p: 4 * (n + 1) for n, p in enumerate(parts)}
    gdn_no = {i: n for n, (k, i) in enumerate([p for p in parts if p[0] == "gdn"])}

    with ExitStack() as ctx:
        def sb(name, shape, dt=F32):
            return ctx.enter_context(nc.sbuf_tensor(name, shape, dt))

        sems, scope = {}, [""]

        def sem(name):
            if not name.startswith(SHARED):
                name = scope[0] + name
            if name not in sems:
                sems[name] = ctx.enter_context(nc.semaphore(name))
            return sems[name]

        class Waits:

            def __init__(self, eng, step):
                self.eng, self.seen, self.step, self.steps = eng, {}, sem(step), 0

            def next(self, name, n=1):
                key = sem(name).name
                self.seen[key] = self.seen.get(key, 0) + n
                return self.seen[key]

            def mark(self, ins):
                self.steps += 1
                ins.then_inc(self.step, 1)
                return self.steps

            def chain(self, ins):
                self.eng.wait_ge(self.step, self.mark(ins))

        def group(name, layer, j, g):
            return groups_before[(name, layer, j)] + g + 1

        xT = sb("xT", [P, DC, T])
        hT = sb("hT", [P, DC, T])
        sq = sb("sq", [P, DC, T])
        rs = sb("rs", [P, T])
        rs_mem = sb("rs_mem", [P, T])
        ring = sb("ring", [P, RING, SLAB])
        const = sb("const", [P, NCONST])
        ones = sb("ones", [P, T])
        epsc = sb("epsc", [P, 1])
        memT = sb("memT", [P, DC, T])
        vec = sb("vec", [P, NVEC])
        bcast = sb("bcast", [P, 40])
        lb = sb("lb", [P, 28])
        gw = sb("gw", [P, 5, DC, 16])
        gbias = sb("gbias", [8, 4])
        gb15 = sb("gb15", [8, 4])
        arena = sb("arena", [P, 22784])
        ps = ctx.enter_context(nc.psum_tensor("ps", [P, 8, 512], F32))

        def cc(name, k=None):
            a, b = CONST[name]
            return const[:, a:b] if k is None else const[:, a + k * P:a + (k + 1) * P]

        def column(name, k):
            return vec[:, VCOL[name] + k:VCOL[name] + k + 1]

        ident = cc("ident")

        class Arena:
            def __init__(self, at=0):
                self.at = at

            def take(self, n, pat=None, **k):
                v = arena[:, self.at:self.at + n]
                self.at += n
                assert self.at <= 22784, self.at
                return v.rearrange(pat, **k) if pat else v

        A = Arena()
        hidden = A.take(32 * T, "p (c t) -> p c t", c=32)
        act_s = A.take(2 * 512, "p (b n) -> p b n", b=2)

        A = Arena()
        qk = A.take(16 * T, "p (c t) -> p c t", c=16)
        v_tok = A.take(TT * D, "p (i n) -> p i n", i=TT)
        gate = A.take(DC * T, "p (c t) -> p c t", c=DC)
        pair = A.take(8 * ED, "p (h n) -> p h n", h=8)
        after_pair = A.at
        kkb = A.take(8 * ED, "p (h n) -> p h n", h=8)
        staging = A.at
        inv = A.take(TT * 8 * P, "p (i h n) -> p i h n", i=TT, h=8)
        invT = A.take(TT * 8 * P, "p (i h n) -> p i h n", i=TT, h=8)
        level = A.take(TT * 8 * P, "p (i h n) -> p i h n", i=TT, h=8)
        scaled = A.take(2 * ED, "p (b n) -> p b n", b=2)
        tokg = A.take(96)
        convw = A.take(96)
        w_sol = level.rearrange("p i h n -> p i (h n)")
        u_sol = inv.rearrange("p i h n -> p i (h n)")
        A = Arena(staging)
        pre = A.take(2 * 2 * 260, "p (b c n) -> p b c n", b=2, c=2)
        conv = A.take(2 * 2 * T, "p (b c n) -> p b c n", b=2, c=2)
        vch = A.take(2 * 2 * T, "p (b c n) -> p b c n", b=2, c=2)
        convrow = A.take(P)

        A = Arena(after_pair)
        rows = A.take(12 * T, "p (r t) -> p r t", r=12)
        rcol = A.take(16, "p (i h) -> p i h", i=TT)
        em_s = A.take(2 * 2 * T, "p (b t) -> p b t", b=2)
        lay = A.at
        raw = A.take(4 * 512, "p (b n) -> p b n", b=4)
        prob = A.take(2 * 2 * 512, "p (b c n) -> p b c n", b=2, c=2)
        probT = A.take(2 * 512, "p (b n) -> p b n", b=2)
        stat = A.take(2 * 2 * 4, "p (b c s) -> p b c s", b=2, c=2)
        num_s = A.take(DC * T, "p (c t) -> p c t", c=DC)
        mem_n = num_s
        A = Arena(lay)
        zcum = A.take(4 * T, "p (h t) -> p h t", h=4)
        glog = A.take(4 * T, "p (h t) -> p h t", h=4)
        factor = num_s.rearrange("p (b h) t -> p b h t", b=2)

        vec_rows, vec_rows2 = arena[:, 0:P], arena[:, P:2 * P]
        brow = arena[0:1, 256:288]
        lrow = arena[0:1, 320:576]
        lwork = arena[0:1, 600:732]
        x_rows = sq[:, :, :].rearrange("p c t -> p (c t)").rearrange("p (i n) -> p i n", i=TT)
        mem_rows = hT[:, :, :].rearrange("p c t -> p (c t)").rearrange("p (i n) -> p i n", i=TT)
        out_rows = memT[:, :, :].rearrange("p c t -> p (c t)").rearrange("p (i n) -> p i n", i=TT)

        def two(v):
            return v.rearrange("p (c t) -> p c t", c=2)

        def slab_source(s):
            name, layer, how, j = s[:4]
            if how == "cols":
                w = io[name][layer].rearrange("(c p) n -> p c n", p=P)
                return [(0, DC * 512, DC, w[:, :, 512 * j:512 * (j + 1)])]
            if how == "gate_up":
                g = io[f"{name}_w_gate_2"][layer].rearrange("(c p) n -> p c n", p=P)
                u = io[f"{name}_w_up_2"][layer].rearrange("(c p) n -> p c n", p=P)
                return [(0, DC * 256, DC, g[:, :, 256 * j:256 * (j + 1)]),
                        (DC * 256, DC * 512, DC, u[:, :, 256 * j:256 * (j + 1)])]
            k = min(4, io[name].shape[1] // P - 4 * j)
            w = io[name][layer][512 * j:512 * j + P * k, :].rearrange("(c p) n -> p c n", p=P)
            return [(0, k * D, k, w)]

        def flat_rows(ap):
            names = "abcd"[:len(ap.shape)]
            if len(names) > 1:
                ap = ap.rearrange(f"{' '.join(names)} -> ({' '.join(names)})")
            return ap

        block = ctx.enter_context(nc.Block())

        @block.sync
        def _(sp):
            sp.dma_start(x_rows, io["x"][0].rearrange("(i p) n -> p i n", p=P)).then_inc(sem("x_in"), 16)
            sp.dma_start(const[:, :], io["shape_constants"]).then_inc(sem("const_in"), 16)
            sp.dma_start(mem_rows, io["mem_2"][0].rearrange("(i p) n -> p i n", p=P)).then_inc(sem("mem_in"), 16)
            for n, s in enumerate(slabs):
                if n >= RING:
                    sp.wait_ge(sem("products_done"), slabs[n - RING][5])
                for a, b, c, src in slab_source(s):
                    sp.dma_start(ring[:, n % RING, a:b].rearrange("p (c n) -> p c n", c=c), src)\
                      .then_inc(sem(f"slab_in{n % RING}"), 16)
            for i in range(TT):
                sp.wait_ge(sem("out_tile"), i + 1)
                sp.dma_start(out[0, i * P:(i + 1) * P, :], out_rows[:, i, :]).then_inc(sem("stored"), 16)
            sp.wait_ge(sem("stored"), 16 * TT)

        @block.gpsimd
        def _(pool):
            scope[0] = ""
            W = Waits(pool, "pool_step")
            pool.memset(ones[:, :], 1.0)
            pool.memset(epsc[:, :], EPS).then_inc(sem("ones_set"), 1)
            at = 0
            for name, n in VROWS:
                dst = vec_rows[0:n, :] if name == "norm_g" else vec_rows2[at - P:at - P + n, :]
                pool.dma_start(dst, flat_rows(io[name]).rearrange("(r q) -> r q", q=P)).then_inc(sem("vec_in"), 16)
                at += n
            for b, name in ((0, "gdn_a_log"), (16, "gdn_dt_bias")):
                pool.dma_start(brow[:, b:b + 16], flat_rows(io[name]).rearrange("(a n) -> a n", a=1))\
                    .then_inc(sem("vec_in"), 16)
            pool.dma_start(lrow, flat_rows(io["diff_lambda"]).rearrange("(a n) -> a n", a=1))\
                .then_inc(sem("vec_in"), 16)
            for k, src in enumerate((io["mlstm_gate_b"][0, 0], io["mlstm_gate_b"][0, 1],
                                     io["fox_f_bias_2"][0], io["fox_f_bias_2"][1])):
                pool.dma_start(gbias[:, k:k + 1], src.rearrange("(h a) -> h a", a=1)).then_inc(sem("gates_in"), 16)
            for k, (name, l, c0, n) in enumerate((("gdn_w_in", 0, 4096, 16), ("gdn_w_in", 1, 4096, 16),
                                                  ("mlstm_w_in", 0, 3072, 16), ("w_in_2", 0, 3584, 8),
                                                  ("w_in_2", 1, 3584, 8))):
                pool.dma_start(gw[:, k, :, 0:n],
                               io[name][l].rearrange("(c p) n -> p c n", p=P)[:, :, c0:c0 + n])\
                    .then_inc(sem("gates_in"), 16)

            def mask(h):
                pool.wait_ge(sem("pair_exp"), W.next("pair_exp"))
                v = pair[:, h, :].rearrange("p (k n) -> p k n", k=3)[:, 0:3:2, :]
                pool.affine_select(out=v, in_=v, compare_op=ALU.is_ge, fill=0.0, base=0,
                                   pattern=[[0, 2], [1, P]], channel_multiplier=-1).then_inc(sem("pair_masked"), 1)

            def gdn(i):
                pool.wait_ge(sem("x_ready"), x_at[("gdn", i)])
                pool.dma_start(convrow[0:96, :], io["gdn_conv"][i // 3].rearrange("k (c q) -> (k c) q", q=P))\
                    .then_inc(sem("conv_in"), 16)
                pool.memset(pre[:, :, :, 0:3], 0.0).then_inc(sem("pad_set"), 1)
                pool.wait_ge(sem("tok_gates"), W.next("tok_gates"))
                for h in range(8):
                    if h >= 2:
                        pool.wait_ge(sem("decay_done"), W.next("decay_done"))
                    pool.tensor_scalar(scaled[:, h % 2, 0:T], cc("upto"), tokg[:, h:h + 1], None, ALU.mult)
                    pool.tensor_scalar(scaled[:, h % 2, T:ED], cc("upto")[:, 0:P], tokg[:, 8 + h:9 + h], None,
                                       ALU.mult).then_inc(sem("scaled_ready"), 1)
                    if h >= 1:
                        mask(h - 1)
                mask(7)
                pool.wait_ge(sem("decay_done"), W.next("decay_done", 2))
                pool.wait_ge(sem("v_done"), W.next("v_done", 4))
                for m in (inv, invT):
                    for t in range(TT):
                        last = pool.tensor_copy(m[:, t, :, :], ident[:, None, :].broadcast_to([P, 8, P]))
                last.then_inc(sem("inverse_start"), 1)

            for kind, i in parts:
                scope[0] = kind[:3] + "_"
                if kind == "gdn":
                    gdn(i)
                elif kind == "mlstm":
                    for h in range(8):
                        mask(h)

        @block.tensor
        def _(pe):
            scope[0] = ""
            W = Waits(pe, "pe_step")

            def mm(o, l, r, start, stop, **k):
                return pe.matmul(o, l, r, start=start, stop=stop, **k)

            def slab(name, layer, j, c):
                n = slab_no[(name, layer, j)]
                pe.wait_ge(sem(f"slab_in{n % RING}"), landed[n])
                return ring[:, n % RING, :].rearrange("p (c n) -> p c n", c=c)

            def banks(s):
                return 4 + (2 * s) % 4, 5 + (2 * s) % 4

            def to_channels(name, layer, j, two_banks, first=False, src=hT, free=None):
                w = slab(name, layer, j, DC)
                for g, bank in enumerate(two_banks):
                    if free and 2 * j + g >= 4:
                        pe.wait_ge(sem(free), W.next(free))
                    for half in range(2):
                        m = 2 * g + half
                        for k in range(DC):
                            if first and m == 0:
                                pe.wait_ge(sem("h_ready"), W.next("h_ready"))
                            last = mm(ps[:, bank, half * T:(half + 1) * T], w[:, k, m * P:(m + 1) * P],
                                      src[:, k, :], k == 0, k == DC - 1)
                    last.then_inc(sem("products_done"), 1)

            def to_tokens(name, layer, j, two_banks, src=hT):
                w = slab(name, layer, j, DC)
                for i, bank in enumerate(two_banks):
                    for k in range(DC):
                        last = mm(ps[:, bank, :], src[:, k, i * P:(i + 1) * P], w[:, k, :], k == 0, k == DC - 1)
                    last.then_inc(sem("products_done"), 1)

            def norm_sum():
                for c in range(4):
                    pe.wait_ge(sem("sq_ready"), W.next("sq_ready"))
                    for k in (2 * c, 2 * c + 1):
                        last = mm(ps[:, 7, 0:T], ones[:, 0:P], sq[:, k, :], k == 0, k == DC - 1)
                last.then_inc(sem("ss_ready"), 1)

            def head_sums(n):
                for b in range(n):
                    pe.wait_ge(sem("sq_ready"), W.next("sq_ready"))
                    mm(ps[:, 4 + b, :], ones[:, 0:P], sq[:, 2 * b:2 * b + 2, :], True, True)\
                        .then_inc(sem("hs_ready"), 1)

            def out_product(name, layer, k0=0):
                for j in range(2):
                    w = slab(name, layer, j, DC)
                    for m in range(4):
                        for k in range(DC):
                            if j == 0 and m == 0 and (k == 0 or k % 2 == 0 and k > k0):
                                pe.wait_ge(sem("mix_ready"), W.next("mix_ready"))
                            last = mm(ps[:, 2 * j + m // 2, (m % 2) * T:(m % 2 + 1) * T], w[:, k, m * P:(m + 1) * P],
                                      hT[:, k, :], k == 0, k == DC - 1)
                        if m % 2:
                            last.then_inc(sem("products_done"), 1)

            def down_product(name, layer, chunks, waited):
                for j in range((chunks + 3) // 4):
                    w = slab(name, layer, j, 4)
                    for kk in range(4 * j, min(4 * j + 4, chunks)):
                        if kk in waited:
                            pe.wait_ge(sem("hidden_ready"), W.next("hidden_ready"))
                        end = kk == chunks - 1
                        for m in range(DC):
                            last = mm(ps[:, m // 2, (m % 2) * T:(m % 2 + 1) * T], w[:, kk % 4, m * P:(m + 1) * P],
                                      hidden[:, kk, :], kk == 0 and m % 2 == 0, end and m % 2 == 1,
                                      skip_group_check=True)
                            if end and m % 2:
                                last.then_inc(sem("products_done"), 1)
                    if not end:
                        last.then_inc(sem("products_done"), 1)

            def mlp(i):
                norm_sum()
                for j in range(8):
                    to_channels("mlp_w1", i, j, banks(j), first=j == 0, free="hidden_ready")
                down_product("mlp_w2", i, 32, (24, 26, 28, 30))
                norm_sum()

            def ffn(kind, l):
                norm_sum()
                for n in range(22):
                    if n % 2 == 0:
                        w = slab(kind, l, n // 2, 2 * DC)
                    if n >= 4:
                        pe.wait_ge(sem("hidden_ready"), W.next("hidden_ready"))
                    for half in range(2):
                        for k in range(DC):
                            if n == 0 and half == 0:
                                pe.wait_ge(sem("h_ready"), W.next("h_ready"))
                            last = mm(ps[:, 4 + n % 4, half * T:(half + 1) * T],
                                      w[:, half * DC + k, (n % 2) * P:(n % 2 + 1) * P], hT[:, k, :],
                                      k == 0, k == DC - 1)
                    last.then_inc(sem("products_done"), 1)
                down_product(f"{kind}_w_down_2", l, 22, (18, 19, 20, 21))

            def outputs(heads, values):
                for h in range(heads):
                    b, c0 = h // 2, (h % 2) * T
                    mm(ps[:, b, c0:c0 + T], values(0, h), pair[:, h, 0:T], True, False)
                    last = mm(ps[:, b, c0 + P:c0 + T], values(1, h), pair[:, h, T:ED], False, True)
                    if h % 2:
                        last.then_inc(sem("o_ready"), 1)

            def gdn(i):
                j = i // 3
                pe.wait_ge(sem("conv_in"), W.next("conv_in", 16))
                pe.transpose(ps[:, 3, 0:96], convrow[0:96, :], ident[0:96, 0:96]).then_inc(sem("conv_turned"), 1)
                norm_sum()
                pe.wait_ge(sem("h_ready"), W.next("h_ready", 8))
                for t in range(TT):
                    for k in range(DC):
                        last = mm(ps[:, 3, 128 + 16 * t:144 + 16 * t], hT[:, k, t * P:(t + 1) * P], gw[:, j, k, :],
                                  k == 0, k == DC - 1)
                last.then_inc(sem("gates_done"), 1)

                def turn_values(g):
                    pe.wait_ge(sem("silu_done"), 12 * gdn_no[i] + 8 + g + 1)
                    if g > 0:
                        pe.wait_ge(sem("v_done"), W.next("v_done"))
                    for c in range(2):
                        for t in range(TT):
                            last = pe.transpose(ps[:, 2, (2 * t + c) * P:(2 * t + c + 1) * P],
                                                vch[:, g % 2, c, t * P:(t + 1) * P], ident)
                    last.then_inc(sem("v_turned"), 1)

                for s in range(8):
                    to_channels("gdn_w_in", j, s, banks(s), free="evac")
                    if s in (6, 7):
                        turn_values(2 * (s - 6))
                        turn_values(2 * (s - 6) + 1)
                pe.wait_ge(sem("evac"), W.next("evac", 4))
                pe.wait_ge(sem("v_done"), W.next("v_done"))
                for h in range(8):
                    pe.wait_ge(sem("scaled_ready"), W.next("scaled_ready"))
                    if h >= 2:
                        pe.wait_ge(sem("pair_exp"), W.next("pair_exp"))
                    b = 4 + h % 2
                    mm(ps[:, b, 0:T], cc("after"), scaled[:, h % 2, 0:T], True, False)
                    mm(ps[:, b, P:T], ones[:, 0:P], scaled[:, h % 2, T:ED], False, True)
                    mm(ps[:, b, T:ED], cc("after"), scaled[:, h % 2, T:ED], True, True).then_inc(sem("decay_done"), 1)
                pe.wait_ge(sem("pair_exp"), W.next("pair_exp", 2))
                for b in range(8):
                    pe.wait_ge(sem("sq_ready"), W.next("sq_ready"))
                    if b >= 4:
                        pe.wait_ge(sem("hs_free"), W.next("hs_free"))
                    mm(ps[:, b % 4, :], ones[:, 0:P], sq[:, 2 * (b % 4):2 * (b % 4) + 2, :], True, True)\
                        .then_inc(sem("hs_ready"), 1)
                pe.wait_ge(sem("hs_free"), W.next("hs_free", 4))
                pe.wait_ge(sem("qk_normed"), W.next("qk_normed", 8))
                for n in range(16):
                    h, b = n % 8, n % 4
                    r = qk[:, (8 if n < 8 else 0) + h, :]
                    if n >= 4:
                        pe.wait_ge(sem("score_free"), W.next("score_free"))
                    mm(ps[:, b, 0:T], qk[:, 8 + h, 0:P], r, True, True)
                    mm(ps[:, b, T:ED], qk[:, 8 + h, P:T], r[:, P:T], True, True).then_inc(sem("score_done"), 1)
                pe.wait_ge(sem("score_free"), W.next("score_free", 4))
                pe.wait_ge(sem("inverse_start"), W.next("inverse_start"))
                for n in range(len(TREE)):
                    for q in range(4):
                        t, h0 = q // 2, 4 * (q % 2)
                        if n:
                            pe.wait_ge(sem("inverse_done"), 28 * gdn_no[i] + 4 * (n - 1) + q + 1)
                        for h in range(4):
                            c0 = 0 if t == 0 else T
                            last = mm(ps[:, 4 + q, h * P:(h + 1) * P], kkb[:, h0 + h, c0:c0 + P],
                                      inv[:, t, h0 + h, :], True, True)
                        last.then_inc(sem("level_done"), 1)
                    for q in range(4):
                        t, h0 = q // 2, 4 * (q % 2)
                        pe.wait_ge(sem("level_masked"), W.next("level_masked"))
                        if q >= 2:
                            pe.wait_ge(sem("inverse_done"), 28 * gdn_no[i] + 4 * n + q - 1)
                        if n < len(TREE) - 1:
                            for h in range(4):
                                mm(ps[:, 2 * (q % 2), h * P:(h + 1) * P], invT[:, t, h0 + h, :],
                                   level[:, t, h0 + h, :], True, True)
                        for h in range(4):
                            last = mm(ps[:, 2 * (q % 2) + 1, h * P:(h + 1) * P], level[:, t, h0 + h, :],
                                      invT[:, t, h0 + h, :], True, True)
                        last.then_inc(sem("delta_done"), 1)
                pe.wait_ge(sem("inverse_done"), 28 * (gdn_no[i] + 1))

                def solve(b0, b, lhs, rhs):
                    for h in range(4 * b, 4 * b + 4):
                        last = mm(ps[:, b0 + b, (h % 4) * P:(h % 4 + 1) * P], lhs(h), rhs(h), True, True)
                    last.then_inc(sem("w_done"), 1)

                for b in range(2):
                    solve(4, b, lambda h: invT[:, 0, h, :], lambda h: v_tok[:, 0, h * P:(h + 1) * P])
                for b in range(2):
                    pe.wait_ge(sem("w_ready"), W.next("w_ready"))
                    solve(6, b, lambda h: kkb[:, h, P:T], lambda h: w_sol[:, 0, h * P:(h + 1) * P])
                for b in range(2):
                    pe.wait_ge(sem("w_ready"), W.next("w_ready"))
                    solve(4, b, lambda h: invT[:, 1, h, :], lambda h: v_tok[:, 1, h * P:(h + 1) * P])
                pe.wait_ge(sem("w_ready"), W.next("w_ready", 2))
                outputs(8, lambda t, h: u_sol[:, t, h * P:(h + 1) * P])
                head_sums(4)
                out_product("gdn_w_out", j)
                norm_sum()

            def spread(dst, h, row):
                return mm(dst, ident[0:8, h:h + 1].broadcast_to([8, P]), row, True, True)

            def mlstm(i):
                norm_sum()
                for s in (0, 1):
                    to_channels("mlstm_w_in", 0, s, banks(s), first=s == 0)
                for g in range(2):
                    for k in range(DC):
                        last = mm(ps[0:8, 0, g * T:(g + 1) * T], gw[:, 2, k, 8 * g:8 * g + 8], hT[:, k, :],
                                  k == 0, k == DC - 1)
                last.then_inc(sem("gates_done"), 1)
                pe.wait_ge(sem("evac"), W.next("evac", 4))
                for s in (2, 3):
                    to_tokens("mlstm_w_in", 0, s, banks(s))
                pe.wait_ge(sem("evac"), W.next("evac", 4))
                for s in (4, 5):
                    to_channels("mlstm_w_in", 0, s, banks(s))
                pe.wait_ge(sem("rows_ready"), W.next("rows_ready"))
                for t in range(TT):
                    last = pe.transpose(ps[:, 1, 8 * t:8 * t + 8], rows[0:8, 6, t * P:(t + 1) * P], ident[0:8, 0:8])
                last.then_inc(sem("r_turned"), 1)
                pe.wait_ge(sem("rcol_ready"), W.next("rcol_ready"))
                pe.wait_ge(sem("evac"), W.next("evac", 4))
                for h in range(8):
                    if h >= 2:
                        pe.wait_ge(sem("pair_exp"), W.next("pair_exp"))
                    spread(ps[:, h % 2, 0:T], h, rows[0:8, 7, :]).then_inc(sem("decay_done"), 1)
                pe.wait_ge(sem("pair_exp"), W.next("pair_exp", 2))
                for h in range(8):
                    if h >= 4:
                        pe.wait_ge(sem("score_free"), W.next("score_free"))
                    r0 = 64 * (h % 2)
                    q_, k_ = qk[r0:r0 + 64, h // 2, :], qk[r0:r0 + 64, 4 + h // 2, :]
                    mm(ps[:, 4 + h % 4, 0:T], k_[:, 0:P], q_, True, True)
                    mm(ps[:, 4 + h % 4, T:ED], k_[:, P:T], q_[:, P:T], True, True).then_inc(sem("score_done"), 1)
                pe.wait_ge(sem("score_free"), W.next("score_free", 4))
                outputs(8, lambda t, h: v_tok[:, t, h * P:(h + 1) * P])
                pe.wait_ge(sem("floor_ready"), W.next("floor_ready"))
                for h in range(8):
                    if h >= 2:
                        pe.wait_ge(sem("den_free"), W.next("den_free"))
                    b = 4 + h % 2
                    mm(ps[:, b, 0:T], ones[:, 0:P], pair[:, h, 0:T], True, False)
                    mm(ps[:, b, P:T], ones[:, 0:P], pair[:, h, T:ED], False, True)
                    spread(ps[:, b, T:2 * T], h, rows[0:8, 8, :]).then_inc(sem("den_done"), 1)
                pe.wait_ge(sem("den_free"), W.next("den_free", 2))
                head_sums(4)
                out_product("mlstm_w_out", 0)
                norm_sum()

            def attention(heads, comps, operands, negative, cum, wide):
                for h in range(heads + 1):
                    for c in range(comps if h < heads else 0):
                        n = comps * h + c
                        if n >= 4:
                            pe.wait_ge(sem("score_free"), W.next("score_free"))
                        b = 4 + n % 4
                        q_, k_ = operands(h, c)
                        for c0, t0, width in ((0, 0, P), (P, P, T)):
                            dst = ps[:, b, c0:c0 + width]
                            mm(dst, q_[:, t0:t0 + P], k_[:, 0:width], True, False)
                            if cum is not None:
                                mm(dst, ident[0:8, h:h + 1].broadcast_to([8, P]), cum[:, 0:width], False, False)
                            last = mm(dst[:, width - P:width], ident, negative, False, True)
                        last.then_inc(sem("score_done"), 1)
                    if h == 0:
                        continue
                    hh = h - 1
                    pe.wait_ge(sem("prob_ready"), W.next("prob_ready"))
                    for k in range(3):
                        last = pe.transpose(ps[:, 3, k * P:(k + 1) * P],
                                            prob[:, hh % 2, comps - 1, k * P:(k + 1) * P], ident)
                    last.then_inc(sem("prob_turned"), 1)
                    pe.wait_ge(sem("probT_ready"), W.next("probT_ready"))
                    if wide:
                        o = ps[:, (hh // 2) % 3, (hh % 2) * T:(hh % 2 + 1) * T]
                        v = [v_tok[:, t, P * hh:P * hh + P] for t in range(TT)]
                        if hh == 6:
                            pe.wait_ge(sem("o_moved"), W.next("o_moved"))
                        end = hh % 2 == 1
                    else:
                        c = hh // 2
                        o = ps[64 * (hh % 2):64 * (hh % 2) + 64, c // 2, (c % 2) * T:(c % 2 + 1) * T]
                        v = [v_tok[:, t, 512 + 64 * hh:576 + 64 * hh] for t in range(TT)]
                        end = hh % 4 == 3
                    mm(o, v[0], probT[:, hh % 2, 0:T], True, False)
                    last = mm(o[:, P:T], v[1], probT[:, hh % 2, T:ED], False, True)
                    if end:
                        last.then_inc(sem("o_ready"), 1)

            def diff(i):
                norm_sum()

                def rotate(s):
                    for g in (2 * s, 2 * s + 1):
                        pe.wait_ge(sem("raw_ready"), W.next("raw_ready"))
                        if g >= 2:
                            pe.wait_ge(sem("roped"), W.next("roped"))
                        mm(ps[:, g % 2, :], cc("rotate"), raw[:, g % 4, :], True, True).then_inc(sem("rotated"), 1)

                for s in range(4):
                    to_channels("diff_w_in", 0, s, banks(s), first=s == 0)
                    if s:
                        rotate(s - 1)
                to_tokens("diff_w_in", 0, 4, banks(4))
                rotate(3)
                to_tokens("diff_w_in", 0, 5, banks(5))
                pe.wait_ge(sem("roped"), W.next("roped", 2))
                pe.wait_ge(sem("evac"), W.next("evac", 4))
                attention(8, 2, lambda h, c: (qk[64 * c:64 * c + 64, h, :], qk[64 * c:64 * c + 64, 8 + h, :]),
                          cc("neg_block"), None, True)
                head_sums(4)
                out_product("diff_w_out", 0)
                norm_sum()

            def hybrid(l):
                norm_sum()
                to_channels("w_in_2", l, 0, banks(0), first=True)
                to_channels("w_in_2", l, 1, banks(1))
                for k in range(DC):
                    last = mm(ps[0:8, 0, 0:T], gw[:, 3 + l, k, 0:8], hT[:, k, :], k == 0, k == DC - 1)
                last.then_inc(sem("gates_done"), 1)
                pe.wait_ge(sem("evac"), W.next("evac", 4))
                to_tokens("w_in_2", l, 2, banks(0))
                to_channels("w_in_2", l, 3, banks(1))
                pe.wait_ge(sem("evac"), W.next("evac", 4))
                to_channels("w_in_2", l, 4, banks(0))
                to_channels("w_in_2", l, 5, banks(1))
                pe.wait_ge(sem("evac"), W.next("evac", 4))
                to_tokens("w_in_2", l, 6, banks(0))
                pe.wait_ge(sem("evac"), W.next("evac", 2))
                m = 0
                for n in range(len(TREE) + 2):
                    if n <= len(TREE):
                        pe.wait_ge(sem("factor_ready"), W.next("factor_ready"))
                    for t in range(1 if n == len(TREE) else TT):
                        if m >= 4:
                            pe.wait_ge(sem("tree_copied"), W.next("tree_copied"))
                        for h in range(4):
                            if n < len(TREE):
                                l_ = r_ = factor[:, n % 2, h, t * P:(t + 1) * P]
                            elif n == len(TREE):
                                l_, r_ = factor[:, n % 2, h, 0:P], factor[:, n % 2, h, P:T]
                            else:
                                l_, r_ = qk[:, 4 + h, t * P:(t + 1) * P], qk[:, h, t * P:(t + 1) * P]
                            last = mm(ps[:, 4 + m % 4, h * P:(h + 1) * P], l_, r_, True, True)
                        last.then_inc(sem("tree_done"), 1)
                        m += 1
                pe.wait_ge(sem("tree_copied"), W.next("tree_copied", 4))
                outputs(4, lambda t, h: v_tok[:, t, h * P:(h + 1) * P])
                head_sums(2)
                pe.wait_ge(sem("hgrn_mixed"), W.next("hgrn_mixed", 2))
                pe.wait_ge(sem("rows_ready"), W.next("rows_ready"))
                attention(8, 1, lambda h, c: (qk[64 * (h % 2):64 * (h % 2) + 64, 8 + h // 2, :],
                                              qk[64 * (h % 2):64 * (h % 2) + 64, 12 + h // 2, :]),
                          cc("neg_causal"), rows[0:8, 7, :], False)
                out_product("w_out_2", l, 4)

            def cross(l):
                norm_sum()
                to_channels("cross_wq_2", l, 0, banks(0), first=True)
                to_channels("cross_wq_2", l, 1, banks(1))
                pe.wait_ge(sem("evac"), W.next("evac", 4))
                pe.wait_ge(sem("mem_normed"), W.next("mem_normed", 8))
                to_channels("cross_wk_2", l, 0, banks(0), src=mem_n)
                to_channels("cross_wk_2", l, 1, banks(1), src=mem_n)
                pe.wait_ge(sem("evac"), W.next("evac", 4))
                to_tokens("cross_wv_2", l, 0, banks(0), src=mem_n)
                to_tokens("cross_wv_2", l, 1, banks(1), src=mem_n)
                pe.wait_ge(sem("evac"), W.next("evac", 4))
                for h in range(5):
                    if h < 4:
                        for t in range(TT):
                            for c in range(2):
                                last = mm(ps[:, 4 + h, t * T:(t + 1) * T], qk[:, 2 * h + c, t * P:(t + 1) * P],
                                          qk[:, 8 + 2 * h + c, :], c == 0, c == 1)
                        last.then_inc(sem("score_done"), 1)
                    if h >= 1:
                        hh = h - 1
                        pe.wait_ge(sem("prob_ready"), W.next("prob_ready"))
                        for t in range(TT):
                            for m in range(2):
                                last = pe.transpose(ps[:, 4 + hh, (2 * m + t) * P:(2 * m + t + 1) * P],
                                                    prob[:, hh % 2, 0, (2 * t + m) * P:(2 * t + m + 1) * P], ident)
                        last.then_inc(sem("prob_turned"), 1)
                        pe.wait_ge(sem("probT_ready"), W.next("probT_ready"))
                        for c in range(2):
                            for m in range(2):
                                last = mm(ps[:, hh, c * T:(c + 1) * T],
                                          v_tok[:, m, hh * T + c * P:hh * T + (c + 1) * P],
                                          probT[:, hh % 2, m * T:(m + 1) * T], m == 0, m == 1)
                        last.then_inc(sem("o_ready"), 1)
                out_product("cross_wo_2", l)

            def turn_in(rows_, name):
                for b in range(4):
                    for c in range(2):
                        for t in range(TT):
                            last = pe.transpose(ps[:, 4 + b, c * T + t * P:c * T + (t + 1) * P],
                                                rows_[:, t, (2 * b + c) * P:(2 * b + c + 1) * P], ident)
                    last.then_inc(sem(name), 1)

            pe.wait_ge(sem("const_in"), W.next("const_in", 16))
            pe.wait_ge(sem("ones_set"), W.next("ones_set"))
            pe.wait_ge(sem("x_in"), W.next("x_in", 16))
            turn_in(x_rows, "x_turned")
            pe.wait_ge(sem("x_ready"), W.next("x_ready", 4))
            pe.wait_ge(sem("mem_in"), W.next("mem_in", 16))
            turn_in(mem_rows, "mem_turned")
            pe.wait_ge(sem("vec_in"), W.next("vec_in", 16 * (len(VROWS) + 3)))
            pe.transpose(ps[:, 0, 0:P], vec_rows, ident)
            pe.transpose(ps[:, 0, P:NVEC], vec_rows2[0:NVEC - P, :], ident[0:NVEC - P, 0:NVEC - P])
            mm(ps[:, 0, 256:288], ones[0:1, 0:P], brow, True, True).then_inc(sem("vec_turned"), 1)
            pe.wait_ge(sem("lambda_ready"), W.next("lambda_ready"))
            mm(ps[:, 1, 0:1], ones[0:1, 0:P], lwork[:, 130:131], True, True).then_inc(sem("lambda_spread"), 1)
            norm_sum()
            pe.wait_ge(sem("mem_rs"), W.next("mem_rs"))
            pe.wait_ge(sem("params_ready"), W.next("params_ready"))
            pe.wait_ge(sem("gates_in"), W.next("gates_in", 16 * 9))

            for kind, i in parts:
                scope[0] = kind[:3] + "_"
                {"gdn": gdn, "mlstm": mlstm, "diff": diff, "mlp": mlp, "hybrid": hybrid, "cross": cross,
                 "ffn1": lambda l: ffn("ffn1", l), "ffn2": lambda l: ffn("ffn2", l)}[kind](i)
            norm_sum()
            pe.wait_ge(sem("h_ready"), W.next("h_ready", 8))
            for t in range(TT):
                for c in range(DC):
                    last = pe.transpose(ps[:, 2 * t + c // 4, (c % 4) * P:(c % 4 + 1) * P],
                                        hT[:, c, t * P:(t + 1) * P], ident)
                last.then_inc(sem("out_turned"), 1)

        @block.scalar
        def _(act):
            scope[0] = ""
            W = Waits(act, "act_step")
            f = act.activation

            def ln_exp():
                act.preload_act_table_set("natural_log_exp_and_others")

            def rsqrt(src, dst, n, name):
                W.chain(f(dst, src, ACT.Ln, scale=1.0 / n, bias=epsc[:, :]))
                f(dst, dst, ACT.Exp, scale=-0.5).then_inc(sem(name), 1)

            def norm(src, ready):
                for c in range(4):
                    ready(c)
                    f(sq[:, 2 * c:2 * c + 2, :], src(c), ACT.Square).then_inc(sem("sq_ready"), 1)
                act.wait_ge(sem("ss_ready"), W.next("ss_ready"))
                rsqrt(ps[:, 7, 0:T], rs[:, :], D, "rs_ready")

            def x_norm():
                ln_exp()
                norm(lambda c: xT[:, 2 * c:2 * c + 2, :], lambda c: act.wait_ge(sem("x_ready"), W.next("x_ready")))

            def post_norm(product):
                norm(lambda c: two(ps[:, c, :]), lambda c: act.wait_ge(sem("products_done"), group(*product(c))))

            def head_norm(n, src, taken=None):
                for b in range(n):
                    if taken:
                        act.wait_ge(sem(taken), W.next(taken))
                    f(sq[:, 2 * b:2 * b + 2, :], src(b), ACT.Square).then_inc(sem("sq_ready"), 1)
                for b in range(n):
                    act.wait_ge(sem("hs_ready"), W.next("hs_ready"))
                    rsqrt(ps[:, 4 + b, :], flat(sq[:, 2 * b:2 * b + 2, :]), P, "hrs_ready")

            def flat(v):
                return v.rearrange("p c t -> p (c t)")

            def channels(name, layer, j, bank0, dst, func=ACT.Copy, scale=1.0):
                for g in range(2):
                    act.wait_ge(sem("products_done"), group(name, layer, j, g))
                    f(dst(g), two(ps[:, bank0 + g, :]), func, scale=scale).then_inc(sem("evac"), 1)

            def tokens(name, layer, j, bank0, c0):
                for t in range(TT):
                    act.wait_ge(sem("products_done"), group(name, layer, j, t))
                    f(v_tok[:, t, c0:c0 + 512], ps[:, bank0 + t, :], ACT.Copy).then_inc(sem("evac"), 1)

            def chunks(v, c):
                return lambda g: v[:, c + 2 * g:c + 2 * g + 2, :]

            def out_key(name, layer):
                return lambda c: (name, layer, c // 2, c % 2)

            def mlp(i):
                x_norm()
                for g in range(16):
                    act.wait_ge(sem("products_done"), group("mlp_w1", i, g // 2, g % 2))
                    if g >= 2:
                        act.wait_ge(sem("hidden_ready"), W.next("hidden_ready"))
                    f(act_s[:, g % 2, :], ps[:, 4 + g % 4, :], ACT.Relu).then_inc(sem("act_ready"), 1)
                act.wait_ge(sem("hidden_ready"), W.next("hidden_ready", 2))
                post_norm(lambda c: ("mlp_w2", i, 7, c))

            def ffn(kind, l):
                x_norm()
                for n in range(22):
                    act.wait_ge(sem("products_done"), group(kind, l, n // 2, n % 2))
                    if n >= 2:
                        act.wait_ge(sem("hidden_ready"), W.next("hidden_ready"))
                    f(act_s[:, n % 2, 0:T], ps[:, 4 + n % 4, 0:T], ACT.Silu).then_inc(sem("act_ready"), 1)
                act.wait_ge(sem("hidden_ready"), W.next("hidden_ready", 2))

            def gdn(i):
                j = i // 3
                x_norm()
                act.wait_ge(sem("tok_raw"), W.next("tok_raw"))
                W.chain(f(tokg[:, 32:48], tokg[:, 16:32], ACT.Abs))
                W.chain(f(tokg[:, 32:48], tokg[:, 32:48], ACT.Exp, scale=-1.0))
                f(tokg[:, 32:48], tokg[:, 32:48], ACT.Ln, bias=1.0)
                f(tokg[:, 64:72], bcast[:, 8 * j:8 * j + 8], ACT.Exp)
                f(tokg[:, 48:64], tokg[:, 48:64], ACT.Exp, scale=-1.0).then_inc(sem("tok_exp"), 1)
                act.wait_ge(sem("pad_set"), W.next("pad_set"))

                def silu(g):
                    act.wait_ge(sem("conv_done"), W.next("conv_done"))
                    if g < 8:
                        dst = qk[:, 2 * g:2 * g + 2, :]
                    else:
                        if g >= 10:
                            move(g - 10)
                        dst = vch[:, g % 2, :, :]
                    f(dst, conv[:, g % 2, :, :], ACT.Silu).then_inc(sem("silu_done"), 1)

                def move(g):
                    act.wait_ge(sem("v_turned"), W.next("v_turned"))
                    f(v_tok[:, :, T * g:T * (g + 1)], ps[:, 2, :].rearrange("p (i n) -> p i n", i=TT),
                      ACT.Copy).then_inc(sem("v_done"), 1)

                for g in range(16):
                    act.wait_ge(sem("products_done"), group("gdn_w_in", j, g // 2, g % 2))
                    if 2 <= g < 12:
                        silu(g - 2)
                    if g < 12:
                        f(pre[:, g % 2, :, 3:3 + T], two(ps[:, 4 + g % 4, :]), ACT.Copy).then_inc(sem("evac"), 1)
                    else:
                        c = 2 * (g - 12)
                        f(gate[:, c:c + 2, :], two(ps[:, 4 + g % 4, :]), ACT.Silu).then_inc(sem("evac"), 1)
                        if g == 13:
                            silu(10)
                            silu(11)
                move(2)
                move(3)
                ln_exp()
                for h in range(8):
                    act.wait_ge(sem("decay_done"), W.next("decay_done"))
                    f(pair[:, h, :], ps[:, 4 + h % 2, 0:ED], ACT.Exp).then_inc(sem("pair_exp"), 1)
                for half in range(2):
                    for b in range(4):
                        if half:
                            act.wait_ge(sem("qk_normed"), W.next("qk_normed"))
                        c = 8 * half + 2 * b
                        f(sq[:, 2 * b:2 * b + 2, :], qk[:, c:c + 2, :], ACT.Square).then_inc(sem("sq_ready"), 1)
                    for b in range(4):
                        act.wait_ge(sem("hs_ready"), W.next("hs_ready"))
                        v = flat(sq[:, 2 * b:2 * b + 2, :])
                        f(v, ps[:, b, :], ACT.Ln, bias=epsc[:, :]).then_inc(sem("hs_free"), 1)
                        act.wait_ge(sem("hs_free"), W.next("hs_free"))
                        f(v, v, ACT.Exp, scale=-0.5).then_inc(sem("hrs_ready"), 1)
                act.wait_ge(sem("qk_normed"), W.next("qk_normed", 4))
                head_norm(4, lambda b: two(ps[:, b, :]), "o_ready")
                post_norm(out_key("gdn_w_out", j))

            def mlstm(i):
                x_norm()
                channels("mlstm_w_in", 0, 0, 4, chunks(qk, 0), scale=0.125)
                channels("mlstm_w_in", 0, 1, 6, chunks(qk, 4))
                act.wait_ge(sem("gates_done"), W.next("gates_done"))
                f(rows[0:8, 0, :], ps[0:8, 0, 0:T], ACT.Tanh, scale=1.0 / 15.0, bias=gb15[:, 0:1])
                W.chain(f(rows[0:8, 1, :], ps[0:8, 0, T:2 * T], ACT.Tanh, scale=1.0 / 15.0, bias=gb15[:, 1:2]))
                ln_exp()
                W.chain(f(rows[0:8, 2, :], rows[0:8, 1, :], ACT.Exp, scale=-15.0))
                f(rows[0:8, 3, :], rows[0:8, 2, :], ACT.Ln, bias=1.0).then_inc(sem("log_ready"), 1)
                tokens("mlstm_w_in", 0, 2, 4, 0)
                tokens("mlstm_w_in", 0, 3, 6, 512)
                act.wait_ge(sem("rows_ready"), W.next("rows_ready"))
                f(rows[0:8, 8, :], rows[0:8, 9, :], ACT.Exp, scale=-1.0).then_inc(sem("floor_ready"), 1)
                channels("mlstm_w_in", 0, 4, 4, chunks(gate, 0), func=ACT.Sigmoid)
                channels("mlstm_w_in", 0, 5, 6, chunks(gate, 4), func=ACT.Sigmoid)
                ln_exp()
                act.wait_ge(sem("rcol_ready"), W.next("rcol_ready"))
                for h in range(8):
                    act.wait_ge(sem("decay_done"), W.next("decay_done"))
                    f(pair[:, h, 0:T], ps[:, h % 2, 0:T], ACT.Exp, bias=rcol[:, 0, h:h + 1])
                    f(pair[:, h, T:ED], ps[:, h % 2, P:T], ACT.Exp, bias=rcol[:, 1, h:h + 1])\
                        .then_inc(sem("pair_exp"), 1)
                for h in range(8):
                    act.wait_ge(sem("den_done"), W.next("den_done"))
                    if h >= 2:
                        act.wait_ge(sem("cell_ready"), W.next("cell_ready"))
                    e = em_s[:, h % 2, 0:T]
                    f(em_s[:, h % 2, T:2 * T], ps[:, 4 + h % 2, T:2 * T], ACT.Copy)
                    f(e, ps[:, 4 + h % 2, 0:T], ACT.Abs).then_inc(sem("em_ready"), 1)
                    act.wait_ge(sem("den_free"), W.next("den_free"))
                    W.chain(f(e, e, ACT.Ln))
                    f(e, e, ACT.Exp, scale=-1.0).then_inc(sem("rden_ready"), 1)
                act.wait_ge(sem("cell_ready"), W.next("cell_ready", 2))
                head_norm(4, lambda b: num_s[:, 2 * b:2 * b + 2, :])
                post_norm(out_key("mlstm_w_out", 0))

            def softmaxes(heads, comps, wide):
                def turned(h):
                    act.wait_ge(sem("prob_turned"), W.next("prob_turned"))
                    f(probT[:, h % 2, 0:ED], ps[:, 3, 0:ED], ACT.Copy).then_inc(sem("probT_ready"), 1)
                    if wide and h % 2:
                        act.wait_ge(sem("o_ready"), W.next("o_ready"))
                        b = h // 2
                        f(num_s[:, 2 * b:2 * b + 2, :], two(ps[:, b % 3, :]), ACT.Copy).then_inc(sem("o_moved"), 1)

                for h in range(heads):
                    for c in range(comps):
                        act.wait_ge(sem("max_ready"), W.next("max_ready"))
                        b = 4 + (comps * h + c) % 4
                        s = stat[:, h % 2, c, :]
                        f(prob[:, h % 2, c, 0:P], ps[:, b, 0:P], ACT.Exp, bias=s[:, 0:1], accum_out=s[:, 2:3])
                        f(prob[:, h % 2, c, P:ED], ps[:, b, P:ED], ACT.Exp, bias=s[:, 1:2], accum_out=s[:, 3:4])\
                            .then_inc(sem("score_free"), 1)
                    if h >= 1:
                        turned(h - 1)
                turned(heads - 1)

            def diff(i):
                x_norm()
                for g in range(8):
                    act.wait_ge(sem("products_done"), group("diff_w_in", 0, g // 2, g % 2))
                    if g >= 4:
                        act.wait_ge(sem("roped"), W.next("roped"))
                    f(raw[:, g % 4, :], ps[:, 4 + g % 4, :], ACT.Copy, scale=0.125 if g < 4 else 1.0)\
                        .then_inc(sem("raw_ready"), 1)
                tokens("diff_w_in", 0, 4, 4, 0)
                tokens("diff_w_in", 0, 5, 6, 512)
                softmaxes(8, 2, True)
                act.wait_ge(sem("o_moved"), W.next("o_moved", 4))
                head_norm(4, lambda b: num_s[:, 2 * b:2 * b + 2, :])
                post_norm(out_key("diff_w_out", 0))

            def hybrid(l):
                x_norm()
                channels("w_in_2", l, 0, 4, chunks(qk, 0), func=ACT.Silu)
                channels("w_in_2", l, 1, 6, chunks(zcum, 0))
                tokens("w_in_2", l, 2, 4, 0)
                channels("w_in_2", l, 3, 6, chunks(gate, 0), func=ACT.Silu)
                channels("w_in_2", l, 4, 4, chunks(qk, 8), scale=0.125)
                channels("w_in_2", l, 5, 6, chunks(qk, 12))
                f(qk[:, 4:8, :], zcum, ACT.Sigmoid, scale=-1.0).then_inc(sem("hk_ready"), 1)
                tokens("w_in_2", l, 6, 4, 512)
                ln_exp()
                W.chain(f(glog, zcum, ACT.Abs))
                W.chain(f(glog, glog, ACT.Exp, scale=-1.0))
                f(glog, glog, ACT.Ln, bias=1.0).then_inc(sem("glog_ready"), 1)
                act.wait_ge(sem("fz_ready"), W.next("fz_ready"))
                W.chain(f(rows[0:8, 2, :], rows[0:8, 1, :], ACT.Abs))
                W.chain(f(rows[0:8, 2, :], rows[0:8, 2, :], ACT.Exp, scale=-1.0))
                f(rows[0:8, 3, :], rows[0:8, 2, :], ACT.Ln, bias=1.0).then_inc(sem("log_ready"), 1)
                if l:
                    act.wait_ge(sem("lse_ready"), W.next("lse_ready"))
                    v = factor[:, 0, :, :]
                    W.chain(f(v, v, ACT.Abs))
                    W.chain(f(v, v, ACT.Exp, scale=-1.0))
                    f(v, v, ACT.Ln, bias=1.0).then_inc(sem("lse_done"), 1)
                for n in range(len(TREE) + 1):
                    act.wait_ge(sem("edge_ready"), W.next("edge_ready"))
                    f(factor[:, n % 2, :, :], factor[:, n % 2, :, :], ACT.Exp).then_inc(sem("factor_exp"), 1)
                head_norm(2, lambda b: two(ps[:, b, :]), "o_ready")
                softmaxes(8, 1, False)
                for b in range(2):
                    act.wait_ge(sem("o_ready"), W.next("o_ready"))
                    f(hT[:, 4 + 2 * b:6 + 2 * b, :], two(ps[:, b, :]), ACT.Copy).then_inc(sem("mix_ready"), 1)

            def cross(l):
                x_norm()
                channels("cross_wq_2", l, 0, 4, chunks(qk, 0), scale=0.0625)
                channels("cross_wq_2", l, 1, 6, chunks(qk, 4), scale=0.0625)
                channels("cross_wk_2", l, 0, 4, chunks(qk, 8))
                channels("cross_wk_2", l, 1, 6, chunks(qk, 12))
                tokens("cross_wv_2", l, 0, 4, 0)
                tokens("cross_wv_2", l, 1, 6, 512)

                def tail(h):
                    act.wait_ge(sem("prob_turned"), W.next("prob_turned"))
                    f(probT[:, h % 2, :], ps[:, 4 + h, :], ACT.Copy).then_inc(sem("probT_ready"), 1)
                    act.wait_ge(sem("o_ready"), W.next("o_ready"))
                    f(hT[:, 2 * h:2 * h + 2, :], two(ps[:, h, :]), ACT.Copy).then_inc(sem("mix_ready"), 1)

                for h in range(4):
                    act.wait_ge(sem("max_ready"), W.next("max_ready"))
                    for t in range(TT):
                        last = f(prob[:, h % 2, 0, t * T:(t + 1) * T], ps[:, 4 + h, t * T:(t + 1) * T], ACT.Exp,
                                 bias=stat[:, h % 2, 0, t:t + 1], accum_out=stat[:, h % 2, 0, 2 + t:3 + t])
                    last.then_inc(sem("score_free"), 1)
                    if h >= 1:
                        tail(h - 1)
                tail(3)

            ln_exp()
            act.wait_ge(sem("ones_set"), W.next("ones_set"))
            act.wait_ge(sem("lambda_sums"), W.next("lambda_sums"))
            f(lwork[:, 130:132], lwork[:, 128:130], ACT.Exp).then_inc(sem("lambda_exp"), 1)
            act.wait_ge(sem("lb_diff"), W.next("lb_diff"))
            W.chain(f(lb[:, 4:8], lb[:, 0:4], ACT.Abs))
            W.chain(f(lb[:, 4:8], lb[:, 4:8], ACT.Exp, scale=-1.0))
            f(lb[:, 8:12], lb[:, 4:8], ACT.Ln, bias=1.0).then_inc(sem("lb_log"), 1)
            act.wait_ge(sem("lb_ready"), W.next("lb_ready"))
            f(lb[:, 24:28], lb[:, 16:20], ACT.Exp).then_inc(sem("lb_prob"), 1)
            act.wait_ge(sem("mem_ready"), W.next("mem_ready", 4))
            for c in range(4):
                f(sq[:, 2 * c:2 * c + 2, :], memT[:, 2 * c:2 * c + 2, :], ACT.Square).then_inc(sem("sq_ready"), 1)
            act.wait_ge(sem("ss_ready"), W.next("ss_ready"))
            rsqrt(ps[:, 7, 0:T], rs_mem[:, :], D, "mem_rs")
            for kind, i in parts:
                scope[0] = kind[:3] + "_"
                {"gdn": gdn, "mlstm": mlstm, "diff": diff, "mlp": mlp, "hybrid": hybrid, "cross": cross,
                 "ffn1": lambda l: ffn("ffn1", l), "ffn2": lambda l: ffn("ffn2", l)}[kind](i)
            x_norm()
            for t in range(TT):
                act.wait_ge(sem("out_turned"), W.next("out_turned"))
                f(out_rows[:, t, :], ps[:, 2 * t:2 * t + 2, :].rearrange("p b n -> p (b n)"), ACT.Copy)\
                    .then_inc(sem("out_tile"), 1)

        @block.vector
        def _(dve):
            scope[0] = ""
            W = Waits(dve, "dve_step")
            tt, ts, stt = dve.tensor_tensor, dve.tensor_scalar, dve.scalar_tensor_tensor

            def x_norm(gain, k0):
                dve.wait_ge(sem("rs_ready"), W.next("rs_ready"))
                for c in range(DC):
                    stt(hT[:, c, :], xT[:, c, :], column(gain, k0 + c), rs[:, :], ALU.mult, ALU.mult)\
                        .then_inc(sem("h_ready"), 1)

            def post_norm(k0):
                dve.wait_ge(sem("rs_ready"), W.next("rs_ready"))
                for c in range(4):
                    for k in (2 * c, 2 * c + 1):
                        ins = stt(sq[:, k, :], ps[:, c, (k % 2) * T:(k % 2 + 1) * T], column("norm_g", k0 + k),
                                  rs[:, :], ALU.mult, ALU.mult)
                    W.chain(ins)
                    tt(xT[:, 2 * c:2 * c + 2, :], xT[:, 2 * c:2 * c + 2, :], sq[:, 2 * c:2 * c + 2, :], ALU.add)\
                        .then_inc(sem("x_ready"), 1)

            def residual(scale, product):
                for c in range(4):
                    dve.wait_ge(sem("products_done"), group(*product(c)))
                    x = xT[:, 2 * c:2 * c + 2, :]
                    stt(x, two(ps[:, c, :]), scale, x, ALU.mult, ALU.add).then_inc(sem("x_ready"), 1)

            def mlp(i):
                x_norm("norm_g", (4 * i + 2) * DC)
                for g in range(16):
                    dve.wait_ge(sem("act_ready"), W.next("act_ready"))
                    tt(hidden[:, 2 * g:2 * g + 2, :], two(act_s[:, g % 2, :]), two(ps[:, 4 + g % 4, :]), ALU.mult)\
                        .then_inc(sem("hidden_ready"), 1)
                post_norm((4 * i + 3) * DC)

            def ffn(kind, l):
                x_norm(f"{kind}_norm_2", l * DC)
                for n in range(22):
                    dve.wait_ge(sem("act_ready"), W.next("act_ready"))
                    tt(hidden[:, n, :], act_s[:, n % 2, 0:T], ps[:, 4 + n % 4, T:2 * T], ALU.mult)\
                        .then_inc(sem("hidden_ready"), 1)
                residual(0.5, lambda c: (f"{kind}_w_down_2", l, 5, c))

            def head_out(n, src, gain, gated, name="mix_ready"):
                for b in range(n):
                    dve.wait_ge(sem("hrs_ready"), W.next("hrs_ready"))
                    for k in (2 * b, 2 * b + 1):
                        s, r = src(k), sq[:, k, :]
                        ins = stt(r if gated else hT[:, k, :], s, gain(k), r, ALU.mult, ALU.mult)
                    if gated:
                        W.chain(ins)
                        ins = tt(hT[:, 2 * b:2 * b + 2, :], sq[:, 2 * b:2 * b + 2, :], gate[:, 2 * b:2 * b + 2, :],
                                 ALU.mult)
                    ins.then_inc(sem(name), 1)

            def in_bank(k):
                return ps[:, k // 2, (k % 2) * T:(k % 2 + 1) * T]

            def gdn(i):
                j, no = i // 3, gdn_no[i]
                dve.wait_ge(sem("conv_turned"), W.next("conv_turned"))
                W.chain(dve.tensor_copy(convw, ps[:, 3, 0:96]))
                x_norm("norm_g", 4 * i * DC)
                dve.wait_ge(sem("gates_done"), W.next("gates_done"))
                ab = ps[:, 3, 128:160].rearrange("p (t n) -> p t n", t=TT)

                def th(a):
                    return tokg[:, a:a + 16].rearrange("p (t h) -> p t h", t=TT)

                tt(th(16), ab[:, :, 0:8], bcast[:, 16 + 8 * j:24 + 8 * j][:, None, :].broadcast_to([P, TT, 8]), ALU.add)
                dve.tensor_copy(th(48), ab[:, :, 8:16]).then_inc(sem("tok_raw"), 1)
                dve.wait_ge(sem("tok_exp"), W.next("tok_exp"))
                W.chain(stt(tokg[:, 16:32], tokg[:, 16:32], 0.0, tokg[:, 32:48], ALU.max, ALU.add))
                stt(th(0), th(16), -1.0, tokg[:, 64:72][:, None, :].broadcast_to([P, TT, 8]), ALU.mult, ALU.mult)
                W.chain(ts(tokg[:, 48:64], tokg[:, 48:64], 1.0, None, ALU.add))
                dve.reciprocal(tokg[:, 80:96], tokg[:, 48:64]).then_inc(sem("tok_gates"), 1)
                for g in range(12):
                    dve.wait_ge(sem("evac"), W.next("evac"))
                    if g >= 2:
                        dve.wait_ge(sem("silu_done"), W.next("silu_done"))
                    b = g % 2
                    done = [0, 0]
                    for k in (3, 2, 1, 0):
                        for c in range(2):
                            w = convw[:, k * 24 + 2 * g + c:k * 24 + 2 * g + c + 1]
                            src, dst = pre[:, b, c, k:k + T], conv[:, b, c, :]
                            if k == 3:
                                done[c] = W.mark(ts(dst, src, w, None, ALU.mult))
                            else:
                                dve.wait_ge(sem("dve_step"), done[c])
                                ins = stt(dst, src, w, dst, ALU.mult, ALU.add)
                                if k or not c:
                                    done[c] = W.mark(ins)
                    ins.then_inc(sem("conv_done"), 1)
                dve.wait_ge(sem("silu_done"), W.next("silu_done", 2))
                dve.wait_ge(sem("evac"), W.next("evac", 4))
                for b in range(8):
                    dve.wait_ge(sem("hrs_ready"), W.next("hrs_ready"))
                    c = 2 * b
                    v = qk[:, c:c + 2, :]
                    tt(v, v, sq[:, c % 8:c % 8 + 2, :], ALU.mult).then_inc(sem("qk_normed"), 1)
                for h in range(8):
                    dve.wait_ge(sem("score_done"), W.next("score_done"))
                    dve.wait_ge(sem("pair_masked"), W.next("pair_masked"))
                    for t, (a, e) in enumerate(((0, T), (T, ED))):
                        ins = stt(kkb[:, h, a:e], ps[:, h % 4, a:e], tokg[:, 80 + 8 * t + h:81 + 8 * t + h],
                                  pair[:, h, a:e], ALU.mult, ALU.mult)
                    ins.then_inc(sem("score_free"), 1)
                for h in range(8):
                    dve.wait_ge(sem("score_done"), W.next("score_done"))
                    stt(pair[:, h, :], ps[:, h % 4, 0:ED], P ** -0.5, pair[:, h, :], ALU.mult, ALU.mult)\
                        .then_inc(sem("score_free"), 1)
                for n in range(len(TREE)):
                    m = cc("tree_ts", n)[:, None, :].broadcast_to([P, 4, P])
                    for q in range(4):
                        t, h0 = q // 2, 4 * (q % 2)
                        dve.wait_ge(sem("level_done"), W.next("level_done"))
                        tt(level[:, t, h0:h0 + 4, :], ps[:, 4 + q, :].rearrange("p (h n) -> p h n", h=4), m, ALU.mult)\
                            .then_inc(sem("level_masked"), 1)
                    for q in range(4):
                        t, h0 = q // 2, 4 * (q % 2)
                        dve.wait_ge(sem("delta_done"), W.next("delta_done"))
                        for bank, x in ((2 * (q % 2), inv), (2 * (q % 2) + 1, invT)):
                            if x is inv and n == len(TREE) - 1:
                                continue
                            v = x[:, t, h0:h0 + 4, :]
                            ins = tt(v, v, ps[:, bank, :].rearrange("p (h n) -> p h n", h=4), ALU.subtract)
                        ins.then_inc(sem("inverse_done"), 1)

                def times_beta(t, b, bank):
                    return tt(u_sol[:, t, 512 * b:512 * (b + 1)].rearrange("p (h n) -> p h n", h=4),
                              ps[:, bank, :].rearrange("p (h n) -> p h n", h=4),
                              tokg[:, 80 + 8 * t + 4 * b:84 + 8 * t + 4 * b][:, :, None].broadcast_to([P, 4, P]),
                              ALU.mult)

                for b in range(2):
                    dve.wait_ge(sem("w_done"), W.next("w_done"))
                    dve.tensor_copy(w_sol[:, 0, 512 * b:512 * (b + 1)], ps[:, 4 + b, :]).then_inc(sem("w_ready"), 1)
                    times_beta(0, b, 4 + b)
                for b in range(2):
                    dve.wait_ge(sem("w_done"), W.next("w_done"))
                    v = v_tok[:, 1, 512 * b:512 * (b + 1)]
                    tt(v, v, ps[:, 6 + b, :], ALU.subtract).then_inc(sem("w_ready"), 1)
                for b in range(2):
                    dve.wait_ge(sem("w_done"), W.next("w_done"))
                    times_beta(1, b, 4 + b).then_inc(sem("w_ready"), 1)
                head_out(4, in_bank, lambda k: column("gdn_norm_g", j), True)
                post_norm((4 * i + 1) * DC)

            def mlstm(i):
                x_norm("norm_g", 4 * i * DC)
                r = lambda k: rows[0:8, k, :]
                one = ones[0:8, :]
                dve.wait_ge(sem("log_ready"), W.next("log_ready"))
                W.chain(dve.tensor_tensor_scan(r(4), one, r(3), 0.0, ALU.mult, ALU.subtract))
                W.chain(stt(r(6), r(0), 15.0, r(4), ALU.mult, ALU.subtract))
                W.chain(dve.tensor_tensor_scan(r(5), one, r(6), 0.0, ALU.mult, ALU.max))
                ts(r(7), r(5), -1.0, None, ALU.mult)
                tt(r(9), r(4), r(5), ALU.add).then_inc(sem("rows_ready"), 1)
                dve.wait_ge(sem("r_turned"), W.next("r_turned"))
                dve.tensor_copy(rcol.rearrange("p i h -> p (i h)"), ps[:, 1, 0:16]).then_inc(sem("rcol_ready"), 1)
                for h in range(8):
                    dve.wait_ge(sem("score_done"), W.next("score_done"))
                    dve.wait_ge(sem("pair_masked"), W.next("pair_masked"))
                    tt(pair[:, h, :], ps[:, 4 + h % 4, 0:ED], pair[:, h, :], ALU.mult).then_inc(sem("score_free"), 1)
                for h in range(8):
                    dve.wait_ge(sem("em_ready"), W.next("em_ready"))
                    e = em_s[:, h % 2, 0:T]
                    tt(e, e, em_s[:, h % 2, T:2 * T], ALU.max).then_inc(sem("den_free"), 1)
                    dve.wait_ge(sem("rden_ready"), W.next("rden_ready"))
                    tt(num_s[:, h, :], in_bank(h), e, ALU.mult).then_inc(sem("cell_ready"), 1)
                head_out(4, lambda k: num_s[:, k, :], lambda k: column("mlstm_norm_g", k), True)
                post_norm((4 * i + 1) * DC)

            def softmaxes(heads, comps):
                def normalize(h):
                    dve.wait_ge(sem("score_free"), W.next("score_free", comps))
                    s = stat[:, h % 2, :, :]
                    W.chain(dve.reciprocal(s[:, 0:comps, 2:4], s[:, 0:comps, 2:4]))
                    if comps == 2:
                        W.chain(ts(s[:, 1, 2:4], s[:, 1, 2:4], bcast[:, 33:34], None, ALU.mult))
                    for k, (a, e) in enumerate(((0, P), (P, ED))):
                        p = prob[:, h % 2, 0, a:e]
                        ins = ts(p, p, s[:, 0, 2 + k:3 + k], None, ALU.mult)
                    if comps == 2:
                        W.chain(ins)
                        for k, (a, e) in enumerate(((0, P), (P, ED))):
                            p = prob[:, h % 2, 1, a:e]
                            ins = stt(p, p, s[:, 1, 2 + k:3 + k], prob[:, h % 2, 0, a:e], ALU.mult, ALU.add)
                    ins.then_inc(sem("prob_ready"), 1)

                for h in range(heads):
                    for c in range(comps):
                        dve.wait_ge(sem("score_done"), W.next("score_done"))
                        b = 4 + (comps * h + c) % 4
                        for k, (a, e) in enumerate(((0, P), (P, ED))):
                            ins = dve.tensor_reduce(stat[:, h % 2, c, k:k + 1], ps[:, b, a:e], AX, ALU.max,
                                                    negate=True)
                        ins.then_inc(sem("max_ready"), 1)
                    if h >= 1:
                        normalize(h - 1)
                normalize(heads - 1)

            def diff(i):
                x_norm("norm_g", 4 * i * DC)
                both = lambda name: cc(name)[:, None, :].broadcast_to([P, 2, T])
                for g in range(8):
                    dve.wait_ge(sem("rotated"), W.next("rotated"))
                    v, s = qk[:, 2 * g:2 * g + 2, :], two(probT[:, g % 2, :])
                    tt(v, two(raw[:, g % 4, :]), both("cos"), ALU.mult)
                    W.chain(tt(s, two(ps[:, g % 2, :]), both("sin"), ALU.mult))
                    tt(v, v, s, ALU.add).then_inc(sem("roped"), 1)
                softmaxes(8, 2)
                head_out(4, lambda k: num_s[:, k, :], lambda k: bcast[:, 34:35], False)
                post_norm((4 * i + 1) * DC)

            def hybrid(l):
                x_norm("mix_norm_2", l * DC)
                dve.memset(pair[:, 0:4, :], 0.0)
                r = lambda k: rows[0:8, k, :]
                dve.wait_ge(sem("gates_done"), W.next("gates_done"))
                ts(r(1), ps[0:8, 0, 0:T], gbias[:, 2 + l:3 + l], None, ALU.add).then_inc(sem("fz_ready"), 1)
                dve.wait_ge(sem("hk_ready"), W.next("hk_ready"))
                if l:
                    for h in range(4):
                        ts(qk[:, 4 + h, :], qk[:, 4 + h, :], lb[:, 24 + h:25 + h], None, ALU.mult)
                dve.wait_ge(sem("glog_ready"), W.next("glog_ready"))
                W.chain(stt(glog, zcum, 0.0, glog, ALU.min, ALU.subtract))
                dve.wait_ge(sem("log_ready"), W.next("log_ready"))
                W.chain(stt(r(4), r(1), 0.0, r(3), ALU.min, ALU.subtract))
                W.chain(dve.tensor_tensor_scan(r(5), ones[0:8, :], r(4), 0.0, ALU.mult, ALU.add))
                ts(r(7), r(5), -1.0, None, ALU.mult).then_inc(sem("rows_ready"), 1)
                if l:
                    for h in range(4):
                        ins = ts(glog[:, h, :], glog[:, h, :], lb[:, 16 + h:17 + h], None, ALU.add)
                    W.chain(ins)
                    for h in range(4):
                        ins = ts(factor[:, 0, h, :], glog[:, h, :], lb[:, 12 + h:13 + h], None, ALU.subtract)
                    ins.then_inc(sem("lse_ready"), 1)
                    dve.wait_ge(sem("lse_done"), W.next("lse_done"))
                    for h in range(4):
                        ins = stt(glog[:, h, :], glog[:, h, :], lb[:, 12 + h:13 + h], factor[:, 0, h, :],
                                  ALU.max, ALU.add)
                    W.chain(ins)
                for h in range(4):
                    ins = dve.tensor_tensor_scan(zcum[:, h, :], ones[:, :], glog[:, h, :], 0.0, ALU.mult, ALU.add)
                W.chain(ins)

                def split(v, m):
                    v = v.rearrange("p h t -> p (h t)").rearrange("p (b n) -> p b n", n=2 * m)
                    return v[:, :, 0:m], v[:, :, m:2 * m], v[:, :, m - 1:m].broadcast_to([P, 4 * T // (2 * m), m])

                spans = TREE + [P]

                def edges(n):
                    gl, gr, edge = split(zcum, spans[n])
                    fl, fr, _ = split(factor[:, n % 2, :, :], spans[n])
                    tt(fl, edge, gl, ALU.subtract)
                    tt(fr, gr, edge, ALU.subtract).then_inc(sem("edge_ready"), 1)

                def apply(n):
                    dve.wait_ge(sem("factor_exp"), W.next("factor_exp"))
                    fl, fr, _ = split(factor[:, n % 2, :, :], spans[n])
                    kl, _, _ = split(qk[:, 4:8, :], spans[n])
                    _, qr, _ = split(qk[:, 0:4, :], spans[n])
                    tt(fl, fl, kl, ALU.mult)
                    tt(fr, fr, qr, ALU.mult).then_inc(sem("factor_ready"), 1)

                def copy_level(n):
                    for t in range(1 if n == len(TREE) else TT):
                        dve.wait_ge(sem("tree_done"), W.next("tree_done"))
                        if tree_m[0] >= 2:
                            dve.wait_ge(sem("tree_copied"), W.next("tree_copied"))
                        data = ps[:, 4 + tree_m[0] % 4, :].rearrange("p (h n) -> p h n", h=4)
                        tree_m[0] += 1
                        if n == len(TREE):
                            dve.tensor_copy(pair[:, 0:4, P:T], data).then_inc(sem("tree_copied"), 1)
                            continue
                        m = ident if n > len(TREE) else cc("tree_st", n)
                        dst = pair[:, 0:4, 0:P] if t == 0 else pair[:, 0:4, T:ED]
                        dve.copy_predicated(dst, m.bitcast(I32)[:, None, :].broadcast_to([P, 4, P]), data)\
                            .then_inc(sem("tree_copied"), 1)

                tree_m = [0]
                edges(0)
                edges(1)
                apply(0)
                for n in range(len(TREE) + 1):
                    if n + 1 <= len(TREE):
                        apply(n + 1)
                    copy_level(n)
                    if n + 2 <= len(TREE):
                        edges(n + 2)
                copy_level(len(TREE) + 1)
                dve.wait_ge(sem("tree_copied"), W.next("tree_copied", 2))
                head_out(2, in_bank, lambda k: column("hgrn_out_norm_2", l), True, "hgrn_mixed")
                softmaxes(8, 1)
                residual(1.0, lambda c: ("w_out_2", l, c // 2, c % 2))

            def cross(l):
                for c in range(DC):
                    stt(mem_n[:, c, :], memT[:, c, :], column("mem_norm_2", l * DC + c), rs_mem[:, :],
                        ALU.mult, ALU.mult).then_inc(sem("mem_normed"), 1)
                x_norm("cross_norm_2", l * DC)

                def normalize(h):
                    dve.wait_ge(sem("score_free"), W.next("score_free"))
                    s = stat[:, h % 2, 0, :]
                    W.chain(dve.reciprocal(s[:, 2:4], s[:, 2:4]))
                    for t in range(TT):
                        p = prob[:, h % 2, 0, t * T:(t + 1) * T]
                        ins = ts(p, p, s[:, 2 + t:3 + t], None, ALU.mult)
                    ins.then_inc(sem("prob_ready"), 1)

                for h in range(4):
                    dve.wait_ge(sem("score_done"), W.next("score_done"))
                    dve.tensor_reduce(stat[:, h % 2, 0, 0:2], two(ps[:, 4 + h, :]), AX, ALU.max, negate=True)\
                        .then_inc(sem("max_ready"), 1)
                    if h >= 1:
                        normalize(h - 1)
                normalize(3)
                residual(1.0, lambda c: ("cross_wo_2", l, c // 2, c % 2))

            for c in range(4):
                dve.wait_ge(sem("x_turned"), W.next("x_turned"))
                dve.tensor_copy(xT[:, 2 * c:2 * c + 2, :], two(ps[:, 4 + c, :])).then_inc(sem("x_ready"), 1)
            for c in range(4):
                dve.wait_ge(sem("mem_turned"), W.next("mem_turned"))
                dve.tensor_copy(memT[:, 2 * c:2 * c + 2, :], two(ps[:, 4 + c, :])).then_inc(sem("mem_ready"), 1)
            dve.wait_ge(sem("vec_turned"), W.next("vec_turned"))
            dve.tensor_copy(vec[:, :], ps[:, 0, 0:NVEC])
            W.chain(dve.tensor_copy(bcast[:, 0:32], ps[:, 0, 256:288]))
            tt(lwork[:, 0:64], lrow[:, 0:64], lrow[:, 64:128], ALU.mult)
            W.chain(tt(lwork[:, 64:128], lrow[:, 128:192], lrow[:, 192:256], ALU.mult))
            dve.tensor_reduce(lwork[:, 128:130], lwork[:, 0:128].rearrange("p (a n) -> p a n", a=2), AX, ALU.add)\
                .then_inc(sem("lambda_sums"), 1)
            k = VCOL["hgrn_lb_2"]
            tt(lb[:, 0:4], vec[:, k:k + 4], vec[:, k + 4:k + 8], ALU.subtract).then_inc(sem("lb_diff"), 1)
            dve.wait_ge(sem("lambda_exp"), W.next("lambda_exp"))
            stt(lwork[:, 130:131], lwork[:, 130:131], LAMBDA_INIT, lwork[:, 131:132], ALU.add, ALU.subtract)\
                .then_inc(sem("lambda_ready"), 1)
            dve.wait_ge(sem("lb_log"), W.next("lb_log"))
            W.chain(ts(lb[:, 20:24], lb[:, 0:4], -1.0, None, ALU.mult))
            stt(lb[:, 12:16], lb[:, 20:24], 0.0, lb[:, 8:12], ALU.min, ALU.subtract)
            stt(lb[:, 16:20], lb[:, 0:4], 0.0, lb[:, 8:12], ALU.min, ALU.subtract).then_inc(sem("lb_ready"), 1)
            dve.wait_ge(sem("lambda_spread"), W.next("lambda_spread"))
            dve.tensor_copy(bcast[:, 32:33], ps[:, 1, 0:1])
            ts(bcast[:, 33:34], ps[:, 1, 0:1], -1.0, None, ALU.mult)
            dve.wait_ge(sem("gates_in"), W.next("gates_in", 16 * 9))
            ts(gb15[:, :], gbias[:, :], 1.0 / 15.0, None, ALU.mult)
            dve.wait_ge(sem("lb_prob"), W.next("lb_prob"))
            dve.wait_ge(sem("mem_rs"), W.next("mem_rs"))
            ts(bcast[:, 34:35], column("diff_norm_g", 0), 1.0 - LAMBDA_INIT, None, ALU.mult)\
                .then_inc(sem("params_ready"), 1)
            for kind, i in parts:
                scope[0] = kind[:3] + "_"
                {"gdn": gdn, "mlstm": mlstm, "diff": diff, "mlp": mlp, "hybrid": hybrid, "cross": cross,
                 "ffn1": lambda l: ffn("ffn1", l), "ffn2": lambda l: ffn("ffn2", l)}[kind](i)
            x_norm("final_norm_2", 0)


_INS = ["x", "norm_g", "mlp_w1", "mlp_w2", "gdn_w_in", "gdn_conv", "gdn_a_log", "gdn_dt_bias", "gdn_norm_g",
        "gdn_w_out", "mlstm_w_in", "mlstm_gate_b", "mlstm_norm_g", "mlstm_w_out", "diff_w_in", "diff_lambda",
        "diff_norm_g", "diff_w_out", "mem_2", "ffn1_norm_2", "ffn1_w_gate_2", "ffn1_w_up_2", "ffn1_w_down_2",
        "mix_norm_2", "w_in_2", "hgrn_lb_2", "hgrn_out_norm_2", "fox_f_bias_2", "w_out_2", "cross_norm_2",
        "mem_norm_2", "cross_wq_2", "cross_wk_2", "cross_wv_2", "cross_wo_2", "ffn2_norm_2", "ffn2_w_gate_2",
        "ffn2_w_up_2", "ffn2_w_down_2", "final_norm_2"]


def kernel(**inputs):
    import concourse.bacc as _bacc
    from concourse.bass_utils import run_bass_kernel_spmd as _run

    nc = _bacc.Bacc("TRN2", target_bir_lowering=False, num_devices=1)
    arrays, io = {}, {}
    for name in _INS:
        a = np.ascontiguousarray(inputs[name])
        arrays[f"in_{name}"] = a
        io[name] = nc.dram_tensor(f"in_{name}", a.shape, F32, kind="ExternalInput").ap()
    arrays["shape_constants"] = shape_constants()
    io["shape_constants"] = nc.dram_tensor("shape_constants", (P, NCONST), F32, kind="ExternalInput").ap()
    out = nc.dram_tensor("out", (1, T, D), F32, kind="ExternalOutput").ap()
    program(nc, io, out)
    r = _run(nc, [arrays], core_ids=[0])
    return r.results[0]["out"]
```

```python
import math
from contextlib import ExitStack

import numpy as np

import concourse.bass as bass
from concourse import mybir

F32 = mybir.dt.float32
F32R = mybir.dt.float32r
I32 = mybir.dt.int32
ALU = mybir.AluOpType
ACT = mybir.ActivationFunctionType
AX = mybir.AxisListType.X

P = 128
T = 256
TT = T // P
D = 1024
DC = D // P
EPS = 1e-6
RING = 3
PARTS = 2
SLAB = 2048
NEG = -1e30
ARENA = 21504
TREE = [1, 2, 4, 8, 16, 32, 64]
ED = 384

CONST = {}
_at = 0
for _name, _n in (("ident", P), ("after", P), ("upto", T), ("neg_causal", P), ("neg_block", P),
                  ("rotate", P), ("cos", T), ("sin", T), ("tree_ts", 7 * P), ("tree_st", 7 * P)):
    CONST[_name] = (_at, _at + _n)
    _at += _n
NCONST = _at


def shape_constants():
    c = np.zeros((P, NCONST), np.float32)
    row, col = np.arange(P)[:, None], np.arange(P)[None, :]

    def put(name, value):
        c[:, CONST[name][0]:CONST[name][1]] = value

    put("ident", row == col)
    put("after", row > col)
    put("upto", row <= np.arange(T)[None, :])
    put("neg_causal", np.where(col > row, NEG, 0.0))
    put("neg_block", np.where(col // 64 > row // 64, NEG, 0.0))
    rot = np.zeros((P, P), np.float32)
    cos, sin = np.ones((P, T), np.float32), np.zeros((P, T), np.float32)
    inv = (np.float32(500000.0) ** (-np.arange(0, 16, 2, dtype=np.float32) / np.float32(16))).astype(np.float32)
    ang = (np.arange(T, dtype=np.float32)[None, :] * inv[:, None]).astype(np.float32)
    for base in (0, 64):
        for j in range(8):
            rot[base + 8 + j, base + j] = -1.0
            rot[base + j, base + 8 + j] = 1.0
            for k in (j, 8 + j):
                cos[base + k] = np.cos(ang[j])
                sin[base + k] = np.sin(ang[j])
    put("rotate", rot)
    put("cos", cos)
    put("sin", sin)
    ts = []
    for m in TREE:
        same = row // (2 * m) == col // (2 * m)
        ts.append((same & (row % (2 * m) >= m) & (col % (2 * m) < m)).astype(np.float32))
    put("tree_ts", np.concatenate(ts, 1))
    put("tree_st", np.concatenate([m.T for m in ts], 1))
    return c


VROWS = [("norm_g", 128), ("ffn1_norm_2", 16), ("mix_norm_2", 16), ("cross_norm_2", 16), ("mem_norm_2", 16),
         ("ffn2_norm_2", 16), ("final_norm_2", 8), ("mlstm_norm_g", 8), ("hgrn_lb_2", 8),
         ("hgrn_out_norm_2", 2), ("gdn_norm_g", 2), ("diff_norm_g", 1)]
VCOL = {}
_at = 0
for _name, _n in VROWS:
    VCOL[_name] = _at
    _at += _n
NVEC = _at

DEPTH = 4
LAYERS2 = 2


def schedule():
    parts = []
    for i in range(DEPTH):
        parts += [(("gdn", "mlstm", "diff")[i % 3], i), ("mlp", i)]
    for l in range(LAYERS2):
        parts += [("ffn1", l), ("hybrid", l), ("cross", l), ("ffn2", l)]
    return parts


def slabs_of(kind, i):
    def cols(name, layer, n):
        return [(name, layer, "cols", j, 1) for j in range(n)]

    if kind == "gdn":
        return cols("gdn_w_in", i // 3, 16) + cols("gdn_w_out", i // 3, 4)
    if kind == "mlstm":
        return cols("mlstm_w_in", i // 3, 12) + cols("mlstm_w_out", i // 3, 4)
    if kind == "diff":
        return cols("diff_w_in", i // 3, 12) + cols("diff_w_out", i // 3, 4)
    if kind == "mlp":
        return cols("mlp_w1", i, 16) + [("mlp_w2", i, "rows", j, 4 if j == 15 else 1) for j in range(16)]
    if kind in ("ffn1", "ffn2"):
        return ([(kind, i, "gate_up", j, 1) for j in range(22)]
                + [(f"{kind}_w_down_2", i, "rows", j, 4 if j == 10 else 1) for j in range(11)])
    if kind == "hybrid":
        return cols("w_in_2", i, 14) + cols("w_out_2", i, 4)
    assert kind == "cross"
    return (cols("cross_wq_2", i, 4) + cols("cross_wk_2", i, 4) + cols("cross_wv_2", i, 4)
            + cols("cross_wo_2", i, 4))


SHARED = ("x_ready", "sq_ready", "ss_ready", "rs_ready", "h_ready", "products_done", "slab_in", "stored", "out_",
          "high_split", "low_split", "hH_ready", "hL_ready", "mixH_ready", "mixL_ready", "pe_step", "act_step", "dve_step", "pool_step", "gates_in")

LAMBDA_INIT = 0.8 - 0.6 * math.exp(-0.3 * 2)


def program(nc, io, out, parts=None):
    parts = schedule() if parts is None else parts

    slabs, slab_no, groups_before = [], {}, {}
    count = 0
    for kind, i in parts:
        for s in slabs_of(kind, i):
            key = (s[0], s[1], s[3])
            slab_no[key] = len(slabs)
            groups_before[key] = count
            count += s[4]
            slabs.append(s + (count,))
    filled, landed = [0] * RING, []
    for n, s in enumerate(slabs):
        filled[n % RING] += 16 * (2 if s[2] == "gate_up" else 1)
        landed.append(filled[n % RING])
    x_at = {p: 4 * (n + 1) for n, p in enumerate(parts)}
    gdn_no = {i: n for n, (k, i) in enumerate([p for p in parts if p[0] == "gdn"])}

    with ExitStack() as ctx:
        def sb(name, shape, dt=F32):
            return ctx.enter_context(nc.sbuf_tensor(name, shape, dt))

        sems, scope = {}, [""]

        def sem(name):
            if not name.startswith(SHARED):
                name = scope[0] + name
            if name not in sems:
                sems[name] = ctx.enter_context(nc.semaphore(name))
            return sems[name]

        class Waits:

            def __init__(self, eng, step):
                self.eng, self.seen, self.step, self.steps = eng, {}, sem(step), 0

            def next(self, name, n=1):
                key = sem(name).name
                self.seen[key] = self.seen.get(key, 0) + n
                return self.seen[key]

            def mark(self, ins):
                self.steps += 1
                ins.then_inc(self.step, 1)
                return self.steps

            def chain(self, ins):
                self.eng.wait_ge(self.step, self.mark(ins))

        def group(name, layer, j, g=0):
            return groups_before[(name, layer, j)] + g + 1

        xT = sb("xT", [P, DC, T])
        hT = sb("hT", [P, DC, T])
        sq = sb("sq", [P, DC, T])
        rs = sb("rs", [P, T])
        rs_mem = sb("rs_mem", [P, T])
        hH = sb("hH", [P, DC, T], F32R)
        hL = sb("hL", [P, DC, T], F32R)
        ring = sb("ring", [P, RING, SLAB])
        wH = sb("wH", [P, PARTS, SLAB], F32R)
        wL = sb("wL", [P, PARTS, SLAB], F32R)
        const = sb("const", [P, NCONST])
        ones = sb("ones", [P, T])
        epsc = sb("epsc", [P, 1])
        memT = sb("memT", [P, DC, T])
        vec = sb("vec", [P, NVEC])
        bcast = sb("bcast", [P, 40])
        lb = sb("lb", [P, 28])
        gw = sb("gw", [P, 5, DC, 16])
        gbias = sb("gbias", [8, 4])
        gb15 = sb("gb15", [8, 4])
        with nc.sbuf_tensor("hidden_parts", [P, 2, 32, T], F32R) as hidden_parts:
            hidH, hidL = hidden_parts[:, 0, :, :], hidden_parts[:, 1, :, :]
        arena = sb("arena", [P, ARENA])
        ps = ctx.enter_context(nc.psum_tensor("ps", [P, 8, 512], F32))

        def cc(name, k=None):
            a, b = CONST[name]
            return const[:, a:b] if k is None else const[:, a + k * P:a + (k + 1) * P]

        def column(name, k):
            return vec[:, VCOL[name] + k:VCOL[name] + k + 1]

        ident = cc("ident")

        class Arena:
            def __init__(self, at=0):
                self.at = at

            def take(self, n, pat=None, **k):
                v = arena[:, self.at:self.at + n]
                self.at += n
                assert self.at <= ARENA, self.at
                return v.rearrange(pat, **k) if pat else v

        A = Arena(2 * 32 * T)
        act_s = A.take(2 * 512, "p (b n) -> p b n", b=2)
        prod_s = A.take(2 * 512, "p (b n) -> p b n", b=2)

        A = Arena()
        qk = A.take(16 * T, "p (c t) -> p c t", c=16)
        v_tok = A.take(TT * D, "p (i n) -> p i n", i=TT)
        gate = A.take(DC * T, "p (c t) -> p c t", c=DC)
        pair = A.take(8 * ED, "p (h n) -> p h n", h=8)
        after_pair = A.at
        kkb = A.take(8 * ED, "p (h n) -> p h n", h=8)
        staging = A.at
        inv = A.take(TT * 8 * P, "p (i h n) -> p i h n", i=TT, h=8)
        invT = A.take(TT * 8 * P, "p (i h n) -> p i h n", i=TT, h=8)
        level = A.take(TT * 8 * P, "p (i h n) -> p i h n", i=TT, h=8)
        scaled = A.take(2 * ED, "p (b n) -> p b n", b=2)
        tokg = A.take(96)
        convw = A.take(96)
        w_sol = level.rearrange("p i h n -> p i (h n)")
        u_sol = inv.rearrange("p i h n -> p i (h n)")
        A = Arena(staging)
        pre = A.take(2 * 2 * 260, "p (b c n) -> p b c n", b=2, c=2)
        conv = A.take(2 * 2 * T, "p (b c n) -> p b c n", b=2, c=2)
        vch = A.take(2 * 2 * T, "p (b c n) -> p b c n", b=2, c=2)
        convrow = A.take(P)

        A = Arena(after_pair)
        rows = A.take(12 * T, "p (r t) -> p r t", r=12)
        rcol = A.take(16, "p (i h) -> p i h", i=TT)
        em_s = A.take(2 * 2 * T, "p (b t) -> p b t", b=2)
        lay = A.at
        raw = arena[:, lay:lay + 4 * 512].rearrange("p (b n) -> p b n", b=4)
        prob = A.take(2 * 2 * 512, "p (b c n) -> p b c n", b=2, c=2)
        probT = A.take(2 * 512, "p (b n) -> p b n", b=2)
        stat = A.take(2 * 2 * 4, "p (b c s) -> p b c s", b=2, c=2)
        num_s = A.take(DC * T, "p (c t) -> p c t", c=DC)
        mem_n = num_s
        memH, memL = hidden_parts[:, 0, 24:32, :], hidden_parts[:, 1, 0:8, :]
        A = Arena(lay)
        zcum = A.take(4 * T, "p (h t) -> p h t", h=4)
        glog = A.take(4 * T, "p (h t) -> p h t", h=4)
        factor = num_s.rearrange("p (b h) t -> p b h t", b=2)

        vec_rows, vec_rows2 = arena[:, 0:P], arena[:, P:2 * P]
        brow = arena[0:1, 256:288]
        lrow = arena[0:1, 320:576]
        lwork = arena[0:1, 600:732]
        x_rows = sq[:, :, :].rearrange("p c t -> p (c t)").rearrange("p (i n) -> p i n", i=TT)
        mem_rows = hT[:, :, :].rearrange("p c t -> p (c t)").rearrange("p (i n) -> p i n", i=TT)
        out_rows = memT[:, :, :].rearrange("p c t -> p (c t)").rearrange("p (i n) -> p i n", i=TT)

        def two(v):
            return v.rearrange("p (c t) -> p c t", c=2)

        def slab_source(s):
            name, layer, how, j = s[:4]
            if how == "cols":
                w = io[name][layer].rearrange("(c p) n -> p c n", p=P)
                return [(0, SLAB, DC, w[:, :, 256 * j:256 * (j + 1)])]
            if how == "gate_up":
                g = io[f"{name}_w_gate_2"][layer].rearrange("(c p) n -> p c n", p=P)
                u = io[f"{name}_w_up_2"][layer].rearrange("(c p) n -> p c n", p=P)
                return [(0, DC * P, DC, g[:, :, P * j:P * (j + 1)]),
                        (DC * P, 2 * DC * P, DC, u[:, :, P * j:P * (j + 1)])]
            w = io[name][layer][2 * P * j:2 * P * (j + 1), :].rearrange("(c p) n -> p c n", p=P)
            return [(0, 2 * D, 2, w)]

        def flat_rows(ap):
            names = "abcd"[:len(ap.shape)]
            if len(names) > 1:
                ap = ap.rearrange(f"{' '.join(names)} -> ({' '.join(names)})")
            return ap

        block = ctx.enter_context(nc.Block())

        @block.sync
        def _(sp):
            sp.dma_start(x_rows, io["x"][0].rearrange("(i p) n -> p i n", p=P)).then_inc(sem("x_in"), 16)
            sp.dma_start(const[:, :], io["shape_constants"]).then_inc(sem("const_in"), 16)
            sp.dma_start(mem_rows, io["mem_2"][0].rearrange("(i p) n -> p i n", p=P)).then_inc(sem("mem_in"), 16)
            for n, s in enumerate(slabs):
                if n >= RING:
                    sp.wait_ge(sem("low_split"), n - RING + 1)
                for a, b, c, src in slab_source(s):
                    sp.dma_start(ring[:, n % RING, a:b].rearrange("p (c n) -> p c n", c=c), src)\
                      .then_inc(sem(f"slab_in{n % RING}"), 16)
            for i in range(TT):
                sp.wait_ge(sem("out_tile"), i + 1)
                sp.dma_start(out[0, i * P:(i + 1) * P, :], out_rows[:, i, :]).then_inc(sem("stored"), 16)
            sp.wait_ge(sem("stored"), 16 * TT)

        @block.gpsimd
        def _(pool):
            scope[0] = ""
            W = Waits(pool, "pool_step")
            pool.memset(ones[:, :], 1.0)
            pool.memset(epsc[:, :], EPS).then_inc(sem("ones_set"), 1)
            at = 0
            for name, n in VROWS:
                dst = vec_rows[0:n, :] if name == "norm_g" else vec_rows2[at - P:at - P + n, :]
                pool.dma_start(dst, flat_rows(io[name]).rearrange("(r q) -> r q", q=P)).then_inc(sem("vec_in"), 16)
                at += n
            for b, name in ((0, "gdn_a_log"), (16, "gdn_dt_bias")):
                pool.dma_start(brow[:, b:b + 16], flat_rows(io[name]).rearrange("(a n) -> a n", a=1))\
                    .then_inc(sem("vec_in"), 16)
            pool.dma_start(lrow, flat_rows(io["diff_lambda"]).rearrange("(a n) -> a n", a=1))\
                .then_inc(sem("vec_in"), 16)
            for k, src in enumerate((io["mlstm_gate_b"][0, 0], io["mlstm_gate_b"][0, 1],
                                     io["fox_f_bias_2"][0], io["fox_f_bias_2"][1])):
                pool.dma_start(gbias[:, k:k + 1], src.rearrange("(h a) -> h a", a=1)).then_inc(sem("gates_in"), 16)
            for k, (name, l, c0, n) in enumerate((("gdn_w_in", 0, 4096, 16), ("gdn_w_in", 1, 4096, 16),
                                                  ("mlstm_w_in", 0, 3072, 16), ("w_in_2", 0, 3584, 8),
                                                  ("w_in_2", 1, 3584, 8))):
                pool.dma_start(gw[:, k, :, 0:n],
                               io[name][l].rearrange("(c p) n -> p c n", p=P)[:, :, c0:c0 + n])\
                    .then_inc(sem("gates_in"), 16)

            def mask(h):
                pool.wait_ge(sem("pair_exp"), W.next("pair_exp"))
                v = pair[:, h, :].rearrange("p (k n) -> p k n", k=3)[:, 0:3:2, :]
                pool.affine_select(out=v, in_=v, compare_op=ALU.is_ge, fill=0.0, base=0,
                                   pattern=[[0, 2], [1, P]], channel_multiplier=-1).then_inc(sem("pair_masked"), 1)

            def gdn(i):
                pool.wait_ge(sem("x_ready"), x_at[("gdn", i)])
                pool.dma_start(convrow[0:96, :], io["gdn_conv"][i // 3].rearrange("k (c q) -> (k c) q", q=P))\
                    .then_inc(sem("conv_in"), 16)
                pool.memset(pre[:, :, :, 0:3], 0.0).then_inc(sem("pad_set"), 1)
                pool.wait_ge(sem("tok_gates"), W.next("tok_gates"))
                for h in range(8):
                    if h >= 2:
                        pool.wait_ge(sem("decay_done"), W.next("decay_done"))
                    pool.tensor_scalar(scaled[:, h % 2, 0:T], cc("upto"), tokg[:, h:h + 1], None, ALU.mult)
                    pool.tensor_scalar(scaled[:, h % 2, T:ED], cc("upto")[:, 0:P], tokg[:, 8 + h:9 + h], None,
                                       ALU.mult).then_inc(sem("scaled_ready"), 1)
                    if h >= 1:
                        mask(h - 1)
                mask(7)
                pool.wait_ge(sem("decay_done"), W.next("decay_done", 2))
                pool.wait_ge(sem("v_done"), W.next("v_done", 4))
                for m in (inv, invT):
                    for t in range(TT):
                        last = pool.tensor_copy(m[:, t, :, :], ident[:, None, :].broadcast_to([P, 8, P]))
                last.then_inc(sem("inverse_start"), 1)

            for kind, i in parts:
                scope[0] = kind[:3] + "_"
                if kind == "gdn":
                    gdn(i)
                elif kind == "mlstm":
                    for h in range(8):
                        mask(h)

        @block.tensor
        def _(pe):
            scope[0] = ""
            W = Waits(pe, "pe_step")

            def mm(o, l, r, start, stop, **k):
                return pe.matmul(o, l, r, start=start, stop=stop, **k)

            def high(n, c):
                pe.wait_ge(sem("high_split"), n + 1)
                return wH[:, n % PARTS, :].rearrange("p (c n) -> p c n", c=c)

            def low(n, c):
                pe.wait_ge(sem("low_split"), n + 1)
                return wL[:, n % PARTS, :].rearrange("p (c n) -> p c n", c=c)

            def three(dst, w, x, chunks, at_start=None, first=True, last=True):
                for n in range(3):
                    for k in range(chunks):
                        a, b = [(w[0], x[0]), (w[1], x[0]), (w[0], x[1])][n]
                        if at_start:
                            at_start(n, k)
                        ins = mm(dst, a(k), b(k), first and n == 0 and k == 0, last and n == 2 and k == chunks - 1,
                                 **({"skip_group_check": True} if chunks == 1 else {}))
                return ins

            def h_waits(n, k):
                if n == 0 and k % 2 == 0:
                    pe.wait_ge(sem("hH_ready"), W.next("hH_ready"))
                if n == 2 and k % 2 == 0:
                    pe.wait_ge(sem("hL_ready"), W.next("hL_ready"))

            def bank_of(j):
                return 4 + j % 4

            def to_channels(name, layer, j, bank, first=False, src=(hH, hL), free=None):
                n = slab_no[(name, layer, j)]
                wh, wl = high(n, DC), low(n, DC)
                if free and j >= 4:
                    pe.wait_ge(sem(free), W.next(free))
                for m in range(2):
                    last = three(ps[:, bank, m * T:(m + 1) * T],
                                 [lambda k: wh[:, k, m * P:(m + 1) * P], lambda k: wl[:, k, m * P:(m + 1) * P]],
                                 [lambda k: src[0][:, k, :], lambda k: src[1][:, k, :]], DC,
                                 h_waits if first and m == 0 else None)
                last.then_inc(sem("products_done"), 1)

            def to_tokens(name, layer, j, bank, src=(hH, hL)):
                n = slab_no[(name, layer, j)]
                wh, wl = high(n, DC), low(n, DC)
                for i in range(TT):
                    last = three(ps[:, bank, i * T:(i + 1) * T],
                                 [lambda k: src[0][:, k, i * P:(i + 1) * P], lambda k: src[1][:, k, i * P:(i + 1) * P]],
                                 [lambda k: wh[:, k, :], lambda k: wl[:, k, :]], DC)
                last.then_inc(sem("products_done"), 1)

            def norm_sum():
                for c in range(4):
                    pe.wait_ge(sem("sq_ready"), W.next("sq_ready"))
                    for k in (2 * c, 2 * c + 1):
                        last = mm(ps[:, 7, 0:T], ones[:, 0:P], sq[:, k, :], k == 0, k == DC - 1)
                last.then_inc(sem("ss_ready"), 1)

            def head_sums(n):
                for b in range(n):
                    pe.wait_ge(sem("sq_ready"), W.next("sq_ready"))
                    mm(ps[:, 4 + b, :], ones[:, 0:P], sq[:, 2 * b:2 * b + 2, :], True, True)\
                        .then_inc(sem("hs_ready"), 1)

            def out_product(name, layer):
                def mix_waits(n, k):
                    if n == 0 and k % 2 == 0:
                        pe.wait_ge(sem("mixH_ready"), W.next("mixH_ready"))
                    if n == 2 and k % 2 == 0:
                        pe.wait_ge(sem("mixL_ready"), W.next("mixL_ready"))

                for j in range(4):
                    n = slab_no[(name, layer, j)]
                    wh, wl = high(n, DC), low(n, DC)
                    for m in range(2):
                        last = three(ps[:, j, m * T:(m + 1) * T],
                                     [lambda k: wh[:, k, m * P:(m + 1) * P], lambda k: wl[:, k, m * P:(m + 1) * P]],
                                     [lambda k: hH[:, k, :], lambda k: hL[:, k, :]], DC,
                                     mix_waits if j == 0 and m == 0 else None)
                    last.then_inc(sem("products_done"), 1)

            def down_product(name, layer, chunks, waited):
                for j in range(chunks // 2):
                    n = slab_no[(name, layer, j)]
                    wh, wl = high(n, 2), low(n, 2)
                    for kk in (2 * j, 2 * j + 1):
                        if kk in waited:
                            pe.wait_ge(sem("hidden_ready"), W.next("hidden_ready"))
                        end = kk == chunks - 1
                        for m in range(DC):
                            last = three(ps[:, m // 2, (m % 2) * T:(m % 2 + 1) * T],
                                         [lambda k: wh[:, kk % 2, m * P:(m + 1) * P],
                                          lambda k: wl[:, kk % 2, m * P:(m + 1) * P]],
                                         [lambda k: hidH[:, kk, :], lambda k: hidL[:, kk, :]], 1,
                                         first=kk == 0 and m % 2 == 0, last=end and m % 2 == 1)
                            if end and m % 2:
                                last.then_inc(sem("products_done"), 1)
                    if not end:
                        last.then_inc(sem("products_done"), 1)

            def mlp(i):
                norm_sum()
                for j in range(16):
                    to_channels("mlp_w1", i, j, bank_of(j), first=j == 0, free="bank_read")
                pe.wait_ge(sem("bank_read"), W.next("bank_read", 4))
                down_product("mlp_w2", i, 32, range(0, 32, 2))
                norm_sum()

            def ffn(kind, l):
                norm_sum()
                for n in range(22):
                    u = slab_no[(kind, l, n)]
                    wh, wl = high(u, 2 * DC), low(u, 2 * DC)
                    if n >= 4:
                        pe.wait_ge(sem("bank_read"), W.next("bank_read"))
                    for half in range(2):
                        last = three(ps[:, 4 + n % 4, half * T:(half + 1) * T],
                                     [lambda k: wh[:, half * DC + k, :], lambda k: wl[:, half * DC + k, :]],
                                     [lambda k: hH[:, k, :], lambda k: hL[:, k, :]], DC,
                                     h_waits if n == 0 and half == 0 else None)
                    last.then_inc(sem("products_done"), 1)
                pe.wait_ge(sem("bank_read"), W.next("bank_read", 4))
                down_product(f"{kind}_w_down_2", l, 22, range(22))

            def outputs(heads, values):
                for h in range(heads):
                    b, c0 = h // 2, (h % 2) * T
                    mm(ps[:, b, c0:c0 + T], values(0, h), pair[:, h, 0:T], True, False)
                    last = mm(ps[:, b, c0 + P:c0 + T], values(1, h), pair[:, h, T:ED], False, True)
                    if h % 2:
                        last.then_inc(sem("o_ready"), 1)

            def gdn(i):
                j = i // 3
                pe.wait_ge(sem("conv_in"), W.next("conv_in", 16))
                pe.transpose(ps[:, 3, 0:96], convrow[0:96, :], ident[0:96, 0:96]).then_inc(sem("conv_turned"), 1)
                norm_sum()
                pe.wait_ge(sem("hH_ready"), W.next("hH_ready", 4))
                pe.wait_ge(sem("hL_ready"), W.next("hL_ready", 4))
                for t in range(TT):
                    for k in range(DC):
                        last = mm(ps[:, 3, 128 + 16 * t:144 + 16 * t], hT[:, k, t * P:(t + 1) * P], gw[:, j, k, :],
                                  k == 0, k == DC - 1)
                last.then_inc(sem("gates_done"), 1)

                def turn_values(g):
                    pe.wait_ge(sem("silu_done"), 12 * gdn_no[i] + 8 + g + 1)
                    if g > 0:
                        pe.wait_ge(sem("v_done"), W.next("v_done"))
                    for c in range(2):
                        for t in range(TT):
                            last = pe.transpose(ps[:, 2, (2 * t + c) * P:(2 * t + c + 1) * P],
                                                vch[:, g % 2, c, t * P:(t + 1) * P], ident)
                    last.then_inc(sem("v_turned"), 1)

                for s in range(16):
                    to_channels("gdn_w_in", j, s, bank_of(s), free="evac")
                    if s >= 12:
                        turn_values(s - 12)
                pe.wait_ge(sem("evac"), W.next("evac", 4))
                pe.wait_ge(sem("v_done"), W.next("v_done"))
                for h in range(8):
                    pe.wait_ge(sem("scaled_ready"), W.next("scaled_ready"))
                    if h >= 2:
                        pe.wait_ge(sem("pair_exp"), W.next("pair_exp"))
                    b = 4 + h % 2
                    mm(ps[:, b, 0:T], cc("after"), scaled[:, h % 2, 0:T], True, False)
                    mm(ps[:, b, P:T], ones[:, 0:P], scaled[:, h % 2, T:ED], False, True)
                    mm(ps[:, b, T:ED], cc("after"), scaled[:, h % 2, T:ED], True, True).then_inc(sem("decay_done"), 1)
                pe.wait_ge(sem("pair_exp"), W.next("pair_exp", 2))
                for b in range(8):
                    pe.wait_ge(sem("sq_ready"), W.next("sq_ready"))
                    if b >= 4:
                        pe.wait_ge(sem("hs_free"), W.next("hs_free"))
                    mm(ps[:, b % 4, :], ones[:, 0:P], sq[:, 2 * (b % 4):2 * (b % 4) + 2, :], True, True)\
                        .then_inc(sem("hs_ready"), 1)
                pe.wait_ge(sem("hs_free"), W.next("hs_free", 4))
                pe.wait_ge(sem("qk_normed"), W.next("qk_normed", 8))
                for n in range(16):
                    h, b = n % 8, n % 4
                    r = qk[:, (8 if n < 8 else 0) + h, :]
                    if n >= 4:
                        pe.wait_ge(sem("score_free"), W.next("score_free"))
                    mm(ps[:, b, 0:T], qk[:, 8 + h, 0:P], r, True, True)
                    mm(ps[:, b, T:ED], qk[:, 8 + h, P:T], r[:, P:T], True, True).then_inc(sem("score_done"), 1)
                pe.wait_ge(sem("score_free"), W.next("score_free", 4))
                pe.wait_ge(sem("inverse_start"), W.next("inverse_start"))
                for n in range(len(TREE)):
                    for q in range(4):
                        t, h0 = q // 2, 4 * (q % 2)
                        if n:
                            pe.wait_ge(sem("inverse_done"), 28 * gdn_no[i] + 4 * (n - 1) + q + 1)
                        for h in range(4):
                            c0 = 0 if t == 0 else T
                            last = mm(ps[:, 4 + q, h * P:(h + 1) * P], kkb[:, h0 + h, c0:c0 + P],
                                      inv[:, t, h0 + h, :], True, True)
                        last.then_inc(sem("level_done"), 1)
                    for q in range(4):
                        t, h0 = q // 2, 4 * (q % 2)
                        pe.wait_ge(sem("level_masked"), W.next("level_masked"))
                        if q >= 2:
                            pe.wait_ge(sem("inverse_done"), 28 * gdn_no[i] + 4 * n + q - 1)
                        if n < len(TREE) - 1:
                            for h in range(4):
                                mm(ps[:, 2 * (q % 2), h * P:(h + 1) * P], invT[:, t, h0 + h, :],
                                   level[:, t, h0 + h, :], True, True)
                        for h in range(4):
                            last = mm(ps[:, 2 * (q % 2) + 1, h * P:(h + 1) * P], level[:, t, h0 + h, :],
                                      invT[:, t, h0 + h, :], True, True)
                        last.then_inc(sem("delta_done"), 1)
                pe.wait_ge(sem("inverse_done"), 28 * (gdn_no[i] + 1))

                def solve(b0, b, lhs, rhs):
                    for h in range(4 * b, 4 * b + 4):
                        last = mm(ps[:, b0 + b, (h % 4) * P:(h % 4 + 1) * P], lhs(h), rhs(h), True, True)
                    last.then_inc(sem("w_done"), 1)

                for b in range(2):
                    solve(4, b, lambda h: invT[:, 0, h, :], lambda h: v_tok[:, 0, h * P:(h + 1) * P])
                for b in range(2):
                    pe.wait_ge(sem("w_ready"), W.next("w_ready"))
                    solve(6, b, lambda h: kkb[:, h, P:T], lambda h: w_sol[:, 0, h * P:(h + 1) * P])
                for b in range(2):
                    pe.wait_ge(sem("w_ready"), W.next("w_ready"))
                    solve(4, b, lambda h: invT[:, 1, h, :], lambda h: v_tok[:, 1, h * P:(h + 1) * P])
                pe.wait_ge(sem("w_ready"), W.next("w_ready", 2))
                outputs(8, lambda t, h: u_sol[:, t, h * P:(h + 1) * P])
                head_sums(4)
                out_product("gdn_w_out", j)
                norm_sum()

            def spread(dst, h, row):
                return mm(dst, ident[0:8, h:h + 1].broadcast_to([8, P]), row, True, True)

            def mlstm(i):
                norm_sum()
                for s in range(4):
                    to_channels("mlstm_w_in", 0, s, bank_of(s), first=s == 0)
                for g in range(2):
                    for k in range(DC):
                        last = mm(ps[0:8, 0, g * T:(g + 1) * T], gw[:, 2, k, 8 * g:8 * g + 8], hT[:, k, :],
                                  k == 0, k == DC - 1)
                last.then_inc(sem("gates_done"), 1)
                pe.wait_ge(sem("evac"), W.next("evac", 4))
                for s in range(4, 8):
                    to_tokens("mlstm_w_in", 0, s, bank_of(s))
                pe.wait_ge(sem("evac"), W.next("evac", 4))
                for s in range(8, 12):
                    to_channels("mlstm_w_in", 0, s, bank_of(s))
                pe.wait_ge(sem("rows_ready"), W.next("rows_ready"))
                for t in range(TT):
                    last = pe.transpose(ps[:, 1, 8 * t:8 * t + 8], rows[0:8, 6, t * P:(t + 1) * P], ident[0:8, 0:8])
                last.then_inc(sem("r_turned"), 1)
                pe.wait_ge(sem("rcol_ready"), W.next("rcol_ready"))
                pe.wait_ge(sem("evac"), W.next("evac", 4))
                for h in range(8):
                    if h >= 2:
                        pe.wait_ge(sem("pair_exp"), W.next("pair_exp"))
                    spread(ps[:, h % 2, 0:T], h, rows[0:8, 7, :]).then_inc(sem("decay_done"), 1)
                pe.wait_ge(sem("pair_exp"), W.next("pair_exp", 2))
                for h in range(8):
                    if h >= 4:
                        pe.wait_ge(sem("score_free"), W.next("score_free"))
                    r0 = 64 * (h % 2)
                    q_, k_ = qk[r0:r0 + 64, h // 2, :], qk[r0:r0 + 64, 4 + h // 2, :]
                    mm(ps[:, 4 + h % 4, 0:T], k_[:, 0:P], q_, True, True)
                    mm(ps[:, 4 + h % 4, T:ED], k_[:, P:T], q_[:, P:T], True, True).then_inc(sem("score_done"), 1)
                pe.wait_ge(sem("score_free"), W.next("score_free", 4))
                outputs(8, lambda t, h: v_tok[:, t, h * P:(h + 1) * P])
                pe.wait_ge(sem("floor_ready"), W.next("floor_ready"))
                for h in range(8):
                    if h >= 2:
                        pe.wait_ge(sem("den_free"), W.next("den_free"))
                    b = 4 + h % 2
                    mm(ps[:, b, 0:T], ones[:, 0:P], pair[:, h, 0:T], True, False)
                    mm(ps[:, b, P:T], ones[:, 0:P], pair[:, h, T:ED], False, True)
                    spread(ps[:, b, T:2 * T], h, rows[0:8, 8, :]).then_inc(sem("den_done"), 1)
                pe.wait_ge(sem("den_free"), W.next("den_free", 2))
                head_sums(4)
                out_product("mlstm_w_out", 0)
                norm_sum()

            def attention(heads, comps, operands, negative, cum, wide):
                for h in range(heads + 1):
                    for c in range(comps if h < heads else 0):
                        n = comps * h + c
                        if n >= 4:
                            pe.wait_ge(sem("score_free"), W.next("score_free"))
                        b = 4 + n % 4
                        q_, k_ = operands(h, c)
                        for c0, t0, width in ((0, 0, P), (P, P, T)):
                            dst = ps[:, b, c0:c0 + width]
                            mm(dst, q_[:, t0:t0 + P], k_[:, 0:width], True, False)
                            if cum is not None:
                                mm(dst, ident[0:8, h:h + 1].broadcast_to([8, P]), cum[:, 0:width], False, False)
                            last = mm(dst[:, width - P:width], ident, negative, False, True)
                        last.then_inc(sem("score_done"), 1)
                    if h == 0:
                        continue
                    hh = h - 1
                    pe.wait_ge(sem("prob_ready"), W.next("prob_ready"))
                    for k in range(3):
                        last = pe.transpose(ps[:, 3, k * P:(k + 1) * P],
                                            prob[:, hh % 2, comps - 1, k * P:(k + 1) * P], ident)
                    last.then_inc(sem("prob_turned"), 1)
                    pe.wait_ge(sem("probT_ready"), W.next("probT_ready"))
                    if wide:
                        o = ps[:, (hh // 2) % 3, (hh % 2) * T:(hh % 2 + 1) * T]
                        v = [v_tok[:, t, P * hh:P * hh + P] for t in range(TT)]
                        if hh == 6:
                            pe.wait_ge(sem("o_moved"), W.next("o_moved"))
                        end = hh % 2 == 1
                    else:
                        c = hh // 2
                        o = ps[64 * (hh % 2):64 * (hh % 2) + 64, 1 + c // 2, (c % 2) * T:(c % 2 + 1) * T]
                        v = [v_tok[:, t, 512 + 64 * hh:576 + 64 * hh] for t in range(TT)]
                        end = hh % 4 == 3
                    mm(o, v[0], probT[:, hh % 2, 0:T], True, False)
                    last = mm(o[:, P:T], v[1], probT[:, hh % 2, T:ED], False, True)
                    if end:
                        last.then_inc(sem("o_ready"), 1)

            def diff(i):
                norm_sum()

                def rotate(g):
                    pe.wait_ge(sem("raw_ready"), W.next("raw_ready"))
                    if g >= 2:
                        pe.wait_ge(sem("roped"), W.next("roped"))
                    mm(ps[:, g % 2, :], cc("rotate"), raw[:, g % 4, :], True, True).then_inc(sem("rotated"), 1)

                for s in range(8):
                    to_channels("diff_w_in", 0, s, bank_of(s), first=s == 0)
                    if s:
                        rotate(s - 1)
                for s in range(8, 12):
                    to_tokens("diff_w_in", 0, s, bank_of(s))
                    if s == 8:
                        rotate(7)
                pe.wait_ge(sem("roped"), W.next("roped", 2))
                pe.wait_ge(sem("evac"), W.next("evac", 4))
                attention(8, 2, lambda h, c: (qk[64 * c:64 * c + 64, h, :], qk[64 * c:64 * c + 64, 8 + h, :]),
                          cc("neg_block"), None, True)
                head_sums(4)
                out_product("diff_w_out", 0)
                norm_sum()

            def hybrid(l):
                norm_sum()
                for s in range(4):
                    to_channels("w_in_2", l, s, bank_of(s), first=s == 0)
                for k in range(DC):
                    last = mm(ps[0:8, 0, 0:T], gw[:, 3 + l, k, 0:8], hT[:, k, :], k == 0, k == DC - 1)
                last.then_inc(sem("gates_done"), 1)
                pe.wait_ge(sem("evac"), W.next("evac", 4))
                for s in range(4, 8):
                    (to_tokens if s < 6 else to_channels)("w_in_2", l, s, bank_of(s))
                pe.wait_ge(sem("evac"), W.next("evac", 4))
                for s in range(8, 12):
                    to_channels("w_in_2", l, s, bank_of(s))
                pe.wait_ge(sem("evac"), W.next("evac", 4))
                for s in range(12, 14):
                    to_tokens("w_in_2", l, s, bank_of(s))
                pe.wait_ge(sem("evac"), W.next("evac", 2))
                m = 0
                for n in range(len(TREE) + 2):
                    if n <= len(TREE):
                        pe.wait_ge(sem("factor_ready"), W.next("factor_ready"))
                    for t in range(1 if n == len(TREE) else TT):
                        if m >= 4:
                            pe.wait_ge(sem("tree_copied"), W.next("tree_copied"))
                        for h in range(4):
                            if n < len(TREE):
                                l_ = r_ = factor[:, n % 2, h, t * P:(t + 1) * P]
                            elif n == len(TREE):
                                l_, r_ = factor[:, n % 2, h, 0:P], factor[:, n % 2, h, P:T]
                            else:
                                l_, r_ = qk[:, 4 + h, t * P:(t + 1) * P], qk[:, h, t * P:(t + 1) * P]
                            last = mm(ps[:, 4 + m % 4, h * P:(h + 1) * P], l_, r_, True, True)
                        last.then_inc(sem("tree_done"), 1)
                        m += 1
                pe.wait_ge(sem("tree_copied"), W.next("tree_copied", 4))
                outputs(4, lambda t, h: v_tok[:, t, h * P:(h + 1) * P])
                head_sums(2)
                pe.wait_ge(sem("mixed"), W.next("mixed", 2))
                pe.wait_ge(sem("rows_ready"), W.next("rows_ready"))
                attention(8, 1, lambda h, c: (qk[64 * (h % 2):64 * (h % 2) + 64, 8 + h // 2, :],
                                              qk[64 * (h % 2):64 * (h % 2) + 64, 12 + h // 2, :]),
                          cc("neg_causal"), rows[0:8, 7, :], False)
                out_product("w_out_2", l)

            def cross(l):
                norm_sum()
                for s in range(4):
                    to_channels("cross_wq_2", l, s, bank_of(s), first=s == 0)
                pe.wait_ge(sem("evac"), W.next("evac", 4))
                pe.wait_ge(sem("mem_split"), W.next("mem_split", 4))
                for s in range(4):
                    to_channels("cross_wk_2", l, s, bank_of(s), src=(memH, memL))
                pe.wait_ge(sem("evac"), W.next("evac", 4))
                for s in range(4):
                    to_tokens("cross_wv_2", l, s, bank_of(s), src=(memH, memL))
                pe.wait_ge(sem("evac"), W.next("evac", 4))
                for h in range(5):
                    if h < 4:
                        for t in range(TT):
                            for c in range(2):
                                last = mm(ps[:, 4 + h, t * T:(t + 1) * T], qk[:, 2 * h + c, t * P:(t + 1) * P],
                                          qk[:, 8 + 2 * h + c, :], c == 0, c == 1)
                        last.then_inc(sem("score_done"), 1)
                    if h >= 1:
                        hh = h - 1
                        pe.wait_ge(sem("prob_ready"), W.next("prob_ready"))
                        for t in range(TT):
                            for m in range(2):
                                last = pe.transpose(ps[:, 4 + hh, (2 * m + t) * P:(2 * m + t + 1) * P],
                                                    prob[:, hh % 2, 0, (2 * t + m) * P:(2 * t + m + 1) * P], ident)
                        last.then_inc(sem("prob_turned"), 1)
                        pe.wait_ge(sem("probT_ready"), W.next("probT_ready"))
                        for c in range(2):
                            for m in range(2):
                                last = mm(ps[:, hh, c * T:(c + 1) * T],
                                          v_tok[:, m, hh * T + c * P:hh * T + (c + 1) * P],
                                          probT[:, hh % 2, m * T:(m + 1) * T], m == 0, m == 1)
                        last.then_inc(sem("o_ready"), 1)
                out_product("cross_wo_2", l)

            def turn_in(rows_, name):
                for b in range(4):
                    for c in range(2):
                        for t in range(TT):
                            last = pe.transpose(ps[:, 4 + b, c * T + t * P:c * T + (t + 1) * P],
                                                rows_[:, t, (2 * b + c) * P:(2 * b + c + 1) * P], ident)
                    last.then_inc(sem(name), 1)

            pe.wait_ge(sem("const_in"), W.next("const_in", 16))
            pe.wait_ge(sem("ones_set"), W.next("ones_set"))
            pe.wait_ge(sem("x_in"), W.next("x_in", 16))
            turn_in(x_rows, "x_turned")
            pe.wait_ge(sem("x_ready"), W.next("x_ready", 4))
            pe.wait_ge(sem("mem_in"), W.next("mem_in", 16))
            turn_in(mem_rows, "mem_turned")
            pe.wait_ge(sem("vec_in"), W.next("vec_in", 16 * (len(VROWS) + 3)))
            pe.transpose(ps[:, 0, 0:P], vec_rows, ident)
            pe.transpose(ps[:, 0, P:NVEC], vec_rows2[0:NVEC - P, :], ident[0:NVEC - P, 0:NVEC - P])
            mm(ps[:, 0, 256:288], ones[0:1, 0:P], brow, True, True).then_inc(sem("vec_turned"), 1)
            pe.wait_ge(sem("lambda_ready"), W.next("lambda_ready"))
            mm(ps[:, 1, 0:1], ones[0:1, 0:P], lwork[:, 130:131], True, True).then_inc(sem("lambda_spread"), 1)
            norm_sum()
            pe.wait_ge(sem("mem_rs"), W.next("mem_rs"))
            pe.wait_ge(sem("params_ready"), W.next("params_ready"))
            pe.wait_ge(sem("gates_in"), W.next("gates_in", 16 * 9))

            for kind, i in parts:
                scope[0] = kind[:3] + "_"
                {"gdn": gdn, "mlstm": mlstm, "diff": diff, "mlp": mlp, "hybrid": hybrid, "cross": cross,
                 "ffn1": lambda l: ffn("ffn1", l), "ffn2": lambda l: ffn("ffn2", l)}[kind](i)
            norm_sum()
            pe.wait_ge(sem("h_ready"), DC * (len(parts) + 1))
            for t in range(TT):
                for c in range(DC):
                    last = pe.transpose(ps[:, 2 * t + c // 4, (c % 4) * P:(c % 4 + 1) * P],
                                        hT[:, c, t * P:(t + 1) * P], ident)
                last.then_inc(sem("out_turned"), 1)

        @block.scalar
        def _(act):
            scope[0] = ""
            W = Waits(act, "act_step")
            f = act.activation

            split_upto = [0]

            def split(upto):
                for n in range(split_upto[0], min(upto, len(slabs))):
                    act.wait_ge(sem(f"slab_in{n % RING}"), landed[n])
                    if n >= PARTS:
                        act.wait_ge(sem("products_done"), slabs[n - PARTS][5])
                    f(wH[:, n % PARTS, :], ring[:, n % RING, :], ACT.Copy).then_inc(sem("high_split"), 1)
                split_upto[0] = max(split_upto[0], upto)

            def ready(name, layer, j, g=0):
                n = slab_no[(name, layer, j)]
                split(n + PARTS)
                act.wait_ge(sem("products_done"), group(name, layer, j, g))
                if g == slabs[n][4] - 1:
                    split(n + PARTS + 1)

            def ln_exp():
                act.preload_act_table_set("natural_log_exp_and_others")

            def rsqrt(src, dst, n, name):
                W.chain(f(dst, src, ACT.Ln, scale=1.0 / n, bias=epsc[:, :]))
                f(dst, dst, ACT.Exp, scale=-0.5).then_inc(sem(name), 1)

            def norm(src, there):
                for c in range(4):
                    there(c)
                    f(sq[:, 2 * c:2 * c + 2, :], src(c), ACT.Square).then_inc(sem("sq_ready"), 1)
                act.wait_ge(sem("ss_ready"), W.next("ss_ready"))
                rsqrt(ps[:, 7, 0:T], rs[:, :], D, "rs_ready")

            def x_norm():
                ln_exp()
                norm(lambda c: xT[:, 2 * c:2 * c + 2, :], lambda c: act.wait_ge(sem("x_ready"), W.next("x_ready")))
                for c in range(4):
                    act.wait_ge(sem("h_ready"), W.next("h_ready", 2))
                    f(hH[:, 2 * c:2 * c + 2, :], hT[:, 2 * c:2 * c + 2, :], ACT.Copy).then_inc(sem("hH_ready"), 1)

            def split_mix(n):
                for c in range(n):
                    act.wait_ge(sem("mixed"), W.next("mixed"))
                    f(hH[:, 2 * c:2 * c + 2, :], hT[:, 2 * c:2 * c + 2, :], ACT.Copy).then_inc(sem("mixH_ready"), 1)

            def post_norm(product):
                norm(lambda c: two(ps[:, c, :]), lambda c: ready(*product(c)))

            def head_norm(n, src, taken=None):
                for b in range(n):
                    if taken:
                        act.wait_ge(sem(taken), W.next(taken))
                    f(sq[:, 2 * b:2 * b + 2, :], src(b), ACT.Square).then_inc(sem("sq_ready"), 1)
                for b in range(n):
                    act.wait_ge(sem("hs_ready"), W.next("hs_ready"))
                    rsqrt(ps[:, 4 + b, :], flat(sq[:, 2 * b:2 * b + 2, :]), P, "hrs_ready")

            def flat(v):
                return v.rearrange("p c t -> p (c t)")

            def channels(name, layer, j, bank0, dst, func=ACT.Copy, scale=1.0):
                for g in range(2):
                    ready(name, layer, 2 * j + g)
                    f(dst(g), two(ps[:, bank0 + g, :]), func, scale=scale).then_inc(sem("evac"), 1)

            def tokens(name, layer, j, bank0, c0):
                for g in range(2):
                    ready(name, layer, 2 * j + g)
                    f(v_tok[:, :, c0 + T * g:c0 + T * (g + 1)], two(ps[:, bank0 + g, :]), ACT.Copy)\
                        .then_inc(sem("evac"), 1)

            def chunks(v, c):
                return lambda g: v[:, c + 2 * g:c + 2 * g + 2, :]

            def out_key(name, layer):
                return lambda c: (name, layer, c)

            def mlp(i):
                x_norm()
                for g in range(16):
                    ready("mlp_w1", i, g)
                    f(act_s[:, g % 2, :], ps[:, 4 + g % 4, :], ACT.Relu).then_inc(sem("act_ready"), 1)
                    if g >= 1:
                        hidden_high(g - 1)
                hidden_high(15)
                post_norm(lambda c: ("mlp_w2", i, 15, c))

            def hidden_high(g):
                act.wait_ge(sem("bank_read"), W.next("bank_read"))
                f(hidH[:, 2 * g:2 * g + 2, :], two(prod_s[:, g % 2, :]), ACT.Copy).then_inc(sem("hiddenH_ready"), 1)

            def ffn(kind, l):
                def hidden_high(n):
                    act.wait_ge(sem("bank_read"), W.next("bank_read"))
                    f(hidH[:, n, :], prod_s[:, n % 2, 0:T], ACT.Copy).then_inc(sem("hiddenH_ready"), 1)

                x_norm()
                for n in range(22):
                    ready(kind, l, n)
                    f(act_s[:, n % 2, 0:T], ps[:, 4 + n % 4, 0:T], ACT.Silu).then_inc(sem("act_ready"), 1)
                    if n >= 1:
                        hidden_high(n - 1)
                hidden_high(21)
                for c in range(4):
                    split(slab_no[(f"{kind}_w_down_2", l, 10)] + PARTS)

            def gdn(i):
                j = i // 3
                x_norm()
                act.wait_ge(sem("tok_raw"), W.next("tok_raw"))
                W.chain(f(tokg[:, 32:48], tokg[:, 16:32], ACT.Abs))
                W.chain(f(tokg[:, 32:48], tokg[:, 32:48], ACT.Exp, scale=-1.0))
                f(tokg[:, 32:48], tokg[:, 32:48], ACT.Ln, bias=1.0)
                f(tokg[:, 64:72], bcast[:, 8 * j:8 * j + 8], ACT.Exp)
                f(tokg[:, 48:64], tokg[:, 48:64], ACT.Exp, scale=-1.0).then_inc(sem("tok_exp"), 1)
                act.wait_ge(sem("pad_set"), W.next("pad_set"))

                def silu(g):
                    act.wait_ge(sem("conv_done"), W.next("conv_done"))
                    if g < 8:
                        dst = qk[:, 2 * g:2 * g + 2, :]
                    else:
                        if g >= 10:
                            move(g - 10)
                        dst = vch[:, g % 2, :, :]
                    f(dst, conv[:, g % 2, :, :], ACT.Silu).then_inc(sem("silu_done"), 1)

                def move(g):
                    act.wait_ge(sem("v_turned"), W.next("v_turned"))
                    f(v_tok[:, :, T * g:T * (g + 1)], ps[:, 2, :].rearrange("p (i n) -> p i n", i=TT),
                      ACT.Copy).then_inc(sem("v_done"), 1)

                for g in range(16):
                    ready("gdn_w_in", j, g)
                    if 2 <= g < 12:
                        silu(g - 2)
                    if g < 12:
                        f(pre[:, g % 2, :, 3:3 + T], two(ps[:, 4 + g % 4, :]), ACT.Copy).then_inc(sem("evac"), 1)
                    else:
                        c = 2 * (g - 12)
                        f(gate[:, c:c + 2, :], two(ps[:, 4 + g % 4, :]), ACT.Silu).then_inc(sem("evac"), 1)
                        if g == 13:
                            silu(10)
                            silu(11)
                move(2)
                move(3)
                ln_exp()
                for h in range(8):
                    act.wait_ge(sem("decay_done"), W.next("decay_done"))
                    f(pair[:, h, :], ps[:, 4 + h % 2, 0:ED], ACT.Exp).then_inc(sem("pair_exp"), 1)
                for half in range(2):
                    for b in range(4):
                        if half:
                            act.wait_ge(sem("qk_normed"), W.next("qk_normed"))
                        c = 8 * half + 2 * b
                        f(sq[:, 2 * b:2 * b + 2, :], qk[:, c:c + 2, :], ACT.Square).then_inc(sem("sq_ready"), 1)
                    for b in range(4):
                        act.wait_ge(sem("hs_ready"), W.next("hs_ready"))
                        v = flat(sq[:, 2 * b:2 * b + 2, :])
                        f(v, ps[:, b, :], ACT.Ln, bias=epsc[:, :]).then_inc(sem("hs_free"), 1)
                        act.wait_ge(sem("hs_free"), W.next("hs_free"))
                        f(v, v, ACT.Exp, scale=-0.5).then_inc(sem("hrs_ready"), 1)
                act.wait_ge(sem("qk_normed"), W.next("qk_normed", 4))
                head_norm(4, lambda b: two(ps[:, b, :]), "o_ready")
                split_mix(4)
                post_norm(out_key("gdn_w_out", j))

            def mlstm(i):
                x_norm()
                channels("mlstm_w_in", 0, 0, 4, chunks(qk, 0), scale=0.125)
                channels("mlstm_w_in", 0, 1, 6, chunks(qk, 4))
                act.wait_ge(sem("gates_done"), W.next("gates_done"))
                f(rows[0:8, 0, :], ps[0:8, 0, 0:T], ACT.Tanh, scale=1.0 / 15.0, bias=gb15[:, 0:1])
                W.chain(f(rows[0:8, 1, :], ps[0:8, 0, T:2 * T], ACT.Tanh, scale=1.0 / 15.0, bias=gb15[:, 1:2]))
                ln_exp()
                W.chain(f(rows[0:8, 2, :], rows[0:8, 1, :], ACT.Exp, scale=-15.0))
                f(rows[0:8, 3, :], rows[0:8, 2, :], ACT.Ln, bias=1.0).then_inc(sem("log_ready"), 1)
                tokens("mlstm_w_in", 0, 2, 4, 0)
                tokens("mlstm_w_in", 0, 3, 6, 512)
                channels("mlstm_w_in", 0, 4, 4, chunks(gate, 0), func=ACT.Sigmoid)
                channels("mlstm_w_in", 0, 5, 6, chunks(gate, 4), func=ACT.Sigmoid)
                ln_exp()
                act.wait_ge(sem("rows_ready"), W.next("rows_ready"))
                f(rows[0:8, 8, :], rows[0:8, 9, :], ACT.Exp, scale=-1.0).then_inc(sem("floor_ready"), 1)
                act.wait_ge(sem("rcol_ready"), W.next("rcol_ready"))
                for h in range(8):
                    act.wait_ge(sem("decay_done"), W.next("decay_done"))
                    f(pair[:, h, 0:T], ps[:, h % 2, 0:T], ACT.Exp, bias=rcol[:, 0, h:h + 1])
                    f(pair[:, h, T:ED], ps[:, h % 2, P:T], ACT.Exp, bias=rcol[:, 1, h:h + 1])\
                        .then_inc(sem("pair_exp"), 1)
                for h in range(8):
                    act.wait_ge(sem("den_done"), W.next("den_done"))
                    if h >= 2:
                        act.wait_ge(sem("cell_ready"), W.next("cell_ready"))
                    e = em_s[:, h % 2, 0:T]
                    f(em_s[:, h % 2, T:2 * T], ps[:, 4 + h % 2, T:2 * T], ACT.Copy)
                    f(e, ps[:, 4 + h % 2, 0:T], ACT.Abs).then_inc(sem("em_ready"), 1)
                    act.wait_ge(sem("den_free"), W.next("den_free"))
                    W.chain(f(e, e, ACT.Ln))
                    f(e, e, ACT.Exp, scale=-1.0).then_inc(sem("rden_ready"), 1)
                act.wait_ge(sem("cell_ready"), W.next("cell_ready", 2))
                head_norm(4, lambda b: num_s[:, 2 * b:2 * b + 2, :])
                split_mix(4)
                post_norm(out_key("mlstm_w_out", 0))

            def softmaxes(heads, comps, wide):
                def turned(h):
                    act.wait_ge(sem("prob_turned"), W.next("prob_turned"))
                    f(probT[:, h % 2, 0:ED], ps[:, 3, 0:ED], ACT.Copy).then_inc(sem("probT_ready"), 1)
                    if wide and h % 2:
                        act.wait_ge(sem("o_ready"), W.next("o_ready"))
                        b = h // 2
                        f(num_s[:, 2 * b:2 * b + 2, :], two(ps[:, b % 3, :]), ACT.Copy).then_inc(sem("o_moved"), 1)

                for h in range(heads):
                    for c in range(comps):
                        act.wait_ge(sem("max_ready"), W.next("max_ready"))
                        b = 4 + (comps * h + c) % 4
                        s = stat[:, h % 2, c, :]
                        f(prob[:, h % 2, c, 0:P], ps[:, b, 0:P], ACT.Exp, bias=s[:, 0:1], accum_out=s[:, 2:3])
                        f(prob[:, h % 2, c, P:ED], ps[:, b, P:ED], ACT.Exp, bias=s[:, 1:2], accum_out=s[:, 3:4])\
                            .then_inc(sem("score_free"), 1)
                    if h >= 1:
                        turned(h - 1)
                turned(heads - 1)

            def diff(i):
                x_norm()
                for g in range(8):
                    ready("diff_w_in", 0, g)
                    if g >= 4:
                        act.wait_ge(sem("roped"), W.next("roped"))
                    f(raw[:, g % 4, :], ps[:, 4 + g % 4, :], ACT.Copy, scale=0.125 if g < 4 else 1.0)\
                        .then_inc(sem("raw_ready"), 1)
                tokens("diff_w_in", 0, 4, 4, 0)
                tokens("diff_w_in", 0, 5, 6, 512)
                softmaxes(8, 2, True)
                act.wait_ge(sem("o_moved"), W.next("o_moved", 4))
                head_norm(4, lambda b: num_s[:, 2 * b:2 * b + 2, :])
                split_mix(4)
                post_norm(out_key("diff_w_out", 0))

            def hybrid(l):
                x_norm()
                channels("w_in_2", l, 0, 4, chunks(qk, 0), func=ACT.Silu)
                channels("w_in_2", l, 1, 6, chunks(zcum, 0))
                tokens("w_in_2", l, 2, 4, 0)
                channels("w_in_2", l, 3, 6, chunks(gate, 0), func=ACT.Silu)
                channels("w_in_2", l, 4, 4, chunks(qk, 8), scale=0.125)
                channels("w_in_2", l, 5, 6, chunks(qk, 12))
                f(qk[:, 4:8, :], zcum, ACT.Sigmoid, scale=-1.0).then_inc(sem("hk_ready"), 1)
                tokens("w_in_2", l, 6, 4, 512)
                ln_exp()
                W.chain(f(glog, zcum, ACT.Abs))
                W.chain(f(glog, glog, ACT.Exp, scale=-1.0))
                f(glog, glog, ACT.Ln, bias=1.0).then_inc(sem("glog_ready"), 1)
                act.wait_ge(sem("fz_ready"), W.next("fz_ready"))
                W.chain(f(rows[0:8, 2, :], rows[0:8, 1, :], ACT.Abs))
                W.chain(f(rows[0:8, 2, :], rows[0:8, 2, :], ACT.Exp, scale=-1.0))
                f(rows[0:8, 3, :], rows[0:8, 2, :], ACT.Ln, bias=1.0).then_inc(sem("log_ready"), 1)
                if l:
                    act.wait_ge(sem("lse_ready"), W.next("lse_ready"))
                    v = factor[:, 0, :, :]
                    W.chain(f(v, v, ACT.Abs))
                    W.chain(f(v, v, ACT.Exp, scale=-1.0))
                    f(v, v, ACT.Ln, bias=1.0).then_inc(sem("lse_done"), 1)
                for n in range(len(TREE) + 1):
                    act.wait_ge(sem("edge_ready"), W.next("edge_ready"))
                    f(factor[:, n % 2, :, :], factor[:, n % 2, :, :], ACT.Exp).then_inc(sem("factor_exp"), 1)
                head_norm(2, lambda b: two(ps[:, b, :]), "o_ready")
                split_mix(2)
                softmaxes(8, 1, False)
                for b in range(2):
                    act.wait_ge(sem("o_ready"), W.next("o_ready"))
                    f(hH[:, 4 + 2 * b:6 + 2 * b, :], two(ps[:, 1 + b, :]), ACT.Copy).then_inc(sem("mixH_ready"), 1)
                split(slab_no[("w_out_2", l, 3)] + PARTS)

            def cross(l):
                for c in range(4):
                    act.wait_ge(sem("mem_normed"), W.next("mem_normed", 2))
                    f(memH[:, 2 * c:2 * c + 2, :], mem_n[:, 2 * c:2 * c + 2, :], ACT.Copy)\
                        .then_inc(sem("memH_ready"), 1)
                x_norm()
                channels("cross_wq_2", l, 0, 4, chunks(qk, 0), scale=0.0625)
                channels("cross_wq_2", l, 1, 6, chunks(qk, 4), scale=0.0625)
                channels("cross_wk_2", l, 0, 4, chunks(qk, 8))
                channels("cross_wk_2", l, 1, 6, chunks(qk, 12))
                tokens("cross_wv_2", l, 0, 4, 0)
                tokens("cross_wv_2", l, 1, 6, 512)

                def tail(h):
                    act.wait_ge(sem("prob_turned"), W.next("prob_turned"))
                    f(probT[:, h % 2, :], ps[:, 4 + h, :], ACT.Copy).then_inc(sem("probT_ready"), 1)
                    act.wait_ge(sem("o_ready"), W.next("o_ready"))
                    f(hH[:, 2 * h:2 * h + 2, :], two(ps[:, h, :]), ACT.Copy).then_inc(sem("mixH_ready"), 1)

                for h in range(4):
                    act.wait_ge(sem("max_ready"), W.next("max_ready"))
                    for t in range(TT):
                        last = f(prob[:, h % 2, 0, t * T:(t + 1) * T], ps[:, 4 + h, t * T:(t + 1) * T], ACT.Exp,
                                 bias=stat[:, h % 2, 0, t:t + 1], accum_out=stat[:, h % 2, 0, 2 + t:3 + t])
                    last.then_inc(sem("score_free"), 1)
                    if h >= 1:
                        tail(h - 1)
                tail(3)
                split(slab_no[("cross_wo_2", l, 3)] + PARTS)

            ln_exp()
            act.wait_ge(sem("ones_set"), W.next("ones_set"))
            act.wait_ge(sem("lambda_sums"), W.next("lambda_sums"))
            f(lwork[:, 130:132], lwork[:, 128:130], ACT.Exp).then_inc(sem("lambda_exp"), 1)
            act.wait_ge(sem("lb_diff"), W.next("lb_diff"))
            W.chain(f(lb[:, 4:8], lb[:, 0:4], ACT.Abs))
            W.chain(f(lb[:, 4:8], lb[:, 4:8], ACT.Exp, scale=-1.0))
            f(lb[:, 8:12], lb[:, 4:8], ACT.Ln, bias=1.0).then_inc(sem("lb_log"), 1)
            act.wait_ge(sem("lb_ready"), W.next("lb_ready"))
            f(lb[:, 24:28], lb[:, 16:20], ACT.Exp).then_inc(sem("lb_prob"), 1)
            act.wait_ge(sem("mem_ready"), W.next("mem_ready", 4))
            for c in range(4):
                f(sq[:, 2 * c:2 * c + 2, :], memT[:, 2 * c:2 * c + 2, :], ACT.Square).then_inc(sem("sq_ready"), 1)
            act.wait_ge(sem("ss_ready"), W.next("ss_ready"))
            rsqrt(ps[:, 7, 0:T], rs_mem[:, :], D, "mem_rs")
            for kind, i in parts:
                scope[0] = kind[:3] + "_"
                {"gdn": gdn, "mlstm": mlstm, "diff": diff, "mlp": mlp, "hybrid": hybrid, "cross": cross,
                 "ffn1": lambda l: ffn("ffn1", l), "ffn2": lambda l: ffn("ffn2", l)}[kind](i)
            norm(lambda c: xT[:, 2 * c:2 * c + 2, :], lambda c: act.wait_ge(sem("x_ready"), W.next("x_ready")))
            for t in range(TT):
                act.wait_ge(sem("out_turned"), W.next("out_turned"))
                f(out_rows[:, t, :], ps[:, 2 * t:2 * t + 2, :].rearrange("p b n -> p (b n)"), ACT.Copy)\
                    .then_inc(sem("out_tile"), 1)

        @block.vector
        def _(dve):
            scope[0] = ""
            W = Waits(dve, "dve_step")
            tt, ts, stt = dve.tensor_tensor, dve.tensor_scalar, dve.scalar_tensor_tensor

            split_upto = [0]

            def split(upto):
                for n in range(split_upto[0], min(upto, len(slabs))):
                    dve.wait_ge(sem("high_split"), n + 1)
                    tt(wL[:, n % PARTS, :], ring[:, n % RING, :], wH[:, n % PARTS, :].bitcast(F32), ALU.subtract)\
                        .then_inc(sem("low_split"), 1)
                split_upto[0] = max(split_upto[0], upto)

            def refill(name, layer, j):
                split(slab_no[(name, layer, j)] + PARTS + 1)

            def x_norm(gain, k0, last=False):
                dve.wait_ge(sem("rs_ready"), W.next("rs_ready"))
                for c in range(DC):
                    stt(hT[:, c, :], xT[:, c, :], column(gain, k0 + c), rs[:, :], ALU.mult, ALU.mult)\
                        .then_inc(sem("h_ready"), 1)
                for c in range(0 if last else 4):
                    dve.wait_ge(sem("hH_ready"), W.next("hH_ready"))
                    v = slice(2 * c, 2 * c + 2)
                    tt(hL[:, v, :], hT[:, v, :], hH[:, v, :].bitcast(F32), ALU.subtract).then_inc(sem("hL_ready"), 1)

            def split_mix(n):
                for c in range(n):
                    dve.wait_ge(sem("mixH_ready"), W.next("mixH_ready"))
                    v = slice(2 * c, 2 * c + 2)
                    tt(hL[:, v, :], hT[:, v, :], hH[:, v, :].bitcast(F32), ALU.subtract)\
                        .then_inc(sem("mixL_ready"), 1)

            def split_bank(c, bank):
                dve.wait_ge(sem("mixH_ready"), W.next("mixH_ready"))
                v = slice(c, c + 2)
                tt(hL[:, v, :], two(ps[:, bank, :]), hH[:, v, :].bitcast(F32), ALU.subtract)\
                    .then_inc(sem("mixL_ready"), 1)

            def post_norm(k0):
                dve.wait_ge(sem("rs_ready"), W.next("rs_ready"))
                for c in range(4):
                    for k in (2 * c, 2 * c + 1):
                        ins = stt(sq[:, k, :], ps[:, c, (k % 2) * T:(k % 2 + 1) * T], column("norm_g", k0 + k),
                                  rs[:, :], ALU.mult, ALU.mult)
                    W.chain(ins)
                    tt(xT[:, 2 * c:2 * c + 2, :], xT[:, 2 * c:2 * c + 2, :], sq[:, 2 * c:2 * c + 2, :], ALU.add)\
                        .then_inc(sem("x_ready"), 1)

            def residual(scale, product):
                for c in range(4):
                    dve.wait_ge(sem("products_done"), group(*product(c)))
                    x = xT[:, 2 * c:2 * c + 2, :]
                    stt(x, two(ps[:, c, :]), scale, x, ALU.mult, ALU.add).then_inc(sem("x_ready"), 1)

            def mlp(i):
                x_norm("norm_g", (4 * i + 2) * DC)
                def hidden_low(g):
                    dve.wait_ge(sem("hiddenH_ready"), W.next("hiddenH_ready"))
                    v = slice(2 * g, 2 * g + 2)
                    tt(hidL[:, v, :], two(prod_s[:, g % 2, :]), hidH[:, v, :].bitcast(F32), ALU.subtract)\
                        .then_inc(sem("hidden_ready"), 1)

                for g in range(16):
                    refill("mlp_w1", i, g)
                    if g >= 2:
                        dve.wait_ge(sem("hidden_ready"), W.next("hidden_ready"))
                    dve.wait_ge(sem("act_ready"), W.next("act_ready"))
                    tt(prod_s[:, g % 2, :], act_s[:, g % 2, :], ps[:, 4 + g % 4, :], ALU.mult)\
                        .then_inc(sem("bank_read"), 1)
                    if g >= 1:
                        hidden_low(g - 1)
                hidden_low(15)
                W.next("hidden_ready", 2)
                refill("mlp_w2", i, 15)
                post_norm((4 * i + 3) * DC)

            def ffn(kind, l):
                x_norm(f"{kind}_norm_2", l * DC)
                def hidden_low(n):
                    dve.wait_ge(sem("hiddenH_ready"), W.next("hiddenH_ready"))
                    tt(hidL[:, n, :], prod_s[:, n % 2, 0:T], hidH[:, n, :].bitcast(F32), ALU.subtract)\
                        .then_inc(sem("hidden_ready"), 1)

                for n in range(22):
                    refill(kind, l, n)
                    if n >= 2:
                        dve.wait_ge(sem("hidden_ready"), W.next("hidden_ready"))
                    dve.wait_ge(sem("act_ready"), W.next("act_ready"))
                    tt(prod_s[:, n % 2, 0:T], act_s[:, n % 2, 0:T], ps[:, 4 + n % 4, T:2 * T], ALU.mult)\
                        .then_inc(sem("bank_read"), 1)
                    if n >= 1:
                        hidden_low(n - 1)
                hidden_low(21)
                W.next("hidden_ready", 2)
                refill(f"{kind}_w_down_2", l, 9)
                residual(0.5, lambda c: (f"{kind}_w_down_2", l, 10, c))

            def head_out(n, src, gain, gated):
                for b in range(n):
                    dve.wait_ge(sem("hrs_ready"), W.next("hrs_ready"))
                    for k in (2 * b, 2 * b + 1):
                        s, r = src(k), sq[:, k, :]
                        ins = stt(r if gated else hT[:, k, :], s, gain(k), r, ALU.mult, ALU.mult)
                    if gated:
                        W.chain(ins)
                        ins = tt(hT[:, 2 * b:2 * b + 2, :], sq[:, 2 * b:2 * b + 2, :], gate[:, 2 * b:2 * b + 2, :],
                                 ALU.mult)
                    ins.then_inc(sem("mixed"), 1)
                split_mix(n)

            def in_bank(k):
                return ps[:, k // 2, (k % 2) * T:(k % 2 + 1) * T]

            def gdn(i):
                j, no = i // 3, gdn_no[i]
                dve.wait_ge(sem("conv_turned"), W.next("conv_turned"))
                W.chain(dve.tensor_copy(convw, ps[:, 3, 0:96]))
                x_norm("norm_g", 4 * i * DC)
                dve.wait_ge(sem("gates_done"), W.next("gates_done"))
                ab = ps[:, 3, 128:160].rearrange("p (t n) -> p t n", t=TT)

                def th(a):
                    return tokg[:, a:a + 16].rearrange("p (t h) -> p t h", t=TT)

                tt(th(16), ab[:, :, 0:8], bcast[:, 16 + 8 * j:24 + 8 * j][:, None, :].broadcast_to([P, TT, 8]), ALU.add)
                dve.tensor_copy(th(48), ab[:, :, 8:16]).then_inc(sem("tok_raw"), 1)
                dve.wait_ge(sem("tok_exp"), W.next("tok_exp"))
                W.chain(stt(tokg[:, 16:32], tokg[:, 16:32], 0.0, tokg[:, 32:48], ALU.max, ALU.add))
                stt(th(0), th(16), -1.0, tokg[:, 64:72][:, None, :].broadcast_to([P, TT, 8]), ALU.mult, ALU.mult)
                W.chain(ts(tokg[:, 48:64], tokg[:, 48:64], 1.0, None, ALU.add))
                dve.reciprocal(tokg[:, 80:96], tokg[:, 48:64]).then_inc(sem("tok_gates"), 1)
                for g in range(12):
                    refill("gdn_w_in", j, g)
                    dve.wait_ge(sem("evac"), W.next("evac"))
                    if g >= 2:
                        dve.wait_ge(sem("silu_done"), W.next("silu_done"))
                    b = g % 2
                    done = [0, 0]
                    for k in (3, 2, 1, 0):
                        for c in range(2):
                            w = convw[:, k * 24 + 2 * g + c:k * 24 + 2 * g + c + 1]
                            src, dst = pre[:, b, c, k:k + T], conv[:, b, c, :]
                            if k == 3:
                                done[c] = W.mark(ts(dst, src, w, None, ALU.mult))
                            else:
                                dve.wait_ge(sem("dve_step"), done[c])
                                ins = stt(dst, src, w, dst, ALU.mult, ALU.add)
                                if k or not c:
                                    done[c] = W.mark(ins)
                    ins.then_inc(sem("conv_done"), 1)
                refill("gdn_w_in", j, 15)
                dve.wait_ge(sem("silu_done"), W.next("silu_done", 2))
                dve.wait_ge(sem("evac"), W.next("evac", 4))
                for b in range(8):
                    dve.wait_ge(sem("hrs_ready"), W.next("hrs_ready"))
                    c = 2 * b
                    v = qk[:, c:c + 2, :]
                    tt(v, v, sq[:, c % 8:c % 8 + 2, :], ALU.mult).then_inc(sem("qk_normed"), 1)
                for h in range(8):
                    dve.wait_ge(sem("score_done"), W.next("score_done"))
                    dve.wait_ge(sem("pair_masked"), W.next("pair_masked"))
                    for t, (a, e) in enumerate(((0, T), (T, ED))):
                        ins = stt(kkb[:, h, a:e], ps[:, h % 4, a:e], tokg[:, 80 + 8 * t + h:81 + 8 * t + h],
                                  pair[:, h, a:e], ALU.mult, ALU.mult)
                    ins.then_inc(sem("score_free"), 1)
                for h in range(8):
                    dve.wait_ge(sem("score_done"), W.next("score_done"))
                    stt(pair[:, h, :], ps[:, h % 4, 0:ED], P ** -0.5, pair[:, h, :], ALU.mult, ALU.mult)\
                        .then_inc(sem("score_free"), 1)
                for n in range(len(TREE)):
                    m = cc("tree_ts", n)[:, None, :].broadcast_to([P, 4, P])
                    for q in range(4):
                        t, h0 = q // 2, 4 * (q % 2)
                        dve.wait_ge(sem("level_done"), W.next("level_done"))
                        tt(level[:, t, h0:h0 + 4, :], ps[:, 4 + q, :].rearrange("p (h n) -> p h n", h=4), m, ALU.mult)\
                            .then_inc(sem("level_masked"), 1)
                    for q in range(4):
                        t, h0 = q // 2, 4 * (q % 2)
                        dve.wait_ge(sem("delta_done"), W.next("delta_done"))
                        for bank, x in ((2 * (q % 2), inv), (2 * (q % 2) + 1, invT)):
                            if x is inv and n == len(TREE) - 1:
                                continue
                            v = x[:, t, h0:h0 + 4, :]
                            ins = tt(v, v, ps[:, bank, :].rearrange("p (h n) -> p h n", h=4), ALU.subtract)
                        ins.then_inc(sem("inverse_done"), 1)

                def times_beta(t, b, bank):
                    return tt(u_sol[:, t, 512 * b:512 * (b + 1)].rearrange("p (h n) -> p h n", h=4),
                              ps[:, bank, :].rearrange("p (h n) -> p h n", h=4),
                              tokg[:, 80 + 8 * t + 4 * b:84 + 8 * t + 4 * b][:, :, None].broadcast_to([P, 4, P]),
                              ALU.mult)

                for b in range(2):
                    dve.wait_ge(sem("w_done"), W.next("w_done"))
                    dve.tensor_copy(w_sol[:, 0, 512 * b:512 * (b + 1)], ps[:, 4 + b, :]).then_inc(sem("w_ready"), 1)
                    times_beta(0, b, 4 + b)
                for b in range(2):
                    dve.wait_ge(sem("w_done"), W.next("w_done"))
                    v = v_tok[:, 1, 512 * b:512 * (b + 1)]
                    tt(v, v, ps[:, 6 + b, :], ALU.subtract).then_inc(sem("w_ready"), 1)
                for b in range(2):
                    dve.wait_ge(sem("w_done"), W.next("w_done"))
                    times_beta(1, b, 4 + b).then_inc(sem("w_ready"), 1)
                head_out(4, in_bank, lambda k: column("gdn_norm_g", j), True)
                refill("gdn_w_out", j, 3)
                post_norm((4 * i + 1) * DC)

            def mlstm(i):
                x_norm("norm_g", 4 * i * DC)
                r = lambda k: rows[0:8, k, :]
                one = ones[0:8, :]
                refill("mlstm_w_in", 0, 3)
                dve.wait_ge(sem("log_ready"), W.next("log_ready"))
                W.chain(dve.tensor_tensor_scan(r(4), one, r(3), 0.0, ALU.mult, ALU.subtract))
                W.chain(stt(r(6), r(0), 15.0, r(4), ALU.mult, ALU.subtract))
                W.chain(dve.tensor_tensor_scan(r(5), one, r(6), 0.0, ALU.mult, ALU.max))
                ts(r(7), r(5), -1.0, None, ALU.mult)
                tt(r(9), r(4), r(5), ALU.add).then_inc(sem("rows_ready"), 1)
                refill("mlstm_w_in", 0, 11)
                dve.wait_ge(sem("r_turned"), W.next("r_turned"))
                dve.tensor_copy(rcol.rearrange("p i h -> p (i h)"), ps[:, 1, 0:16]).then_inc(sem("rcol_ready"), 1)
                for h in range(8):
                    dve.wait_ge(sem("score_done"), W.next("score_done"))
                    dve.wait_ge(sem("pair_masked"), W.next("pair_masked"))
                    tt(pair[:, h, :], ps[:, 4 + h % 4, 0:ED], pair[:, h, :], ALU.mult).then_inc(sem("score_free"), 1)
                for h in range(8):
                    dve.wait_ge(sem("em_ready"), W.next("em_ready"))
                    e = em_s[:, h % 2, 0:T]
                    tt(e, e, em_s[:, h % 2, T:2 * T], ALU.max).then_inc(sem("den_free"), 1)
                    dve.wait_ge(sem("rden_ready"), W.next("rden_ready"))
                    tt(num_s[:, h, :], in_bank(h), e, ALU.mult).then_inc(sem("cell_ready"), 1)
                head_out(4, lambda k: num_s[:, k, :], lambda k: column("mlstm_norm_g", k), True)
                refill("mlstm_w_out", 0, 3)
                post_norm((4 * i + 1) * DC)

            def softmaxes(heads, comps):
                def normalize(h):
                    dve.wait_ge(sem("score_free"), W.next("score_free", comps))
                    s = stat[:, h % 2, :, :]
                    W.chain(dve.reciprocal(s[:, 0:comps, 2:4], s[:, 0:comps, 2:4]))
                    if comps == 2:
                        W.chain(ts(s[:, 1, 2:4], s[:, 1, 2:4], bcast[:, 33:34], None, ALU.mult))
                    for k, (a, e) in enumerate(((0, P), (P, ED))):
                        p = prob[:, h % 2, 0, a:e]
                        ins = ts(p, p, s[:, 0, 2 + k:3 + k], None, ALU.mult)
                    if comps == 2:
                        W.chain(ins)
                        for k, (a, e) in enumerate(((0, P), (P, ED))):
                            p = prob[:, h % 2, 1, a:e]
                            ins = stt(p, p, s[:, 1, 2 + k:3 + k], prob[:, h % 2, 0, a:e], ALU.mult, ALU.add)
                    ins.then_inc(sem("prob_ready"), 1)

                for h in range(heads):
                    for c in range(comps):
                        dve.wait_ge(sem("score_done"), W.next("score_done"))
                        b = 4 + (comps * h + c) % 4
                        for k, (a, e) in enumerate(((0, P), (P, ED))):
                            ins = dve.tensor_reduce(stat[:, h % 2, c, k:k + 1], ps[:, b, a:e], AX, ALU.max,
                                                    negate=True)
                        ins.then_inc(sem("max_ready"), 1)
                    if h >= 1:
                        normalize(h - 1)
                normalize(heads - 1)

            def diff(i):
                x_norm("norm_g", 4 * i * DC)
                both = lambda name: cc(name)[:, None, :].broadcast_to([P, 2, T])
                for g in range(8):
                    refill("diff_w_in", 0, g)
                    dve.wait_ge(sem("rotated"), W.next("rotated"))
                    v, s = qk[:, 2 * g:2 * g + 2, :], two(probT[:, g % 2, :])
                    tt(v, two(raw[:, g % 4, :]), both("cos"), ALU.mult)
                    W.chain(tt(s, two(ps[:, g % 2, :]), both("sin"), ALU.mult))
                    tt(v, v, s, ALU.add).then_inc(sem("roped"), 1)
                refill("diff_w_in", 0, 11)
                softmaxes(8, 2)
                head_out(4, lambda k: num_s[:, k, :], lambda k: bcast[:, 34:35], False)
                refill("diff_w_out", 0, 3)
                post_norm((4 * i + 1) * DC)

            def hybrid(l):
                x_norm("mix_norm_2", l * DC)
                dve.memset(pair[:, 0:4, :], 0.0)
                r = lambda k: rows[0:8, k, :]
                refill("w_in_2", l, 3)
                dve.wait_ge(sem("gates_done"), W.next("gates_done"))
                ts(r(1), ps[0:8, 0, 0:T], gbias[:, 2 + l:3 + l], None, ALU.add).then_inc(sem("fz_ready"), 1)
                refill("w_in_2", l, 13)
                dve.wait_ge(sem("hk_ready"), W.next("hk_ready"))
                if l:
                    for h in range(4):
                        ts(qk[:, 4 + h, :], qk[:, 4 + h, :], lb[:, 24 + h:25 + h], None, ALU.mult)
                dve.wait_ge(sem("glog_ready"), W.next("glog_ready"))
                W.chain(stt(glog, zcum, 0.0, glog, ALU.min, ALU.subtract))
                dve.wait_ge(sem("log_ready"), W.next("log_ready"))
                W.chain(stt(r(4), r(1), 0.0, r(3), ALU.min, ALU.subtract))
                W.chain(dve.tensor_tensor_scan(r(5), ones[0:8, :], r(4), 0.0, ALU.mult, ALU.add))
                ts(r(7), r(5), -1.0, None, ALU.mult).then_inc(sem("rows_ready"), 1)
                if l:
                    for h in range(4):
                        ins = ts(glog[:, h, :], glog[:, h, :], lb[:, 16 + h:17 + h], None, ALU.add)
                    W.chain(ins)
                    for h in range(4):
                        ins = ts(factor[:, 0, h, :], glog[:, h, :], lb[:, 12 + h:13 + h], None, ALU.subtract)
                    ins.then_inc(sem("lse_ready"), 1)
                    dve.wait_ge(sem("lse_done"), W.next("lse_done"))
                    for h in range(4):
                        ins = stt(glog[:, h, :], glog[:, h, :], lb[:, 12 + h:13 + h], factor[:, 0, h, :],
                                  ALU.max, ALU.add)
                    W.chain(ins)
                for h in range(4):
                    ins = dve.tensor_tensor_scan(zcum[:, h, :], ones[:, :], glog[:, h, :], 0.0, ALU.mult, ALU.add)
                W.chain(ins)

                def split(v, m):
                    v = v.rearrange("p h t -> p (h t)").rearrange("p (b n) -> p b n", n=2 * m)
                    return v[:, :, 0:m], v[:, :, m:2 * m], v[:, :, m - 1:m].broadcast_to([P, 4 * T // (2 * m), m])

                spans = TREE + [P]

                def edges(n):
                    gl, gr, edge = split(zcum, spans[n])
                    fl, fr, _ = split(factor[:, n % 2, :, :], spans[n])
                    tt(fl, edge, gl, ALU.subtract)
                    tt(fr, gr, edge, ALU.subtract).then_inc(sem("edge_ready"), 1)

                def apply(n):
                    dve.wait_ge(sem("factor_exp"), W.next("factor_exp"))
                    fl, fr, _ = split(factor[:, n % 2, :, :], spans[n])
                    kl, _, _ = split(qk[:, 4:8, :], spans[n])
                    _, qr, _ = split(qk[:, 0:4, :], spans[n])
                    tt(fl, fl, kl, ALU.mult)
                    tt(fr, fr, qr, ALU.mult).then_inc(sem("factor_ready"), 1)

                def copy_level(n):
                    for t in range(1 if n == len(TREE) else TT):
                        dve.wait_ge(sem("tree_done"), W.next("tree_done"))
                        if tree_m[0] >= 2:
                            dve.wait_ge(sem("tree_copied"), W.next("tree_copied"))
                        data = ps[:, 4 + tree_m[0] % 4, :].rearrange("p (h n) -> p h n", h=4)
                        tree_m[0] += 1
                        if n == len(TREE):
                            dve.tensor_copy(pair[:, 0:4, P:T], data).then_inc(sem("tree_copied"), 1)
                            continue
                        m = ident if n > len(TREE) else cc("tree_st", n)
                        dst = pair[:, 0:4, 0:P] if t == 0 else pair[:, 0:4, T:ED]
                        dve.copy_predicated(dst, m.bitcast(I32)[:, None, :].broadcast_to([P, 4, P]), data)\
                            .then_inc(sem("tree_copied"), 1)

                tree_m = [0]
                edges(0)
                edges(1)
                apply(0)
                for n in range(len(TREE) + 1):
                    if n + 1 <= len(TREE):
                        apply(n + 1)
                    copy_level(n)
                    if n + 2 <= len(TREE):
                        edges(n + 2)
                copy_level(len(TREE) + 1)
                dve.wait_ge(sem("tree_copied"), W.next("tree_copied", 2))
                head_out(2, in_bank, lambda k: column("hgrn_out_norm_2", l), True)
                softmaxes(8, 1)
                for b in range(2):
                    split_bank(4 + 2 * b, 1 + b)
                refill("w_out_2", l, 2)
                residual(1.0, lambda c: ("w_out_2", l, c))

            def cross(l):
                for c in range(DC):
                    stt(mem_n[:, c, :], memT[:, c, :], column("mem_norm_2", l * DC + c), rs_mem[:, :],
                        ALU.mult, ALU.mult).then_inc(sem("mem_normed"), 1)
                for c in range(4):
                    dve.wait_ge(sem("memH_ready"), W.next("memH_ready"))
                    v = slice(2 * c, 2 * c + 2)
                    tt(memL[:, v, :], mem_n[:, v, :], memH[:, v, :].bitcast(F32), ALU.subtract)\
                        .then_inc(sem("mem_split"), 1)
                x_norm("cross_norm_2", l * DC)
                refill("cross_wv_2", l, 3)

                def normalize(h):
                    dve.wait_ge(sem("score_free"), W.next("score_free"))
                    s = stat[:, h % 2, 0, :]
                    W.chain(dve.reciprocal(s[:, 2:4], s[:, 2:4]))
                    for t in range(TT):
                        p = prob[:, h % 2, 0, t * T:(t + 1) * T]
                        ins = ts(p, p, s[:, 2 + t:3 + t], None, ALU.mult)
                    ins.then_inc(sem("prob_ready"), 1)

                for h in range(4):
                    dve.wait_ge(sem("score_done"), W.next("score_done"))
                    dve.tensor_reduce(stat[:, h % 2, 0, 0:2], two(ps[:, 4 + h, :]), AX, ALU.max, negate=True)\
                        .then_inc(sem("max_ready"), 1)
                    if h >= 1:
                        normalize(h - 1)
                    if h >= 2:
                        split_bank(2 * (h - 2), h - 2)
                normalize(3)
                split_bank(4, 2)
                split_bank(6, 3)
                refill("cross_wo_2", l, 2)
                residual(1.0, lambda c: ("cross_wo_2", l, c))

            for c in range(4):
                dve.wait_ge(sem("x_turned"), W.next("x_turned"))
                dve.tensor_copy(xT[:, 2 * c:2 * c + 2, :], two(ps[:, 4 + c, :])).then_inc(sem("x_ready"), 1)
            for c in range(4):
                dve.wait_ge(sem("mem_turned"), W.next("mem_turned"))
                dve.tensor_copy(memT[:, 2 * c:2 * c + 2, :], two(ps[:, 4 + c, :])).then_inc(sem("mem_ready"), 1)
            dve.wait_ge(sem("vec_turned"), W.next("vec_turned"))
            dve.tensor_copy(vec[:, :], ps[:, 0, 0:NVEC])
            W.chain(dve.tensor_copy(bcast[:, 0:32], ps[:, 0, 256:288]))
            tt(lwork[:, 0:64], lrow[:, 0:64], lrow[:, 64:128], ALU.mult)
            W.chain(tt(lwork[:, 64:128], lrow[:, 128:192], lrow[:, 192:256], ALU.mult))
            dve.tensor_reduce(lwork[:, 128:130], lwork[:, 0:128].rearrange("p (a n) -> p a n", a=2), AX, ALU.add)\
                .then_inc(sem("lambda_sums"), 1)
            k = VCOL["hgrn_lb_2"]
            tt(lb[:, 0:4], vec[:, k:k + 4], vec[:, k + 4:k + 8], ALU.subtract).then_inc(sem("lb_diff"), 1)
            dve.wait_ge(sem("lambda_exp"), W.next("lambda_exp"))
            stt(lwork[:, 130:131], lwork[:, 130:131], LAMBDA_INIT, lwork[:, 131:132], ALU.add, ALU.subtract)\
                .then_inc(sem("lambda_ready"), 1)
            dve.wait_ge(sem("lb_log"), W.next("lb_log"))
            W.chain(ts(lb[:, 20:24], lb[:, 0:4], -1.0, None, ALU.mult))
            stt(lb[:, 12:16], lb[:, 20:24], 0.0, lb[:, 8:12], ALU.min, ALU.subtract)
            stt(lb[:, 16:20], lb[:, 0:4], 0.0, lb[:, 8:12], ALU.min, ALU.subtract).then_inc(sem("lb_ready"), 1)
            dve.wait_ge(sem("lambda_spread"), W.next("lambda_spread"))
            dve.tensor_copy(bcast[:, 32:33], ps[:, 1, 0:1])
            ts(bcast[:, 33:34], ps[:, 1, 0:1], -1.0, None, ALU.mult)
            dve.wait_ge(sem("gates_in"), W.next("gates_in", 16 * 9))
            ts(gb15[:, :], gbias[:, :], 1.0 / 15.0, None, ALU.mult)
            dve.wait_ge(sem("lb_prob"), W.next("lb_prob"))
            dve.wait_ge(sem("mem_rs"), W.next("mem_rs"))
            ts(bcast[:, 34:35], column("diff_norm_g", 0), 1.0 - LAMBDA_INIT, None, ALU.mult)\
                .then_inc(sem("params_ready"), 1)
            for kind, i in parts:
                scope[0] = kind[:3] + "_"
                {"gdn": gdn, "mlstm": mlstm, "diff": diff, "mlp": mlp, "hybrid": hybrid, "cross": cross,
                 "ffn1": lambda l: ffn("ffn1", l), "ffn2": lambda l: ffn("ffn2", l)}[kind](i)
            x_norm("final_norm_2", 0, last=True)


_INS = ["x", "norm_g", "mlp_w1", "mlp_w2", "gdn_w_in", "gdn_conv", "gdn_a_log", "gdn_dt_bias", "gdn_norm_g",
        "gdn_w_out", "mlstm_w_in", "mlstm_gate_b", "mlstm_norm_g", "mlstm_w_out", "diff_w_in", "diff_lambda",
        "diff_norm_g", "diff_w_out", "mem_2", "ffn1_norm_2", "ffn1_w_gate_2", "ffn1_w_up_2", "ffn1_w_down_2",
        "mix_norm_2", "w_in_2", "hgrn_lb_2", "hgrn_out_norm_2", "fox_f_bias_2", "w_out_2", "cross_norm_2",
        "mem_norm_2", "cross_wq_2", "cross_wk_2", "cross_wv_2", "cross_wo_2", "ffn2_norm_2", "ffn2_w_gate_2",
        "ffn2_w_up_2", "ffn2_w_down_2", "final_norm_2"]


def kernel(**inputs):
    import concourse.bacc as _bacc
    from concourse.bass_utils import run_bass_kernel_spmd as _run

    nc = _bacc.Bacc("TRN2", target_bir_lowering=False, num_devices=1)
    arrays, io = {}, {}
    for name in _INS:
        a = np.ascontiguousarray(inputs[name])
        arrays[f"in_{name}"] = a
        io[name] = nc.dram_tensor(f"in_{name}", a.shape, F32, kind="ExternalInput").ap()
    arrays["shape_constants"] = shape_constants()
    io["shape_constants"] = nc.dram_tensor("shape_constants", (P, NCONST), F32, kind="ExternalInput").ap()
    out = nc.dram_tensor("out", (1, T, D), F32, kind="ExternalOutput").ap()
    program(nc, io, out)
    r = _run(nc, [arrays], core_ids=[0])
    return r.results[0]["out"]
```

```python
import math
from contextlib import ExitStack

import numpy as np

import concourse.bass as bass
from concourse import mybir

F32 = mybir.dt.float32
F32R = mybir.dt.float32r
I32 = mybir.dt.int32
ALU = mybir.AluOpType
ACT = mybir.ActivationFunctionType
AX = mybir.AxisListType.X

P = 128
T = 256
TT = T // P
D = 1024
DC = D // P
EPS = 1e-6
RING = 3
PARTS = 2
SLAB = 2048
NEG = -1e30
ARENA = 21504
GATE_LOADS = 16 * 8
TREE = [1, 2, 4, 8, 16, 32, 64]
ED = 384

CONST = {}
_at = 0
for _name, _n in (("ident", P), ("after", P), ("upto", T), ("neg_causal", P), ("neg_block", P),
                  ("rotate", P), ("cos", T), ("sin", T), ("tree_ts", 7 * P), ("tree_st", 7 * P)):
    CONST[_name] = (_at, _at + _n)
    _at += _n
NCONST = _at


def shape_constants():
    c = np.zeros((P, NCONST), np.float32)
    row, col = np.arange(P)[:, None], np.arange(P)[None, :]

    def put(name, value):
        c[:, CONST[name][0]:CONST[name][1]] = value

    put("ident", row == col)
    put("after", row > col)
    put("upto", row <= np.arange(T)[None, :])
    put("neg_causal", np.where(col > row, NEG, 0.0))
    put("neg_block", np.where(col // 64 > row // 64, NEG, 0.0))
    rot = np.zeros((P, P), np.float32)
    cos, sin = np.ones((P, T), np.float32), np.zeros((P, T), np.float32)
    inv = (np.float32(500000.0) ** (-np.arange(0, 16, 2, dtype=np.float32) / np.float32(16))).astype(np.float32)
    ang = (np.arange(T, dtype=np.float32)[None, :] * inv[:, None]).astype(np.float32)
    for base in (0, 64):
        for j in range(8):
            rot[base + 8 + j, base + j] = -1.0
            rot[base + j, base + 8 + j] = 1.0
            for k in (j, 8 + j):
                cos[base + k] = np.cos(ang[j])
                sin[base + k] = np.sin(ang[j])
    put("rotate", rot)
    put("cos", cos)
    put("sin", sin)
    ts = []
    for m in TREE:
        same = row // (2 * m) == col // (2 * m)
        ts.append((same & (row % (2 * m) >= m) & (col % (2 * m) < m)).astype(np.float32))
    put("tree_ts", np.concatenate(ts, 1))
    put("tree_st", np.concatenate([m.T for m in ts], 1))
    return c


VROWS = [("norm_g", 128), ("ffn1_norm_2", 16), ("mix_norm_2", 16), ("cross_norm_2", 16), ("mem_norm_2", 16),
         ("ffn2_norm_2", 16), ("final_norm_2", 8), ("mlstm_norm_g", 8), ("hgrn_lb_2", 8),
         ("hgrn_out_norm_2", 2), ("gdn_norm_g", 2), ("diff_norm_g", 1)]
VCOL = {}
_at = 0
for _name, _n in VROWS:
    VCOL[_name] = _at
    _at += _n
NVEC = _at

DEPTH = 4
LAYERS2 = 2


def schedule():
    parts = []
    for i in range(DEPTH):
        parts += [(("gdn", "mlstm", "diff")[i % 3], i), ("mlp", i)]
    for l in range(LAYERS2):
        parts += [("ffn1", l), ("hybrid", l), ("cross", l), ("ffn2", l)]
    return parts


HYBRID_ORDER = (0, 1, 6, 7, 2, 3, 4, 5, 8, 9, 10, 11, 12, 13)
BETWEEN_LEVELS = {0: 9, 1: 10, 3: 11, 4: 12, 6: 13}


def slabs_of(kind, i):
    def cols(name, layer, n):
        return [(name, layer, "cols", j, 1) for j in range(n)]

    if kind == "gdn":
        return cols("gdn_w_in", i // 3, 16) + cols("gdn_w_out", i // 3, 4)
    if kind == "mlstm":
        return cols("mlstm_w_in", i // 3, 12) + cols("mlstm_w_out", i // 3, 4)
    if kind == "diff":
        return cols("diff_w_in", i // 3, 12) + cols("diff_w_out", i // 3, 4)
    if kind == "mlp":
        return cols("mlp_w1", i, 16) + [("mlp_w2", i, "rows", j, 4 if j == 15 else 1) for j in range(16)]
    if kind in ("ffn1", "ffn2"):
        return ([(kind, i, "gate_up", j, 1) for j in range(22)]
                + [(f"{kind}_w_down_2", i, "rows", j, 4 if j == 10 else 1) for j in range(11)])
    if kind == "hybrid":
        return [("w_in_2", i, "cols", j, 1) for j in HYBRID_ORDER] + cols("w_out_2", i, 4)
    assert kind == "cross"
    return (cols("cross_wq_2", i, 4) + cols("cross_wk_2", i, 4) + cols("cross_wv_2", i, 4)
            + cols("cross_wo_2", i, 4))


SHARED = ("x_ready", "sq_ready", "ss_ready", "rs_ready", "h_ready", "products_done", "slab_in", "stored", "out_",
          "high_split", "low_split", "hH_ready", "hL_ready", "mixH_ready", "mixL_ready", "pe_step", "act_step", "dve_step", "pool_step",
          "gates_in", "first_gates_in", "conv_in")

LAMBDA_INIT = 0.8 - 0.6 * math.exp(-0.3 * 2)


def program(nc, io, out, parts=None):
    parts = schedule() if parts is None else parts

    slabs, slab_no, groups_before = [], {}, {}
    count = 0
    for kind, i in parts:
        for s in slabs_of(kind, i):
            key = (s[0], s[1], s[3])
            slab_no[key] = len(slabs)
            groups_before[key] = count
            count += s[4]
            slabs.append(s + (count,))
    filled, landed = [0] * RING, []
    for n, s in enumerate(slabs):
        filled[n % RING] += 16 * (2 if s[2] == "gate_up" else 1)
        landed.append(filled[n % RING])
    x_at = {p: 4 * (n + 1) for n, p in enumerate(parts)}
    gdn_no = {i: n for n, (k, i) in enumerate([p for p in parts if p[0] == "gdn"])}

    with ExitStack() as ctx:
        def sb(name, shape, dt=F32):
            return ctx.enter_context(nc.sbuf_tensor(name, shape, dt))

        sems, scope = {}, [""]

        def sem(name):
            if not name.startswith(SHARED):
                name = scope[0] + name
            if name not in sems:
                sems[name] = ctx.enter_context(nc.semaphore(name))
            return sems[name]

        class Waits:

            def __init__(self, eng, step):
                self.eng, self.seen, self.step, self.steps = eng, {}, sem(step), 0

            def next(self, name, n=1):
                key = sem(name).name
                self.seen[key] = self.seen.get(key, 0) + n
                return self.seen[key]

            def mark(self, ins):
                self.steps += 1
                ins.then_inc(self.step, 1)
                return self.steps

            def chain(self, ins):
                self.eng.wait_ge(self.step, self.mark(ins))

        def group(name, layer, j, g=0):
            return groups_before[(name, layer, j)] + g + 1

        xT = sb("xT", [P, DC, T])
        hT = sb("hT", [P, DC, T])
        sq = sb("sq", [P, DC, T])
        rs = sb("rs", [P, T])
        rs_mem = sb("rs_mem", [P, T])
        hH = sb("hH", [P, DC, T], F32R)
        hL = sb("hL", [P, DC, T], F32R)
        ring = sb("ring", [P, RING, SLAB])
        wH = sb("wH", [P, PARTS, SLAB], F32R)
        wL = sb("wL", [P, PARTS, SLAB], F32R)
        const = sb("const", [P, NCONST])
        ones = sb("ones", [P, T])
        epsc = sb("epsc", [P, 1])
        memT = sb("memT", [P, DC, T])
        vec = sb("vec", [P, NVEC])
        bcast = sb("bcast", [P, 40])
        lb = sb("lb", [P, 28])
        gw = sb("gw", [P, 5, DC, 16])
        gbias = sb("gbias", [8, 4])
        gb15 = sb("gb15", [8, 4])
        convrow = sb("convrow", [96, P])
        with nc.sbuf_tensor("hidden_parts", [P, 2, 32, T], F32R) as hidden_parts:
            hidH, hidL = hidden_parts[:, 0, :, :], hidden_parts[:, 1, :, :]
        arena = sb("arena", [P, ARENA])
        ps = ctx.enter_context(nc.psum_tensor("ps", [P, 8, 512], F32))

        def cc(name, k=None):
            a, b = CONST[name]
            return const[:, a:b] if k is None else const[:, a + k * P:a + (k + 1) * P]

        def column(name, k):
            return vec[:, VCOL[name] + k:VCOL[name] + k + 1]

        ident = cc("ident")

        class Arena:
            def __init__(self, at=0):
                self.at = at

            def take(self, n, pat=None, **k):
                v = arena[:, self.at:self.at + n]
                self.at += n
                assert self.at <= ARENA, self.at
                return v.rearrange(pat, **k) if pat else v

        A = Arena(2 * 32 * T)
        act_s = A.take(2 * 512, "p (b n) -> p b n", b=2)
        prod_s = A.take(2 * 512, "p (b n) -> p b n", b=2)

        A = Arena()
        qk = A.take(16 * T, "p (c t) -> p c t", c=16)
        v_tok = A.take(TT * D, "p (i n) -> p i n", i=TT)
        gate = A.take(DC * T, "p (c t) -> p c t", c=DC)
        pair = A.take(8 * ED, "p (h n) -> p h n", h=8)
        after_pair = A.at
        kkb = A.take(8 * ED, "p (h n) -> p h n", h=8)
        staging = A.at
        inv = A.take(TT * 8 * P, "p (i h n) -> p i h n", i=TT, h=8)
        invT = A.take(TT * 8 * P, "p (i h n) -> p i h n", i=TT, h=8)
        level = A.take(TT * 8 * P, "p (i h n) -> p i h n", i=TT, h=8)
        scaled = A.take(2 * ED, "p (b n) -> p b n", b=2)
        tokg = A.take(96)
        convw = A.take(96)
        w_sol = level.rearrange("p i h n -> p i (h n)")
        u_sol = inv.rearrange("p i h n -> p i (h n)")
        A = Arena(staging)
        pre = A.take(2 * 2 * 260, "p (b c n) -> p b c n", b=2, c=2)
        conv = A.take(2 * 2 * T, "p (b c n) -> p b c n", b=2, c=2)
        vch = A.take(2 * 2 * T, "p (b c n) -> p b c n", b=2, c=2)

        A = Arena(after_pair)
        rows = A.take(12 * T, "p (r t) -> p r t", r=12)
        rcol = A.take(16, "p (i h) -> p i h", i=TT)
        em_s = A.take(2 * 2 * T, "p (b t) -> p b t", b=2)
        lay = A.at
        raw = arena[:, lay:lay + 4 * 512].rearrange("p (b n) -> p b n", b=4)
        prob = A.take(2 * 2 * 512, "p (b c n) -> p b c n", b=2, c=2)
        probT = A.take(2 * 512, "p (b n) -> p b n", b=2)
        stat = A.take(2 * 2 * 4, "p (b c s) -> p b c s", b=2, c=2)
        num_s = A.take(DC * T, "p (c t) -> p c t", c=DC)
        mem_n = num_s
        memH, memL = hidden_parts[:, 0, 24:32, :], hidden_parts[:, 1, 0:8, :]
        A = Arena(lay)
        zcum = A.take(4 * T, "p (h t) -> p h t", h=4)
        glog = A.take(4 * T, "p (h t) -> p h t", h=4)
        factor = num_s.rearrange("p (b h) t -> p b h t", b=2)

        vec_rows, vec_rows2 = arena[:, 0:P], arena[:, P:2 * P]
        brow = arena[0:1, 256:288]
        lrow = arena[0:1, 320:576]
        lwork = arena[0:1, 600:732]
        x_rows = sq[:, :, :].rearrange("p c t -> p (c t)").rearrange("p (i n) -> p i n", i=TT)
        mem_rows = hT[:, :, :].rearrange("p c t -> p (c t)").rearrange("p (i n) -> p i n", i=TT)
        out_rows = memT[:, :, :].rearrange("p c t -> p (c t)").rearrange("p (i n) -> p i n", i=TT)

        def two(v):
            return v.rearrange("p (c t) -> p c t", c=2)

        def slab_source(s):
            name, layer, how, j = s[:4]
            if how == "cols":
                w = io[name][layer].rearrange("(c p) n -> p c n", p=P)
                return [(0, SLAB, DC, w[:, :, 256 * j:256 * (j + 1)])]
            if how == "gate_up":
                g = io[f"{name}_w_gate_2"][layer].rearrange("(c p) n -> p c n", p=P)
                u = io[f"{name}_w_up_2"][layer].rearrange("(c p) n -> p c n", p=P)
                return [(0, DC * P, DC, g[:, :, P * j:P * (j + 1)]),
                        (DC * P, 2 * DC * P, DC, u[:, :, P * j:P * (j + 1)])]
            w = io[name][layer][2 * P * j:2 * P * (j + 1), :].rearrange("(c p) n -> p c n", p=P)
            return [(0, 2 * D, 2, w)]

        def flat_rows(ap):
            names = "abcd"[:len(ap.shape)]
            if len(names) > 1:
                ap = ap.rearrange(f"{' '.join(names)} -> ({' '.join(names)})")
            return ap

        block = ctx.enter_context(nc.Block())

        @block.sync
        def _(sp):
            sp.dma_start(ident, io["shape_constants"][:, 0:P]).then_inc(sem("ident_in"), 16)
            sp.dma_start(x_rows, io["x"][0].rearrange("(i p) n -> p i n", p=P)).then_inc(sem("x_in"), 16)
            sp.dma_start(mem_rows, io["mem_2"][0].rearrange("(i p) n -> p i n", p=P)).then_inc(sem("mem_in"), 16)
            at = 0
            for name, n in VROWS:
                dst = vec_rows[0:n, :] if name == "norm_g" else vec_rows2[at - P:at - P + n, :]
                sp.dma_start(dst, flat_rows(io[name]).rearrange("(r q) -> r q", q=P)).then_inc(sem("vec_in"), 16)
                at += n
            for b, name in ((0, "gdn_a_log"), (16, "gdn_dt_bias")):
                sp.dma_start(brow[:, b:b + 16], flat_rows(io[name]).rearrange("(a n) -> a n", a=1))\
                    .then_inc(sem("vec_in"), 16)
            sp.dma_start(lrow, flat_rows(io["diff_lambda"]).rearrange("(a n) -> a n", a=1))\
                .then_inc(sem("vec_in"), 16)
            for n, s in enumerate(slabs):
                if n == PARTS:
                    sp.dma_start(const[:, P:NCONST], io["shape_constants"][:, P:NCONST])\
                        .then_inc(sem("const_in"), 16)
                if n >= RING:
                    sp.wait_ge(sem("low_split"), n - RING + 1)
                for a, b, c, src in slab_source(s):
                    sp.dma_start(ring[:, n % RING, a:b].rearrange("p (c n) -> p c n", c=c), src)\
                      .then_inc(sem(f"slab_in{n % RING}"), 16)
            for i in range(TT):
                sp.wait_ge(sem("out_tile"), i + 1)
                sp.dma_start(out[0, i * P:(i + 1) * P, :], out_rows[:, i, :]).then_inc(sem("stored"), 16)
            sp.wait_ge(sem("stored"), 16 * TT)

        @block.gpsimd
        def _(pool):
            scope[0] = ""
            W = Waits(pool, "pool_step")
            pool.memset(ones[:, :], 1.0)
            pool.memset(epsc[:, :], EPS).then_inc(sem("ones_set"), 1)
            def gate_columns(k, name, l, c0, n, done):
                pool.dma_start(gw[:, k, :, 0:n], io[name][l].rearrange("(c p) n -> p c n", p=P)[:, :, c0:c0 + n])\
                    .then_inc(sem(done), 16)

            def conv_weights(j, done):
                pool.dma_start(convrow[:, :], io["gdn_conv"][j].rearrange("k (c q) -> (k c) q", q=P))\
                    .then_inc(sem(done), 16)

            gate_columns(0, "gdn_w_in", 0, 4096, 16, "first_gates_in")
            conv_weights(0, "conv_in")
            gate_columns(1, "gdn_w_in", 1, 4096, 16, "gates_in")
            gate_columns(2, "mlstm_w_in", 0, 3072, 16, "gates_in")
            for l in range(2):
                gate_columns(3 + l, "w_in_2", l, 3584, 8, "gates_in")
            for k, src in enumerate((io["mlstm_gate_b"][0, 0], io["mlstm_gate_b"][0, 1],
                                     io["fox_f_bias_2"][0], io["fox_f_bias_2"][1])):
                pool.dma_start(gbias[:, k:k + 1], src.rearrange("(h a) -> h a", a=1)).then_inc(sem("gates_in"), 16)

            def mask(h):
                pool.wait_ge(sem("pair_exp"), W.next("pair_exp"))
                v = pair[:, h, :].rearrange("p (k n) -> p k n", k=3)[:, 0:3:2, :]
                pool.affine_select(out=v, in_=v, compare_op=ALU.is_ge, fill=0.0, base=0,
                                   pattern=[[0, 2], [1, P]], channel_multiplier=-1).then_inc(sem("pair_masked"), 1)

            def gdn(i):
                pool.wait_ge(sem("x_ready"), x_at[("gdn", i)])
                pool.memset(pre[:, :, :, 0:3], 0.0).then_inc(sem("pad_set"), 1)
                pool.wait_ge(sem("tok_gates"), W.next("tok_gates"))
                for h in range(8):
                    if h >= 2:
                        pool.wait_ge(sem("decay_done"), W.next("decay_done"))
                    pool.tensor_scalar(scaled[:, h % 2, 0:T], cc("upto"), tokg[:, h:h + 1], None, ALU.mult)
                    pool.tensor_scalar(scaled[:, h % 2, T:ED], cc("upto")[:, 0:P], tokg[:, 8 + h:9 + h], None,
                                       ALU.mult).then_inc(sem("scaled_ready"), 1)
                    if h >= 1:
                        mask(h - 1)
                mask(7)
                pool.wait_ge(sem("decay_done"), W.next("decay_done", 2))
                pool.wait_ge(sem("v_done"), W.next("v_done", 4))
                for m in (inv, invT):
                    for t in range(TT):
                        last = pool.tensor_copy(m[:, t, :, :], ident[:, None, :].broadcast_to([P, 8, P]))
                last.then_inc(sem("inverse_start"), 1)
                if i == 0:
                    pool.wait_ge(sem("conv_turned"), 1)
                    conv_weights(1, "conv_in")

            for kind, i in parts:
                scope[0] = kind[:3] + "_"
                if kind == "gdn":
                    gdn(i)
                elif kind == "mlstm":
                    for h in range(8):
                        mask(h)

        @block.tensor
        def _(pe):
            scope[0] = ""
            W = Waits(pe, "pe_step")

            def mm(o, l, r, start, stop, **k):
                return pe.matmul(o, l, r, start=start, stop=stop, **k)

            def high(n, c):
                pe.wait_ge(sem("high_split"), n + 1)
                return wH[:, n % PARTS, :].rearrange("p (c n) -> p c n", c=c)

            def low(n, c):
                return wL[:, n % PARTS, :].rearrange("p (c n) -> p c n", c=c)

            def three(dst, w, x, chunks, before=None, first=True, last=True, second="x"):
                ins = None
                for pair in (((0, 0), (0, 1), (1, 0)) if second == "x" else ((0, 0), (1, 0), (0, 1))):
                    for k in range(chunks):
                        if before:
                            before(pair, k)
                        ins = mm(dst, w[pair[0]](k), x[pair[1]](k), first and pair == (0, 0) and k == 0,
                                 last and pair == ((1, 0) if second == "x" else (0, 1)) and k == chunks - 1,
                                 **({"skip_group_check": True} if chunks == 1 else {}))
                return ins

            def low_weights(n, pair_):
                def before(pair, k):
                    if pair == pair_ and k == 0:
                        pe.wait_ge(sem("low_split"), n + 1)
                return before

            def bank_of(j):
                return 4 + j % 4

            def first_products(name, layer, js, c, at):
                n = [slab_no[(name, layer, j)] for j in js]
                high_w = [high(n[0], c), high(n[1], c)]
                low_w = [low(n[0], c), low(n[1], c)]
                pe.wait_ge(sem("low_split"), n[0] + 1)

                def both_halves(b, w, x, k, ends=False):
                    for m in range(2):
                        ins = mm(ps[:, 4 + b, m * T:(m + 1) * T], at(w, k, m), x[:, k, :],
                                 w is high_w[b] and x is hH and k == 0 and m == 0, ends and k == DC - 1 and m == 1,
                                 skip_group_check=True)
                    return ins

                for k0 in range(0, DC, 2):
                    pe.wait_ge(sem("hH_ready"), W.next("hH_ready"))
                    for b, w in ((0, high_w[0]), (0, low_w[0]), (1, high_w[1])):
                        for k in (k0, k0 + 1):
                            both_halves(b, w, hH, k)
                for k in range(DC):
                    if k % 2 == 0:
                        pe.wait_ge(sem("hL_ready"), W.next("hL_ready"))
                    last = both_halves(0, high_w[0], hL, k, ends=True)
                last.then_inc(sem("products_done"), 1)
                for k in range(DC):
                    both_halves(1, high_w[1], hL, k)
                pe.wait_ge(sem("low_split"), n[1] + 1)
                for k in range(DC):
                    last = both_halves(1, low_w[1], hH, k, ends=True)
                last.then_inc(sem("products_done"), 1)

            def columns(w, k, m):
                return w[:, k, m * P:(m + 1) * P]

            def to_channels(name, layer, j, bank, src=(hH, hL), free=None):
                n = slab_no[(name, layer, j)]
                wh, wl = high(n, DC), low(n, DC)
                if free and j >= 4:
                    pe.wait_ge(sem(free), W.next(free))
                for m in range(2):
                    last = three(ps[:, bank, m * T:(m + 1) * T],
                                 [lambda k: wh[:, k, m * P:(m + 1) * P], lambda k: wl[:, k, m * P:(m + 1) * P]],
                                 [lambda k: src[0][:, k, :], lambda k: src[1][:, k, :]], DC,
                                 low_weights(n, (1, 0)) if m == 0 else None)
                last.then_inc(sem("products_done"), 1)

            def to_tokens(name, layer, j, bank, src=(hH, hL)):
                n = slab_no[(name, layer, j)]
                wh, wl = high(n, DC), low(n, DC)
                for i in range(TT):
                    last = three(ps[:, bank, i * T:(i + 1) * T],
                                 [lambda k: src[0][:, k, i * P:(i + 1) * P], lambda k: src[1][:, k, i * P:(i + 1) * P]],
                                 [lambda k: wh[:, k, :], lambda k: wl[:, k, :]], DC,
                                 low_weights(n, (0, 1)) if i == 0 else None, second="w")
                last.then_inc(sem("products_done"), 1)

            def norm_sum(bank=7):
                for c in range(4):
                    pe.wait_ge(sem("sq_ready"), W.next("sq_ready"))
                    for k in (2 * c, 2 * c + 1):
                        last = mm(ps[:, bank, 0:T], ones[:, 0:P], sq[:, k, :], k == 0, k == DC - 1)
                last.then_inc(sem("ss_ready"), 1)

            def head_sums(n):
                for b in range(n):
                    pe.wait_ge(sem("sq_ready"), W.next("sq_ready"))
                    mm(ps[:, 4 + b, :], ones[:, 0:P], sq[:, 2 * b:2 * b + 2, :], True, True)\
                        .then_inc(sem("hs_ready"), 1)

            def out_product(name, layer):
                def mix_waits(pair, k):
                    if pair == (0, 0) and k % 2 == 0:
                        pe.wait_ge(sem("mixH_ready"), W.next("mixH_ready"))
                    if pair == (1, 0) and k == 0:
                        pe.wait_ge(sem("low_split"), slab_no[(name, layer, 0)] + 1)
                    if pair == (0, 1) and k % 2 == 0:
                        pe.wait_ge(sem("mixL_ready"), W.next("mixL_ready"))

                for j in range(4):
                    n = slab_no[(name, layer, j)]
                    wh, wl = high(n, DC), low(n, DC)
                    for m in range(2):
                        last = three(ps[:, j, m * T:(m + 1) * T],
                                     [lambda k: wh[:, k, m * P:(m + 1) * P], lambda k: wl[:, k, m * P:(m + 1) * P]],
                                     [lambda k: hH[:, k, :], lambda k: hL[:, k, :]], DC,
                                     mix_waits if j + m == 0 else low_weights(n, (1, 0)) if m == 0 else None,
                                     second="w" if j + m == 0 else "x")
                    last.then_inc(sem("products_done"), 1)

            def down_product(name, layer, chunks, waited):
                for j in range(chunks // 2):
                    n = slab_no[(name, layer, j)]
                    wh, wl = high(n, 2), low(n, 2)
                    for kk in (2 * j, 2 * j + 1):
                        if kk in waited:
                            pe.wait_ge(sem("hidden_ready"), W.next("hidden_ready"))
                        end = kk == chunks - 1
                        for m in range(DC):
                            last = three(ps[:, m // 2, (m % 2) * T:(m % 2 + 1) * T],
                                         [lambda k: wh[:, kk % 2, m * P:(m + 1) * P],
                                          lambda k: wl[:, kk % 2, m * P:(m + 1) * P]],
                                         [lambda k: hidH[:, kk, :], lambda k: hidL[:, kk, :]], 1,
                                         low_weights(n, (1, 0)) if m == 0 and kk % 2 == 0 else None,
                                         first=kk == 0 and m % 2 == 0, last=end and m % 2 == 1)
                            if end and m % 2:
                                last.then_inc(sem("products_done"), 1)
                    if not end:
                        last.then_inc(sem("products_done"), 1)

            def mlp(i):
                norm_sum()
                first_products("mlp_w1", i, (0, 1), DC, columns)
                for j in range(2, 16):
                    to_channels("mlp_w1", i, j, bank_of(j), free="bank_read")
                down_product("mlp_w2", i, 32, range(0, 32, 2))
                pe.wait_ge(sem("bank_read"), W.next("bank_read", 4))
                norm_sum()

            def ffn(kind, l):
                norm_sum()
                first_products(kind, l, (0, 1), 2 * DC, lambda w, k, half: w[:, half * DC + k, :])
                for n in range(2, 22):
                    u = slab_no[(kind, l, n)]
                    wh, wl = high(u, 2 * DC), low(u, 2 * DC)
                    if n >= 4:
                        pe.wait_ge(sem("bank_read"), W.next("bank_read"))
                    for half in range(2):
                        last = three(ps[:, 4 + n % 4, half * T:(half + 1) * T],
                                     [lambda k: wh[:, half * DC + k, :], lambda k: wl[:, half * DC + k, :]],
                                     [lambda k: hH[:, k, :], lambda k: hL[:, k, :]], DC,
                                     low_weights(u, (1, 0)) if half == 0 else None)
                    last.then_inc(sem("products_done"), 1)
                down_product(f"{kind}_w_down_2", l, 22, range(22))
                pe.wait_ge(sem("bank_read"), W.next("bank_read", 4))

            def outputs(heads, values):
                for h in range(heads):
                    b, c0 = h // 2, (h % 2) * T
                    mm(ps[:, b, c0:c0 + T], values(0, h), pair[:, h, 0:T], True, False)
                    last = mm(ps[:, b, c0 + P:c0 + T], values(1, h), pair[:, h, T:ED], False, True)
                    if h % 2:
                        last.then_inc(sem("o_ready"), 1)

            def gdn(i):
                j = i // 3
                if j == 0:
                    pe.wait_ge(sem("first_gates_in"), 16)
                else:
                    pe.wait_ge(sem("gates_in"), GATE_LOADS)
                norm_sum()
                pe.wait_ge(sem("conv_in"), 16 * (j + 1))
                pe.transpose(ps[:, 3, 0:96], convrow[0:96, :], ident[0:96, 0:96]).then_inc(sem("conv_turned"), 1)
                first_products("gdn_w_in", j, (0, 1), DC, columns)
                for t in range(TT):
                    for k in range(DC):
                        last = mm(ps[:, 3, 128 + 16 * t:144 + 16 * t], hT[:, k, t * P:(t + 1) * P], gw[:, j, k, :],
                                  k == 0, k == DC - 1)
                last.then_inc(sem("gates_done"), 1)

                def turn_values(g):
                    pe.wait_ge(sem("silu_done"), 12 * gdn_no[i] + 8 + g + 1)
                    if g > 0:
                        pe.wait_ge(sem("v_done"), W.next("v_done"))
                    for c in range(2):
                        for t in range(TT):
                            last = pe.transpose(ps[:, 2, (2 * t + c) * P:(2 * t + c + 1) * P],
                                                vch[:, g % 2, c, t * P:(t + 1) * P], ident)
                    last.then_inc(sem("v_turned"), 1)

                for s in range(2, 16):
                    to_channels("gdn_w_in", j, s, bank_of(s), free="evac")
                    if s >= 12:
                        turn_values(s - 12)
                pe.wait_ge(sem("evac"), W.next("evac", 4))
                pe.wait_ge(sem("v_done"), W.next("v_done"))
                for h in range(8):
                    pe.wait_ge(sem("scaled_ready"), W.next("scaled_ready"))
                    if h >= 2:
                        pe.wait_ge(sem("pair_exp"), W.next("pair_exp"))
                    b = 4 + h % 2
                    mm(ps[:, b, 0:T], cc("after"), scaled[:, h % 2, 0:T], True, False)
                    mm(ps[:, b, P:T], ones[:, 0:P], scaled[:, h % 2, T:ED], False, True)
                    mm(ps[:, b, T:ED], cc("after"), scaled[:, h % 2, T:ED], True, True).then_inc(sem("decay_done"), 1)
                pe.wait_ge(sem("pair_exp"), W.next("pair_exp", 2))
                for b in range(8):
                    pe.wait_ge(sem("sq_ready"), W.next("sq_ready"))
                    if b >= 4:
                        pe.wait_ge(sem("hs_free"), W.next("hs_free"))
                    mm(ps[:, b % 4, :], ones[:, 0:P], sq[:, 2 * (b % 4):2 * (b % 4) + 2, :], True, True)\
                        .then_inc(sem("hs_ready"), 1)
                pe.wait_ge(sem("hs_free"), W.next("hs_free", 4))
                pe.wait_ge(sem("qk_normed"), W.next("qk_normed", 8))
                for n in range(16):
                    h, b = n % 8, n % 4
                    r = qk[:, (8 if n < 8 else 0) + h, :]
                    if n >= 4:
                        pe.wait_ge(sem("score_free"), W.next("score_free"))
                    mm(ps[:, b, 0:T], qk[:, 8 + h, 0:P], r, True, True)
                    mm(ps[:, b, T:ED], qk[:, 8 + h, P:T], r[:, P:T], True, True).then_inc(sem("score_done"), 1)
                pe.wait_ge(sem("score_free"), W.next("score_free", 4))
                pe.wait_ge(sem("inverse_start"), W.next("inverse_start"))
                for n in range(len(TREE)):
                    for q in range(4):
                        t, h0 = q // 2, 4 * (q % 2)
                        if n:
                            pe.wait_ge(sem("inverse_done"), 28 * gdn_no[i] + 4 * (n - 1) + q + 1)
                        for h in range(4):
                            c0 = 0 if t == 0 else T
                            last = mm(ps[:, 4 + q, h * P:(h + 1) * P], kkb[:, h0 + h, c0:c0 + P],
                                      inv[:, t, h0 + h, :], True, True)
                        last.then_inc(sem("level_done"), 1)
                    for q in range(4):
                        t, h0 = q // 2, 4 * (q % 2)
                        pe.wait_ge(sem("level_masked"), W.next("level_masked"))
                        if q >= 2:
                            pe.wait_ge(sem("inverse_done"), 28 * gdn_no[i] + 4 * n + q - 1)
                        if n < len(TREE) - 1:
                            for h in range(4):
                                mm(ps[:, 2 * (q % 2), h * P:(h + 1) * P], invT[:, t, h0 + h, :],
                                   level[:, t, h0 + h, :], True, True)
                        for h in range(4):
                            last = mm(ps[:, 2 * (q % 2) + 1, h * P:(h + 1) * P], level[:, t, h0 + h, :],
                                      invT[:, t, h0 + h, :], True, True)
                        last.then_inc(sem("delta_done"), 1)
                pe.wait_ge(sem("inverse_done"), 28 * (gdn_no[i] + 1))

                def solve(b0, b, lhs, rhs):
                    for h in range(4 * b, 4 * b + 4):
                        last = mm(ps[:, b0 + b, (h % 4) * P:(h % 4 + 1) * P], lhs(h), rhs(h), True, True)
                    last.then_inc(sem("w_done"), 1)

                for b in range(2):
                    solve(4, b, lambda h: invT[:, 0, h, :], lambda h: v_tok[:, 0, h * P:(h + 1) * P])
                for b in range(2):
                    pe.wait_ge(sem("w_ready"), W.next("w_ready"))
                    solve(6, b, lambda h: kkb[:, h, P:T], lambda h: w_sol[:, 0, h * P:(h + 1) * P])
                for b in range(2):
                    pe.wait_ge(sem("w_ready"), W.next("w_ready"))
                    solve(4, b, lambda h: invT[:, 1, h, :], lambda h: v_tok[:, 1, h * P:(h + 1) * P])
                pe.wait_ge(sem("w_ready"), W.next("w_ready", 2))
                outputs(8, lambda t, h: u_sol[:, t, h * P:(h + 1) * P])
                head_sums(4)
                out_product("gdn_w_out", j)
                norm_sum()

            def spread(dst, h, row):
                return mm(dst, ident[0:8, h:h + 1].broadcast_to([8, P]), row, True, True)

            def mlstm(i):
                norm_sum()
                first_products("mlstm_w_in", 0, (0, 1), DC, columns)
                for s in range(2, 4):
                    to_channels("mlstm_w_in", 0, s, bank_of(s))
                pe.wait_ge(sem("gates_in"), GATE_LOADS)
                for g in range(2):
                    for k in range(DC):
                        last = mm(ps[0:8, 0, g * T:(g + 1) * T], gw[:, 2, k, 8 * g:8 * g + 8], hT[:, k, :],
                                  k == 0, k == DC - 1)
                last.then_inc(sem("gates_done"), 1)
                for s in range(4, 12):
                    pe.wait_ge(sem("evac"), W.next("evac"))
                    (to_tokens if s < 8 else to_channels)("mlstm_w_in", 0, s, bank_of(s))
                pe.wait_ge(sem("rows_ready"), W.next("rows_ready"))
                for t in range(TT):
                    last = pe.transpose(ps[:, 1, 8 * t:8 * t + 8], rows[0:8, 6, t * P:(t + 1) * P], ident[0:8, 0:8])
                last.then_inc(sem("r_turned"), 1)
                pe.wait_ge(sem("rcol_ready"), W.next("rcol_ready"))
                pe.wait_ge(sem("evac"), W.next("evac", 4))
                for h in range(8):
                    if h >= 2:
                        pe.wait_ge(sem("pair_exp"), W.next("pair_exp"))
                    spread(ps[:, h % 2, 0:T], h, rows[0:8, 7, :]).then_inc(sem("decay_done"), 1)
                pe.wait_ge(sem("pair_exp"), W.next("pair_exp", 2))
                for h in range(8):
                    if h >= 4:
                        pe.wait_ge(sem("score_free"), W.next("score_free"))
                    r0 = 64 * (h % 2)
                    q_, k_ = qk[r0:r0 + 64, h // 2, :], qk[r0:r0 + 64, 4 + h // 2, :]
                    mm(ps[:, 4 + h % 4, 0:T], k_[:, 0:P], q_, True, True)
                    mm(ps[:, 4 + h % 4, T:ED], k_[:, P:T], q_[:, P:T], True, True).then_inc(sem("score_done"), 1)
                pe.wait_ge(sem("score_free"), W.next("score_free", 4))
                outputs(8, lambda t, h: v_tok[:, t, h * P:(h + 1) * P])
                pe.wait_ge(sem("floor_ready"), W.next("floor_ready"))
                for h in range(8):
                    if h >= 2:
                        pe.wait_ge(sem("den_free"), W.next("den_free"))
                    b = 4 + h % 2
                    mm(ps[:, b, 0:T], ones[:, 0:P], pair[:, h, 0:T], True, False)
                    mm(ps[:, b, P:T], ones[:, 0:P], pair[:, h, T:ED], False, True)
                    spread(ps[:, b, T:2 * T], h, rows[0:8, 8, :]).then_inc(sem("den_done"), 1)
                pe.wait_ge(sem("den_free"), W.next("den_free", 2))
                head_sums(4)
                out_product("mlstm_w_out", 0)
                norm_sum()

            def attention(heads, comps, operands, negative, cum, wide):
                for h in range(heads + 1):
                    for c in range(comps if h < heads else 0):
                        n = comps * h + c
                        if n >= 4:
                            pe.wait_ge(sem("score_free"), W.next("score_free"))
                        b = 4 + n % 4
                        q_, k_ = operands(h, c)
                        for c0, t0, width in ((0, 0, P), (P, P, T)):
                            dst = ps[:, b, c0:c0 + width]
                            mm(dst, q_[:, t0:t0 + P], k_[:, 0:width], True, False)
                            if cum is not None:
                                mm(dst, ident[0:8, h:h + 1].broadcast_to([8, P]), cum[:, 0:width], False, False)
                            last = mm(dst[:, width - P:width], ident, negative, False, True)
                        last.then_inc(sem("score_done"), 1)
                    if h == 0:
                        continue
                    hh = h - 1
                    pe.wait_ge(sem("prob_ready"), W.next("prob_ready"))
                    for k in range(3):
                        last = pe.transpose(ps[:, 3, k * P:(k + 1) * P],
                                            prob[:, hh % 2, comps - 1, k * P:(k + 1) * P], ident)
                    last.then_inc(sem("prob_turned"), 1)
                    pe.wait_ge(sem("probT_ready"), W.next("probT_ready"))
                    if wide:
                        o = ps[:, (hh // 2) % 3, (hh % 2) * T:(hh % 2 + 1) * T]
                        v = [v_tok[:, t, P * hh:P * hh + P] for t in range(TT)]
                        if hh == 6:
                            pe.wait_ge(sem("o_moved"), W.next("o_moved"))
                        end = hh % 2 == 1
                    else:
                        c = hh // 2
                        o = ps[64 * (hh % 2):64 * (hh % 2) + 64, 1 + c // 2, (c % 2) * T:(c % 2 + 1) * T]
                        v = [v_tok[:, t, 512 + 64 * hh:576 + 64 * hh] for t in range(TT)]
                        end = hh % 4 == 3
                    mm(o, v[0], probT[:, hh % 2, 0:T], True, False)
                    last = mm(o[:, P:T], v[1], probT[:, hh % 2, T:ED], False, True)
                    if end:
                        last.then_inc(sem("o_ready"), 1)

            def diff(i):
                norm_sum()

                def rotate(g):
                    pe.wait_ge(sem("raw_ready"), W.next("raw_ready"))
                    if g >= 2:
                        pe.wait_ge(sem("roped"), W.next("roped"))
                    mm(ps[:, g % 2, :], cc("rotate"), raw[:, g % 4, :], True, True).then_inc(sem("rotated"), 1)

                first_products("diff_w_in", 0, (0, 1), DC, columns)
                for s in range(2, 8):
                    to_channels("diff_w_in", 0, s, bank_of(s))
                    if s == 2:
                        rotate(0)
                    rotate(s - 1)
                for s in range(8, 12):
                    to_tokens("diff_w_in", 0, s, bank_of(s))
                    if s == 8:
                        rotate(7)
                pe.wait_ge(sem("roped"), W.next("roped", 2))
                pe.wait_ge(sem("evac"), W.next("evac", 4))
                attention(8, 2, lambda h, c: (qk[64 * c:64 * c + 64, h, :], qk[64 * c:64 * c + 64, 8 + h, :]),
                          cc("neg_block"), None, True)
                head_sums(4)
                out_product("diff_w_out", 0)
                norm_sum()

            def hybrid(l):
                norm_sum()
                first_products("w_in_2", l, HYBRID_ORDER[0:2], DC, columns)
                for n, s in list(enumerate(HYBRID_ORDER))[2:8]:
                    if n == 4:
                        pe.wait_ge(sem("gates_in"), GATE_LOADS)
                        for k in range(DC):
                            last = mm(ps[0:8, 0, 0:T], gw[:, 3 + l, k, 0:8], hT[:, k, :], k == 0, k == DC - 1)
                        last.then_inc(sem("gates_done"), 1)
                    if n >= 4:
                        pe.wait_ge(sem("evac"), W.next("evac"))
                    (to_tokens if s in (4, 5) else to_channels)("w_in_2", l, s, bank_of(n))
                to_channels("w_in_2", l, 8, 1)
                pe.wait_ge(sem("evac"), W.next("evac", 4))
                m = 0
                for n in range(len(TREE) + 2):
                    if n <= len(TREE):
                        pe.wait_ge(sem("factor_ready"), W.next("factor_ready"))
                    for t in range(1 if n == len(TREE) else TT):
                        if m >= 4:
                            pe.wait_ge(sem("tree_copied"), W.next("tree_copied"))
                        for h in range(4):
                            if n < len(TREE):
                                l_ = r_ = factor[:, n % 2, h, t * P:(t + 1) * P]
                            elif n == len(TREE):
                                l_, r_ = factor[:, n % 2, h, 0:P], factor[:, n % 2, h, P:T]
                            else:
                                l_, r_ = qk[:, 4 + h, t * P:(t + 1) * P], qk[:, h, t * P:(t + 1) * P]
                            last = mm(ps[:, 4 + m % 4, h * P:(h + 1) * P], l_, r_, True, True)
                        last.then_inc(sem("tree_done"), 1)
                        m += 1
                    if n in BETWEEN_LEVELS:
                        s = BETWEEN_LEVELS[n]
                        if s == 11:
                            pe.wait_ge(sem("fz_ready"), W.next("fz_ready"))
                        if s >= 12:
                            pe.wait_ge(sem("evac"), W.next("evac"))
                        (to_tokens if s >= 12 else to_channels)("w_in_2", l, s, (s - 7) % 4)
                pe.wait_ge(sem("evac"), W.next("evac", 4))
                pe.wait_ge(sem("tree_copied"), W.next("tree_copied", 4))
                outputs(4, lambda t, h: v_tok[:, t, h * P:(h + 1) * P])
                head_sums(2)
                pe.wait_ge(sem("mixed"), W.next("mixed", 2))
                pe.wait_ge(sem("rows_ready"), W.next("rows_ready"))
                attention(8, 1, lambda h, c: (qk[64 * (h % 2):64 * (h % 2) + 64, 8 + h // 2, :],
                                              qk[64 * (h % 2):64 * (h % 2) + 64, 12 + h // 2, :]),
                          cc("neg_causal"), rows[0:8, 7, :], False)
                out_product("w_out_2", l)

            def cross(l):
                norm_sum()
                first_products("cross_wq_2", l, (0, 1), DC, columns)
                to_channels("cross_wq_2", l, 2, bank_of(2))
                if l == 0:
                    norm_sum(3)
                to_channels("cross_wq_2", l, 3, bank_of(3))
                pe.wait_ge(sem("mem_split"), W.next("mem_split", 4))
                for s in range(4):
                    pe.wait_ge(sem("evac"), W.next("evac"))
                    to_channels("cross_wk_2", l, s, bank_of(s), src=(memH, memL))
                for s in range(4):
                    pe.wait_ge(sem("evac"), W.next("evac"))
                    to_tokens("cross_wv_2", l, s, bank_of(s), src=(memH, memL))
                pe.wait_ge(sem("evac"), W.next("evac", 4))
                for h in range(5):
                    if h < 4:
                        for t in range(TT):
                            for c in range(2):
                                last = mm(ps[:, 4 + h, t * T:(t + 1) * T], qk[:, 2 * h + c, t * P:(t + 1) * P],
                                          qk[:, 8 + 2 * h + c, :], c == 0, c == 1)
                        last.then_inc(sem("score_done"), 1)
                    if h >= 1:
                        hh = h - 1
                        pe.wait_ge(sem("prob_ready"), W.next("prob_ready"))
                        for t in range(TT):
                            for m in range(2):
                                last = pe.transpose(ps[:, 4 + hh, (2 * m + t) * P:(2 * m + t + 1) * P],
                                                    prob[:, hh % 2, 0, (2 * t + m) * P:(2 * t + m + 1) * P], ident)
                        last.then_inc(sem("prob_turned"), 1)
                        pe.wait_ge(sem("probT_ready"), W.next("probT_ready"))
                        for c in range(2):
                            for m in range(2):
                                last = mm(ps[:, hh, c * T:(c + 1) * T],
                                          v_tok[:, m, hh * T + c * P:hh * T + (c + 1) * P],
                                          probT[:, hh % 2, m * T:(m + 1) * T], m == 0, m == 1)
                        last.then_inc(sem("o_ready"), 1)
                out_product("cross_wo_2", l)

            def turn_in(rows_, name):
                for b in range(4):
                    for c in range(2):
                        for t in range(TT):
                            last = pe.transpose(ps[:, 4 + b, c * T + t * P:c * T + (t + 1) * P],
                                                rows_[:, t, (2 * b + c) * P:(2 * b + c + 1) * P], ident)
                    last.then_inc(sem(name), 1)

            pe.wait_ge(sem("ident_in"), W.next("ident_in", 16))
            pe.wait_ge(sem("ones_set"), W.next("ones_set"))
            pe.wait_ge(sem("x_in"), W.next("x_in", 16))
            turn_in(x_rows, "x_turned")
            pe.wait_ge(sem("x_ready"), W.next("x_ready", 4))
            pe.wait_ge(sem("mem_in"), W.next("mem_in", 16))
            turn_in(mem_rows, "mem_turned")
            pe.wait_ge(sem("vec_in"), W.next("vec_in", 16 * (len(VROWS) + 3)))
            pe.transpose(ps[:, 0, 0:P], vec_rows, ident)
            pe.transpose(ps[:, 0, P:NVEC], vec_rows2[0:NVEC - P, :], ident[0:NVEC - P, 0:NVEC - P])
            mm(ps[:, 0, 256:288], ones[0:1, 0:P], brow, True, True).then_inc(sem("vec_turned"), 1)
            pe.wait_ge(sem("lambda_ready"), W.next("lambda_ready"))
            mm(ps[:, 1, 0:1], ones[0:1, 0:P], lwork[:, 130:131], True, True).then_inc(sem("lambda_spread"), 1)
            pe.wait_ge(sem("params_ready"), W.next("params_ready"))
            pe.wait_ge(sem("const_in"), W.next("const_in", 16))

            for kind, i in parts:
                scope[0] = kind[:3] + "_"
                {"gdn": gdn, "mlstm": mlstm, "diff": diff, "mlp": mlp, "hybrid": hybrid, "cross": cross,
                 "ffn1": lambda l: ffn("ffn1", l), "ffn2": lambda l: ffn("ffn2", l)}[kind](i)
            norm_sum()
            pe.wait_ge(sem("h_ready"), DC * (len(parts) + 1))
            for t in range(TT):
                for c in range(DC):
                    last = pe.transpose(ps[:, 2 * t + c // 4, (c % 4) * P:(c % 4 + 1) * P],
                                        hT[:, c, t * P:(t + 1) * P], ident)
                last.then_inc(sem("out_turned"), 1)

        @block.scalar
        def _(act):
            scope[0] = ""
            W = Waits(act, "act_step")
            f = act.activation

            split_upto = [0]

            def split(upto):
                for n in range(split_upto[0], min(upto, len(slabs))):
                    act.wait_ge(sem(f"slab_in{n % RING}"), landed[n])
                    if n >= PARTS:
                        act.wait_ge(sem("products_done"), slabs[n - PARTS][5])
                    f(wH[:, n % PARTS, :], ring[:, n % RING, :], ACT.Copy).then_inc(sem("high_split"), 1)
                split_upto[0] = max(split_upto[0], upto)

            def ready(name, layer, j, g=0, ahead=True):
                n = slab_no[(name, layer, j)]
                if ahead:
                    split(n + PARTS)
                act.wait_ge(sem("products_done"), group(name, layer, j, g))
                if ahead and g == slabs[n][4] - 1:
                    split(n + PARTS + 1)

            def ln_exp():
                act.preload_act_table_set("natural_log_exp_and_others")

            def rsqrt(src, dst, n, name):
                W.chain(f(dst, src, ACT.Ln, scale=1.0 / n, bias=epsc[:, :]))
                f(dst, dst, ACT.Exp, scale=-0.5).then_inc(sem(name), 1)

            def norm(src, there, ahead):
                for c in range(4):
                    there(c)
                    f(sq[:, 2 * c:2 * c + 2, :], src(c), ACT.Square).then_inc(sem("sq_ready"), 1)
                split(ahead)
                act.wait_ge(sem("ss_ready"), W.next("ss_ready"))
                rsqrt(ps[:, 7, 0:T], rs[:, :], D, "rs_ready")

            def x_norm(name, layer, j=0):
                ln_exp()
                norm(lambda c: xT[:, 2 * c:2 * c + 2, :], lambda c: act.wait_ge(sem("x_ready"), W.next("x_ready")),
                     slab_no[(name, layer, j)] + PARTS)
                for c in range(4):
                    act.wait_ge(sem("h_ready"), W.next("h_ready", 2))
                    f(hH[:, 2 * c:2 * c + 2, :], hT[:, 2 * c:2 * c + 2, :], ACT.Copy).then_inc(sem("hH_ready"), 1)

            def split_mix(n):
                for c in range(n):
                    act.wait_ge(sem("mixed"), W.next("mixed"))
                    f(hH[:, 2 * c:2 * c + 2, :], hT[:, 2 * c:2 * c + 2, :], ACT.Copy).then_inc(sem("mixH_ready"), 1)

            def post_norm(product):
                norm(lambda c: two(ps[:, c, :]), lambda c: ready(*product(c), ahead=c < 3),
                     slab_no[product(3)[0:3]] + PARTS + 1)

            def head_norm(n, src, taken=None):
                for b in range(n):
                    if taken:
                        act.wait_ge(sem(taken), W.next(taken))
                    f(sq[:, 2 * b:2 * b + 2, :], src(b), ACT.Square).then_inc(sem("sq_ready"), 1)
                for b in range(n):
                    act.wait_ge(sem("hs_ready"), W.next("hs_ready"))
                    rsqrt(ps[:, 4 + b, :], flat(sq[:, 2 * b:2 * b + 2, :]), P, "hrs_ready")

            def flat(v):
                return v.rearrange("p c t -> p (c t)")

            def channels(name, layer, j, bank0, dst, func=ACT.Copy, scale=1.0):
                for g in range(2):
                    ready(name, layer, 2 * j + g)
                    f(dst(g), two(ps[:, bank0 + g, :]), func, scale=scale).then_inc(sem("evac"), 1)

            def token_slab(name, layer, j, bank, c0):
                ready(name, layer, j)
                f(v_tok[:, :, c0:c0 + T], two(ps[:, bank, :]), ACT.Copy).then_inc(sem("evac"), 1)

            def tokens(name, layer, j, bank0, c0):
                for g in range(2):
                    token_slab(name, layer, 2 * j + g, bank0 + g, c0 + T * g)

            def chunks(v, c):
                return lambda g: v[:, c + 2 * g:c + 2 * g + 2, :]

            def out_key(name, layer):
                return lambda c: (name, layer, c)

            def mlp(i):
                x_norm("mlp_w1", i)
                for g in range(16):
                    ready("mlp_w1", i, g)
                    f(act_s[:, g % 2, :], ps[:, 4 + g % 4, :], ACT.Relu).then_inc(sem("act_ready"), 1)
                    if g >= 1:
                        hidden_high(g - 1)
                hidden_high(15)
                post_norm(lambda c: ("mlp_w2", i, 15, c))

            def hidden_high(g):
                act.wait_ge(sem("bank_read"), W.next("bank_read"))
                f(hidH[:, 2 * g:2 * g + 2, :], two(prod_s[:, g % 2, :]), ACT.Copy).then_inc(sem("hiddenH_ready"), 1)

            def ffn(kind, l):
                def hidden_high(n):
                    act.wait_ge(sem("bank_read"), W.next("bank_read"))
                    f(hidH[:, n, :], prod_s[:, n % 2, 0:T], ACT.Copy).then_inc(sem("hiddenH_ready"), 1)

                x_norm(kind, l)
                for n in range(22):
                    ready(kind, l, n)
                    f(act_s[:, n % 2, 0:T], ps[:, 4 + n % 4, 0:T], ACT.Silu).then_inc(sem("act_ready"), 1)
                    if n >= 1:
                        hidden_high(n - 1)
                hidden_high(21)
                for c in range(4):
                    split(slab_no[(f"{kind}_w_down_2", l, 10)] + PARTS)

            def gdn(i):
                j = i // 3
                x_norm("gdn_w_in", j)
                split(slab_no[("gdn_w_in", j, 0)] + PARTS + 1)
                act.wait_ge(sem("tok_raw"), W.next("tok_raw"))
                W.chain(f(tokg[:, 32:48], tokg[:, 16:32], ACT.Abs))
                W.chain(f(tokg[:, 32:48], tokg[:, 32:48], ACT.Exp, scale=-1.0))
                f(tokg[:, 32:48], tokg[:, 32:48], ACT.Ln, bias=1.0)
                f(tokg[:, 64:72], bcast[:, 8 * j:8 * j + 8], ACT.Exp)
                f(tokg[:, 48:64], tokg[:, 48:64], ACT.Exp, scale=-1.0).then_inc(sem("tok_exp"), 1)
                act.wait_ge(sem("pad_set"), W.next("pad_set"))

                def silu(g):
                    act.wait_ge(sem("conv_done"), W.next("conv_done"))
                    if g < 8:
                        dst = qk[:, 2 * g:2 * g + 2, :]
                    else:
                        if g >= 10:
                            move(g - 10)
                        dst = vch[:, g % 2, :, :]
                    f(dst, conv[:, g % 2, :, :], ACT.Silu).then_inc(sem("silu_done"), 1)

                def move(g):
                    act.wait_ge(sem("v_turned"), W.next("v_turned"))
                    f(v_tok[:, :, T * g:T * (g + 1)], ps[:, 2, :].rearrange("p (i n) -> p i n", i=TT),
                      ACT.Copy).then_inc(sem("v_done"), 1)

                for g in range(16):
                    ready("gdn_w_in", j, g)
                    if 2 <= g < 12:
                        silu(g - 2)
                    if g < 12:
                        f(pre[:, g % 2, :, 3:3 + T], two(ps[:, 4 + g % 4, :]), ACT.Copy).then_inc(sem("evac"), 1)
                    else:
                        c = 2 * (g - 12)
                        f(gate[:, c:c + 2, :], two(ps[:, 4 + g % 4, :]), ACT.Silu).then_inc(sem("evac"), 1)
                        if g == 13:
                            silu(10)
                            silu(11)
                move(2)
                move(3)
                ln_exp()
                for h in range(8):
                    act.wait_ge(sem("decay_done"), W.next("decay_done"))
                    f(pair[:, h, :], ps[:, 4 + h % 2, 0:ED], ACT.Exp).then_inc(sem("pair_exp"), 1)
                for half in range(2):
                    for b in range(4):
                        if half:
                            act.wait_ge(sem("qk_normed"), W.next("qk_normed"))
                        c = 8 * half + 2 * b
                        f(sq[:, 2 * b:2 * b + 2, :], qk[:, c:c + 2, :], ACT.Square).then_inc(sem("sq_ready"), 1)
                    for b in range(4):
                        act.wait_ge(sem("hs_ready"), W.next("hs_ready"))
                        v = flat(sq[:, 2 * b:2 * b + 2, :])
                        f(v, ps[:, b, :], ACT.Ln, bias=epsc[:, :]).then_inc(sem("hs_free"), 1)
                        act.wait_ge(sem("hs_free"), W.next("hs_free"))
                        f(v, v, ACT.Exp, scale=-0.5).then_inc(sem("hrs_ready"), 1)
                act.wait_ge(sem("qk_normed"), W.next("qk_normed", 4))
                head_norm(4, lambda b: two(ps[:, b, :]), "o_ready")
                split_mix(4)
                post_norm(out_key("gdn_w_out", j))

            def mlstm(i):
                x_norm("mlstm_w_in", 0)
                channels("mlstm_w_in", 0, 0, 4, chunks(qk, 0), scale=0.125)
                channels("mlstm_w_in", 0, 1, 6, chunks(qk, 4))
                act.wait_ge(sem("gates_done"), W.next("gates_done"))
                f(rows[0:8, 0, :], ps[0:8, 0, 0:T], ACT.Tanh, scale=1.0 / 15.0, bias=gb15[:, 0:1])
                W.chain(f(rows[0:8, 1, :], ps[0:8, 0, T:2 * T], ACT.Tanh, scale=1.0 / 15.0, bias=gb15[:, 1:2]))
                ln_exp()
                W.chain(f(rows[0:8, 2, :], rows[0:8, 1, :], ACT.Exp, scale=-15.0))
                f(rows[0:8, 3, :], rows[0:8, 2, :], ACT.Ln, bias=1.0).then_inc(sem("log_ready"), 1)
                tokens("mlstm_w_in", 0, 2, 4, 0)
                tokens("mlstm_w_in", 0, 3, 6, 512)
                channels("mlstm_w_in", 0, 4, 4, chunks(gate, 0), func=ACT.Sigmoid)
                channels("mlstm_w_in", 0, 5, 6, chunks(gate, 4), func=ACT.Sigmoid)
                ln_exp()
                act.wait_ge(sem("rows_ready"), W.next("rows_ready"))
                f(rows[0:8, 8, :], rows[0:8, 9, :], ACT.Exp, scale=-1.0).then_inc(sem("floor_ready"), 1)
                act.wait_ge(sem("rcol_ready"), W.next("rcol_ready"))
                for h in range(8):
                    act.wait_ge(sem("decay_done"), W.next("decay_done"))
                    f(pair[:, h, 0:T], ps[:, h % 2, 0:T], ACT.Exp, bias=rcol[:, 0, h:h + 1])
                    f(pair[:, h, T:ED], ps[:, h % 2, P:T], ACT.Exp, bias=rcol[:, 1, h:h + 1])\
                        .then_inc(sem("pair_exp"), 1)
                for h in range(8):
                    act.wait_ge(sem("den_done"), W.next("den_done"))
                    if h >= 2:
                        act.wait_ge(sem("cell_ready"), W.next("cell_ready"))
                    e = em_s[:, h % 2, 0:T]
                    f(em_s[:, h % 2, T:2 * T], ps[:, 4 + h % 2, T:2 * T], ACT.Copy)
                    f(e, ps[:, 4 + h % 2, 0:T], ACT.Abs).then_inc(sem("em_ready"), 1)
                    act.wait_ge(sem("den_free"), W.next("den_free"))
                    W.chain(f(e, e, ACT.Ln))
                    f(e, e, ACT.Exp, scale=-1.0).then_inc(sem("rden_ready"), 1)
                act.wait_ge(sem("cell_ready"), W.next("cell_ready", 2))
                head_norm(4, lambda b: num_s[:, 2 * b:2 * b + 2, :])
                split_mix(4)
                post_norm(out_key("mlstm_w_out", 0))

            def softmaxes(heads, comps, wide):
                def turned(h):
                    act.wait_ge(sem("prob_turned"), W.next("prob_turned"))
                    f(probT[:, h % 2, 0:ED], ps[:, 3, 0:ED], ACT.Copy).then_inc(sem("probT_ready"), 1)
                    if wide and h % 2:
                        act.wait_ge(sem("o_ready"), W.next("o_ready"))
                        b = h // 2
                        f(num_s[:, 2 * b:2 * b + 2, :], two(ps[:, b % 3, :]), ACT.Copy).then_inc(sem("o_moved"), 1)

                for h in range(heads):
                    for c in range(comps):
                        act.wait_ge(sem("max_ready"), W.next("max_ready"))
                        b = 4 + (comps * h + c) % 4
                        s = stat[:, h % 2, c, :]
                        f(prob[:, h % 2, c, 0:P], ps[:, b, 0:P], ACT.Exp, bias=s[:, 0:1], accum_out=s[:, 2:3])
                        f(prob[:, h % 2, c, P:ED], ps[:, b, P:ED], ACT.Exp, bias=s[:, 1:2], accum_out=s[:, 3:4])\
                            .then_inc(sem("score_free"), 1)
                    if h >= 1:
                        turned(h - 1)
                turned(heads - 1)

            def diff(i):
                x_norm("diff_w_in", 0)
                for g in range(8):
                    ready("diff_w_in", 0, g)
                    if g >= 4:
                        act.wait_ge(sem("roped"), W.next("roped"))
                    f(raw[:, g % 4, :], ps[:, 4 + g % 4, :], ACT.Copy, scale=0.125 if g < 4 else 1.0)\
                        .then_inc(sem("raw_ready"), 1)
                tokens("diff_w_in", 0, 4, 4, 0)
                tokens("diff_w_in", 0, 5, 6, 512)
                softmaxes(8, 2, True)
                act.wait_ge(sem("o_moved"), W.next("o_moved", 4))
                head_norm(4, lambda b: num_s[:, 2 * b:2 * b + 2, :])
                split_mix(4)
                post_norm(out_key("diff_w_out", 0))

            def hybrid(l):
                x_norm("w_in_2", l)
                channels("w_in_2", l, 0, 4, chunks(qk, 0), func=ACT.Silu)
                channels("w_in_2", l, 3, 6, chunks(gate, 0), func=ACT.Silu)
                channels("w_in_2", l, 1, 4, chunks(zcum, 0))
                act.wait_ge(sem("evac"), W.next("evac", 6))
                f(qk[:, 4:8, :], zcum, ACT.Sigmoid, scale=-1.0).then_inc(sem("hk_ready"), 1)
                split(slab_no[("w_in_2", l, 4)] + PARTS + 1)
                ln_exp()
                W.chain(f(glog, zcum, ACT.Abs))
                W.chain(f(glog, glog, ACT.Exp, scale=-1.0))
                f(glog, glog, ACT.Ln, bias=1.0).then_inc(sem("glog_ready"), 1)
                act.wait_ge(sem("fz_ready"), W.next("fz_ready"))
                W.chain(f(rows[0:8, 2, :], rows[0:8, 1, :], ACT.Abs))
                W.chain(f(rows[0:8, 2, :], rows[0:8, 2, :], ACT.Exp, scale=-1.0))
                f(rows[0:8, 3, :], rows[0:8, 2, :], ACT.Ln, bias=1.0).then_inc(sem("log_ready"), 1)
                token_slab("w_in_2", l, 4, 6, 0)
                if l:
                    act.wait_ge(sem("lse_ready"), W.next("lse_ready"))
                    v = factor[:, 0, :, :]
                    W.chain(f(v, v, ACT.Abs))
                    W.chain(f(v, v, ACT.Exp, scale=-1.0))
                    f(v, v, ACT.Ln, bias=1.0).then_inc(sem("lse_done"), 1)
                token_slab("w_in_2", l, 5, 7, T)

                def attention_slab(s):
                    if s >= 12:
                        token_slab("w_in_2", l, s, (s - 7) % 4, 512 + T * (s - 12))
                        return
                    ready("w_in_2", l, s)
                    f(qk[:, 8 + 2 * (s - 8):10 + 2 * (s - 8), :], two(ps[:, (s - 7) % 4, :]), ACT.Copy,
                      scale=0.125 if s < 10 else 1.0).then_inc(sem("evac"), 1)

                def decays(n):
                    act.wait_ge(sem("edge_ready"), W.next("edge_ready"))
                    f(factor[:, n % 2, :, :], factor[:, n % 2, :, :], ACT.Exp).then_inc(sem("factor_exp"), 1)

                decays(0)
                attention_slab(8)
                for n in range(1, len(TREE) + 1):
                    decays(n)
                    if n - 1 in BETWEEN_LEVELS:
                        attention_slab(BETWEEN_LEVELS[n - 1])
                W.next("evac", 8)
                head_norm(2, lambda b: two(ps[:, b, :]), "o_ready")
                split_mix(2)
                softmaxes(8, 1, False)
                for b in range(2):
                    act.wait_ge(sem("o_ready"), W.next("o_ready"))
                    f(hH[:, 4 + 2 * b:6 + 2 * b, :], two(ps[:, 1 + b, :]), ACT.Copy).then_inc(sem("mixH_ready"), 1)
                split(slab_no[("w_out_2", l, 3)] + PARTS)

            def cross(l):
                x_norm("cross_wq_2", l)
                if l == 0:
                    for c in range(4):
                        f(sq[:, 2 * c:2 * c + 2, :], memT[:, 2 * c:2 * c + 2, :], ACT.Square)\
                            .then_inc(sem("sq_ready"), 1)
                channels("cross_wq_2", l, 0, 4, chunks(qk, 0), scale=0.0625)
                if l == 0:
                    act.wait_ge(sem("ss_ready"), W.next("ss_ready"))
                    rsqrt(ps[:, 3, 0:T], rs_mem[:, :], D, "mem_rs")
                for c in range(4):
                    act.wait_ge(sem("mem_normed"), W.next("mem_normed", 2))
                    f(memH[:, 2 * c:2 * c + 2, :], mem_n[:, 2 * c:2 * c + 2, :], ACT.Copy)\
                        .then_inc(sem("memH_ready"), 1)
                channels("cross_wq_2", l, 1, 6, chunks(qk, 4), scale=0.0625)
                channels("cross_wk_2", l, 0, 4, chunks(qk, 8))
                channels("cross_wk_2", l, 1, 6, chunks(qk, 12))
                tokens("cross_wv_2", l, 0, 4, 0)
                tokens("cross_wv_2", l, 1, 6, 512)

                def tail(h):
                    act.wait_ge(sem("prob_turned"), W.next("prob_turned"))
                    f(probT[:, h % 2, :], ps[:, 4 + h, :], ACT.Copy).then_inc(sem("probT_ready"), 1)
                    act.wait_ge(sem("o_ready"), W.next("o_ready"))
                    f(hH[:, 2 * h:2 * h + 2, :], two(ps[:, h, :]), ACT.Copy).then_inc(sem("mixH_ready"), 1)

                for h in range(4):
                    act.wait_ge(sem("max_ready"), W.next("max_ready"))
                    for t in range(TT):
                        last = f(prob[:, h % 2, 0, t * T:(t + 1) * T], ps[:, 4 + h, t * T:(t + 1) * T], ACT.Exp,
                                 bias=stat[:, h % 2, 0, t:t + 1], accum_out=stat[:, h % 2, 0, 2 + t:3 + t])
                    last.then_inc(sem("score_free"), 1)
                    if h >= 1:
                        tail(h - 1)
                tail(3)
                split(slab_no[("cross_wo_2", l, 3)] + PARTS)

            ln_exp()
            split(1)
            act.wait_ge(sem("ones_set"), W.next("ones_set"))
            act.wait_ge(sem("lambda_sums"), W.next("lambda_sums"))
            f(lwork[:, 130:132], lwork[:, 128:130], ACT.Exp).then_inc(sem("lambda_exp"), 1)
            act.wait_ge(sem("lb_diff"), W.next("lb_diff"))
            W.chain(f(lb[:, 4:8], lb[:, 0:4], ACT.Abs))
            W.chain(f(lb[:, 4:8], lb[:, 4:8], ACT.Exp, scale=-1.0))
            f(lb[:, 8:12], lb[:, 4:8], ACT.Ln, bias=1.0).then_inc(sem("lb_log"), 1)
            act.wait_ge(sem("lb_ready"), W.next("lb_ready"))
            f(lb[:, 24:28], lb[:, 16:20], ACT.Exp).then_inc(sem("lb_prob"), 1)
            for kind, i in parts:
                scope[0] = kind[:3] + "_"
                {"gdn": gdn, "mlstm": mlstm, "diff": diff, "mlp": mlp, "hybrid": hybrid, "cross": cross,
                 "ffn1": lambda l: ffn("ffn1", l), "ffn2": lambda l: ffn("ffn2", l)}[kind](i)
            norm(lambda c: xT[:, 2 * c:2 * c + 2, :], lambda c: act.wait_ge(sem("x_ready"), W.next("x_ready")),
                 len(slabs))
            for t in range(TT):
                act.wait_ge(sem("out_turned"), W.next("out_turned"))
                f(out_rows[:, t, :], ps[:, 2 * t:2 * t + 2, :].rearrange("p b n -> p (b n)"), ACT.Copy)\
                    .then_inc(sem("out_tile"), 1)

        @block.vector
        def _(dve):
            scope[0] = ""
            W = Waits(dve, "dve_step")
            tt, ts, stt = dve.tensor_tensor, dve.tensor_scalar, dve.scalar_tensor_tensor

            split_upto = [0]

            def split(upto):
                for n in range(split_upto[0], min(upto, len(slabs))):
                    dve.wait_ge(sem("high_split"), n + 1)
                    tt(wL[:, n % PARTS, :], ring[:, n % RING, :], wH[:, n % PARTS, :].bitcast(F32), ALU.subtract)\
                        .then_inc(sem("low_split"), 1)
                split_upto[0] = max(split_upto[0], upto)

            def refill(name, layer, j):
                split(slab_no[(name, layer, j)] + PARTS + 1)

            def x_norm(gain, k0, name=None, layer=0, j=0):
                dve.wait_ge(sem("rs_ready"), W.next("rs_ready"))
                for c in range(DC):
                    stt(hT[:, c, :], xT[:, c, :], column(gain, k0 + c), rs[:, :], ALU.mult, ALU.mult)\
                        .then_inc(sem("h_ready"), 1)
                for c in range(4 if name else 0):
                    dve.wait_ge(sem("hH_ready"), W.next("hH_ready"))
                    v = slice(2 * c, 2 * c + 2)
                    tt(hL[:, v, :], hT[:, v, :], hH[:, v, :].bitcast(F32), ALU.subtract).then_inc(sem("hL_ready"), 1)
                if name:
                    split(slab_no[(name, layer, j)] + PARTS)

            def split_mix(n):
                for c in range(n):
                    dve.wait_ge(sem("mixH_ready"), W.next("mixH_ready"))
                    v = slice(2 * c, 2 * c + 2)
                    tt(hL[:, v, :], hT[:, v, :], hH[:, v, :].bitcast(F32), ALU.subtract)\
                        .then_inc(sem("mixL_ready"), 1)

            def split_bank(c, bank):
                dve.wait_ge(sem("mixH_ready"), W.next("mixH_ready"))
                v = slice(c, c + 2)
                tt(hL[:, v, :], two(ps[:, bank, :]), hH[:, v, :].bitcast(F32), ALU.subtract)\
                    .then_inc(sem("mixL_ready"), 1)

            def post_norm(k0):
                dve.wait_ge(sem("rs_ready"), W.next("rs_ready"))
                for c in range(4):
                    for k in (2 * c, 2 * c + 1):
                        ins = stt(sq[:, k, :], ps[:, c, (k % 2) * T:(k % 2 + 1) * T], column("norm_g", k0 + k),
                                  rs[:, :], ALU.mult, ALU.mult)
                    W.chain(ins)
                    tt(xT[:, 2 * c:2 * c + 2, :], xT[:, 2 * c:2 * c + 2, :], sq[:, 2 * c:2 * c + 2, :], ALU.add)\
                        .then_inc(sem("x_ready"), 1)

            def residual(scale, product):
                for c in range(4):
                    dve.wait_ge(sem("products_done"), group(*product(c)))
                    x = xT[:, 2 * c:2 * c + 2, :]
                    stt(x, two(ps[:, c, :]), scale, x, ALU.mult, ALU.add).then_inc(sem("x_ready"), 1)

            def mlp(i):
                x_norm("norm_g", (4 * i + 2) * DC, "mlp_w1", i)
                def hidden_low(g):
                    dve.wait_ge(sem("hiddenH_ready"), W.next("hiddenH_ready"))
                    v = slice(2 * g, 2 * g + 2)
                    tt(hidL[:, v, :], two(prod_s[:, g % 2, :]), hidH[:, v, :].bitcast(F32), ALU.subtract)\
                        .then_inc(sem("hidden_ready"), 1)

                for g in range(16):
                    refill("mlp_w1", i, g)
                    if g >= 2:
                        dve.wait_ge(sem("hidden_ready"), W.next("hidden_ready"))
                    dve.wait_ge(sem("act_ready"), W.next("act_ready"))
                    tt(prod_s[:, g % 2, :], act_s[:, g % 2, :], ps[:, 4 + g % 4, :], ALU.mult)\
                        .then_inc(sem("bank_read"), 1)
                    if g >= 1:
                        hidden_low(g - 1)
                hidden_low(15)
                W.next("hidden_ready", 2)
                refill("mlp_w2", i, 14)
                post_norm((4 * i + 3) * DC)

            def ffn(kind, l):
                x_norm(f"{kind}_norm_2", l * DC, kind, l)
                def hidden_low(n):
                    dve.wait_ge(sem("hiddenH_ready"), W.next("hiddenH_ready"))
                    tt(hidL[:, n, :], prod_s[:, n % 2, 0:T], hidH[:, n, :].bitcast(F32), ALU.subtract)\
                        .then_inc(sem("hidden_ready"), 1)

                for n in range(22):
                    refill(kind, l, n)
                    if n >= 2:
                        dve.wait_ge(sem("hidden_ready"), W.next("hidden_ready"))
                    dve.wait_ge(sem("act_ready"), W.next("act_ready"))
                    tt(prod_s[:, n % 2, 0:T], act_s[:, n % 2, 0:T], ps[:, 4 + n % 4, T:2 * T], ALU.mult)\
                        .then_inc(sem("bank_read"), 1)
                    if n >= 1:
                        hidden_low(n - 1)
                hidden_low(21)
                W.next("hidden_ready", 2)
                refill(f"{kind}_w_down_2", l, 9)
                residual(0.5, lambda c: (f"{kind}_w_down_2", l, 10, c))

            def head_out(n, src, gain, gated):
                for b in range(n):
                    dve.wait_ge(sem("hrs_ready"), W.next("hrs_ready"))
                    for k in (2 * b, 2 * b + 1):
                        s, r = src(k), sq[:, k, :]
                        ins = stt(r if gated else hT[:, k, :], s, gain(k), r, ALU.mult, ALU.mult)
                    if gated:
                        W.chain(ins)
                        ins = tt(hT[:, 2 * b:2 * b + 2, :], sq[:, 2 * b:2 * b + 2, :], gate[:, 2 * b:2 * b + 2, :],
                                 ALU.mult)
                    ins.then_inc(sem("mixed"), 1)
                split_mix(n)

            def in_bank(k):
                return ps[:, k // 2, (k % 2) * T:(k % 2 + 1) * T]

            def gdn(i):
                j, no = i // 3, gdn_no[i]
                dve.wait_ge(sem("conv_turned"), W.next("conv_turned"))
                W.chain(dve.tensor_copy(convw, ps[:, 3, 0:96]))
                x_norm("norm_g", 4 * i * DC, "gdn_w_in", j)
                refill("gdn_w_in", j, 0)
                dve.wait_ge(sem("gates_done"), W.next("gates_done"))
                ab = ps[:, 3, 128:160].rearrange("p (t n) -> p t n", t=TT)

                def th(a):
                    return tokg[:, a:a + 16].rearrange("p (t h) -> p t h", t=TT)

                tt(th(16), ab[:, :, 0:8], bcast[:, 16 + 8 * j:24 + 8 * j][:, None, :].broadcast_to([P, TT, 8]), ALU.add)
                dve.tensor_copy(th(48), ab[:, :, 8:16]).then_inc(sem("tok_raw"), 1)
                dve.wait_ge(sem("tok_exp"), W.next("tok_exp"))
                W.chain(stt(tokg[:, 16:32], tokg[:, 16:32], 0.0, tokg[:, 32:48], ALU.max, ALU.add))
                stt(th(0), th(16), -1.0, tokg[:, 64:72][:, None, :].broadcast_to([P, TT, 8]), ALU.mult, ALU.mult)
                W.chain(ts(tokg[:, 48:64], tokg[:, 48:64], 1.0, None, ALU.add))
                dve.reciprocal(tokg[:, 80:96], tokg[:, 48:64]).then_inc(sem("tok_gates"), 1)
                for g in range(12):
                    refill("gdn_w_in", j, g)
                    dve.wait_ge(sem("evac"), W.next("evac"))
                    if g >= 2:
                        dve.wait_ge(sem("silu_done"), W.next("silu_done"))
                    b = g % 2
                    done = [0, 0]
                    for k in (3, 2, 1, 0):
                        for c in range(2):
                            w = convw[:, k * 24 + 2 * g + c:k * 24 + 2 * g + c + 1]
                            src, dst = pre[:, b, c, k:k + T], conv[:, b, c, :]
                            if k == 3:
                                done[c] = W.mark(ts(dst, src, w, None, ALU.mult))
                            else:
                                dve.wait_ge(sem("dve_step"), done[c])
                                ins = stt(dst, src, w, dst, ALU.mult, ALU.add)
                                if k or not c:
                                    done[c] = W.mark(ins)
                    ins.then_inc(sem("conv_done"), 1)
                refill("gdn_w_in", j, 15)
                dve.wait_ge(sem("silu_done"), W.next("silu_done", 2))
                dve.wait_ge(sem("evac"), W.next("evac", 4))
                for b in range(8):
                    dve.wait_ge(sem("hrs_ready"), W.next("hrs_ready"))
                    c = 2 * b
                    v = qk[:, c:c + 2, :]
                    tt(v, v, sq[:, c % 8:c % 8 + 2, :], ALU.mult).then_inc(sem("qk_normed"), 1)
                for h in range(8):
                    dve.wait_ge(sem("score_done"), W.next("score_done"))
                    dve.wait_ge(sem("pair_masked"), W.next("pair_masked"))
                    for t, (a, e) in enumerate(((0, T), (T, ED))):
                        ins = stt(kkb[:, h, a:e], ps[:, h % 4, a:e], tokg[:, 80 + 8 * t + h:81 + 8 * t + h],
                                  pair[:, h, a:e], ALU.mult, ALU.mult)
                    ins.then_inc(sem("score_free"), 1)
                for h in range(8):
                    dve.wait_ge(sem("score_done"), W.next("score_done"))
                    stt(pair[:, h, :], ps[:, h % 4, 0:ED], P ** -0.5, pair[:, h, :], ALU.mult, ALU.mult)\
                        .then_inc(sem("score_free"), 1)
                for n in range(len(TREE)):
                    m = cc("tree_ts", n)[:, None, :].broadcast_to([P, 4, P])
                    for q in range(4):
                        t, h0 = q // 2, 4 * (q % 2)
                        dve.wait_ge(sem("level_done"), W.next("level_done"))
                        tt(level[:, t, h0:h0 + 4, :], ps[:, 4 + q, :].rearrange("p (h n) -> p h n", h=4), m, ALU.mult)\
                            .then_inc(sem("level_masked"), 1)
                    for q in range(4):
                        t, h0 = q // 2, 4 * (q % 2)
                        dve.wait_ge(sem("delta_done"), W.next("delta_done"))
                        for bank, x in ((2 * (q % 2), inv), (2 * (q % 2) + 1, invT)):
                            if x is inv and n == len(TREE) - 1:
                                continue
                            v = x[:, t, h0:h0 + 4, :]
                            ins = tt(v, v, ps[:, bank, :].rearrange("p (h n) -> p h n", h=4), ALU.subtract)
                        ins.then_inc(sem("inverse_done"), 1)

                def times_beta(t, b, bank):
                    return tt(u_sol[:, t, 512 * b:512 * (b + 1)].rearrange("p (h n) -> p h n", h=4),
                              ps[:, bank, :].rearrange("p (h n) -> p h n", h=4),
                              tokg[:, 80 + 8 * t + 4 * b:84 + 8 * t + 4 * b][:, :, None].broadcast_to([P, 4, P]),
                              ALU.mult)

                for b in range(2):
                    dve.wait_ge(sem("w_done"), W.next("w_done"))
                    dve.tensor_copy(w_sol[:, 0, 512 * b:512 * (b + 1)], ps[:, 4 + b, :]).then_inc(sem("w_ready"), 1)
                    times_beta(0, b, 4 + b)
                for b in range(2):
                    dve.wait_ge(sem("w_done"), W.next("w_done"))
                    v = v_tok[:, 1, 512 * b:512 * (b + 1)]
                    tt(v, v, ps[:, 6 + b, :], ALU.subtract).then_inc(sem("w_ready"), 1)
                for b in range(2):
                    dve.wait_ge(sem("w_done"), W.next("w_done"))
                    times_beta(1, b, 4 + b).then_inc(sem("w_ready"), 1)
                head_out(4, in_bank, lambda k: column("gdn_norm_g", j), True)
                refill("gdn_w_out", j, 2)
                post_norm((4 * i + 1) * DC)

            def mlstm(i):
                dve.wait_ge(sem("gates_in"), GATE_LOADS)
                ts(gb15[:, :], gbias[:, :], 1.0 / 15.0, None, ALU.mult)
                x_norm("norm_g", 4 * i * DC, "mlstm_w_in", 0)
                r = lambda k: rows[0:8, k, :]
                one = ones[0:8, :]
                refill("mlstm_w_in", 0, 3)
                dve.wait_ge(sem("log_ready"), W.next("log_ready"))
                W.chain(dve.tensor_tensor_scan(r(4), one, r(3), 0.0, ALU.mult, ALU.subtract))
                W.chain(stt(r(6), r(0), 15.0, r(4), ALU.mult, ALU.subtract))
                W.chain(dve.tensor_tensor_scan(r(5), one, r(6), 0.0, ALU.mult, ALU.max))
                ts(r(7), r(5), -1.0, None, ALU.mult)
                tt(r(9), r(4), r(5), ALU.add).then_inc(sem("rows_ready"), 1)
                refill("mlstm_w_in", 0, 11)
                dve.wait_ge(sem("r_turned"), W.next("r_turned"))
                dve.tensor_copy(rcol.rearrange("p i h -> p (i h)"), ps[:, 1, 0:16]).then_inc(sem("rcol_ready"), 1)
                for h in range(8):
                    dve.wait_ge(sem("score_done"), W.next("score_done"))
                    dve.wait_ge(sem("pair_masked"), W.next("pair_masked"))
                    tt(pair[:, h, :], ps[:, 4 + h % 4, 0:ED], pair[:, h, :], ALU.mult).then_inc(sem("score_free"), 1)
                for h in range(8):
                    dve.wait_ge(sem("em_ready"), W.next("em_ready"))
                    e = em_s[:, h % 2, 0:T]
                    tt(e, e, em_s[:, h % 2, T:2 * T], ALU.max).then_inc(sem("den_free"), 1)
                    dve.wait_ge(sem("rden_ready"), W.next("rden_ready"))
                    tt(num_s[:, h, :], in_bank(h), e, ALU.mult).then_inc(sem("cell_ready"), 1)
                head_out(4, lambda k: num_s[:, k, :], lambda k: column("mlstm_norm_g", k), True)
                refill("mlstm_w_out", 0, 2)
                post_norm((4 * i + 1) * DC)

            def softmaxes(heads, comps):
                def normalize(h):
                    dve.wait_ge(sem("score_free"), W.next("score_free", comps))
                    s = stat[:, h % 2, :, :]
                    W.chain(dve.reciprocal(s[:, 0:comps, 2:4], s[:, 0:comps, 2:4]))
                    if comps == 2:
                        W.chain(ts(s[:, 1, 2:4], s[:, 1, 2:4], bcast[:, 33:34], None, ALU.mult))
                    for k, (a, e) in enumerate(((0, P), (P, ED))):
                        p = prob[:, h % 2, 0, a:e]
                        ins = ts(p, p, s[:, 0, 2 + k:3 + k], None, ALU.mult)
                    if comps == 2:
                        W.chain(ins)
                        for k, (a, e) in enumerate(((0, P), (P, ED))):
                            p = prob[:, h % 2, 1, a:e]
                            ins = stt(p, p, s[:, 1, 2 + k:3 + k], prob[:, h % 2, 0, a:e], ALU.mult, ALU.add)
                    ins.then_inc(sem("prob_ready"), 1)

                for h in range(heads):
                    if h >= 1:
                        normalize(h - 1)
                    for c in range(comps):
                        dve.wait_ge(sem("score_done"), W.next("score_done"))
                        b = 4 + (comps * h + c) % 4
                        for k, (a, e) in enumerate(((0, P), (P, ED))):
                            ins = dve.tensor_reduce(stat[:, h % 2, c, k:k + 1], ps[:, b, a:e], AX, ALU.max,
                                                    negate=True)
                        ins.then_inc(sem("max_ready"), 1)
                normalize(heads - 1)

            def diff(i):
                x_norm("norm_g", 4 * i * DC, "diff_w_in", 0)
                both = lambda name: cc(name)[:, None, :].broadcast_to([P, 2, T])
                for g in range(8):
                    refill("diff_w_in", 0, g)
                    dve.wait_ge(sem("rotated"), W.next("rotated"))
                    v, s = qk[:, 2 * g:2 * g + 2, :], two(probT[:, g % 2, :])
                    tt(v, two(raw[:, g % 4, :]), both("cos"), ALU.mult)
                    W.chain(tt(s, two(ps[:, g % 2, :]), both("sin"), ALU.mult))
                    tt(v, v, s, ALU.add).then_inc(sem("roped"), 1)
                refill("diff_w_in", 0, 11)
                softmaxes(8, 2)
                head_out(4, lambda k: num_s[:, k, :], lambda k: bcast[:, 34:35], False)
                refill("diff_w_out", 0, 2)
                post_norm((4 * i + 1) * DC)

            def hybrid(l):
                x_norm("mix_norm_2", l * DC, "w_in_2", l)
                dve.memset(pair[:, 0:4, :], 0.0)
                r = lambda k: rows[0:8, k, :]
                refill("w_in_2", l, 7)
                dve.wait_ge(sem("gates_done"), W.next("gates_done"))
                ts(r(1), ps[0:8, 0, 0:T], gbias[:, 2 + l:3 + l], None, ALU.add).then_inc(sem("fz_ready"), 1)
                refill("w_in_2", l, 3)
                dve.wait_ge(sem("hk_ready"), W.next("hk_ready"))
                if l:
                    for h in range(4):
                        ts(qk[:, 4 + h, :], qk[:, 4 + h, :], lb[:, 24 + h:25 + h], None, ALU.mult)
                refill("w_in_2", l, 4)
                dve.wait_ge(sem("glog_ready"), W.next("glog_ready"))
                W.chain(stt(glog, zcum, 0.0, glog, ALU.min, ALU.subtract))
                dve.wait_ge(sem("log_ready"), W.next("log_ready"))
                W.chain(stt(r(4), r(1), 0.0, r(3), ALU.min, ALU.subtract))
                W.chain(dve.tensor_tensor_scan(r(5), ones[0:8, :], r(4), 0.0, ALU.mult, ALU.add))
                ts(r(7), r(5), -1.0, None, ALU.mult).then_inc(sem("rows_ready"), 1)
                if l:
                    for h in range(4):
                        ins = ts(glog[:, h, :], glog[:, h, :], lb[:, 16 + h:17 + h], None, ALU.add)
                    W.chain(ins)
                    for h in range(4):
                        ins = ts(factor[:, 0, h, :], glog[:, h, :], lb[:, 12 + h:13 + h], None, ALU.subtract)
                    ins.then_inc(sem("lse_ready"), 1)
                    dve.wait_ge(sem("lse_done"), W.next("lse_done"))
                    for h in range(4):
                        ins = stt(glog[:, h, :], glog[:, h, :], lb[:, 12 + h:13 + h], factor[:, 0, h, :],
                                  ALU.max, ALU.add)
                    W.chain(ins)
                for h in range(4):
                    ins = dve.tensor_tensor_scan(zcum[:, h, :], ones[:, :], glog[:, h, :], 0.0, ALU.mult, ALU.add)
                W.chain(ins)

                def split(v, m):
                    v = v.rearrange("p h t -> p (h t)").rearrange("p (b n) -> p b n", n=2 * m)
                    return v[:, :, 0:m], v[:, :, m:2 * m], v[:, :, m - 1:m].broadcast_to([P, 4 * T // (2 * m), m])

                spans = TREE + [P]

                def edges(n):
                    gl, gr, edge = split(zcum, spans[n])
                    fl, fr, _ = split(factor[:, n % 2, :, :], spans[n])
                    tt(fl, edge, gl, ALU.subtract)
                    tt(fr, gr, edge, ALU.subtract).then_inc(sem("edge_ready"), 1)

                def apply(n):
                    dve.wait_ge(sem("factor_exp"), W.next("factor_exp"))
                    fl, fr, _ = split(factor[:, n % 2, :, :], spans[n])
                    kl, _, _ = split(qk[:, 4:8, :], spans[n])
                    _, qr, _ = split(qk[:, 0:4, :], spans[n])
                    tt(fl, fl, kl, ALU.mult)
                    tt(fr, fr, qr, ALU.mult).then_inc(sem("factor_ready"), 1)

                def copy_level(n):
                    for t in range(1 if n == len(TREE) else TT):
                        dve.wait_ge(sem("tree_done"), W.next("tree_done"))
                        if tree_m[0] >= 2:
                            dve.wait_ge(sem("tree_copied"), W.next("tree_copied"))
                        data = ps[:, 4 + tree_m[0] % 4, :].rearrange("p (h n) -> p h n", h=4)
                        tree_m[0] += 1
                        if n == len(TREE):
                            dve.tensor_copy(pair[:, 0:4, P:T], data).then_inc(sem("tree_copied"), 1)
                            continue
                        m = ident if n > len(TREE) else cc("tree_st", n)
                        dst = pair[:, 0:4, 0:P] if t == 0 else pair[:, 0:4, T:ED]
                        dve.copy_predicated(dst, m.bitcast(I32)[:, None, :].broadcast_to([P, 4, P]), data)\
                            .then_inc(sem("tree_copied"), 1)

                tree_m = [0]
                edges(0)
                edges(1)
                apply(0)
                refill("w_in_2", l, 5)
                for n in range(len(TREE) + 1):
                    if n + 1 <= len(TREE):
                        apply(n + 1)
                    copy_level(n)
                    if n + 2 <= len(TREE):
                        edges(n + 2)
                    if n in BETWEEN_LEVELS:
                        refill("w_in_2", l, BETWEEN_LEVELS[n] - 1)
                copy_level(len(TREE) + 1)
                refill("w_in_2", l, 13)
                dve.wait_ge(sem("tree_copied"), W.next("tree_copied", 2))
                head_out(2, in_bank, lambda k: column("hgrn_out_norm_2", l), True)
                softmaxes(8, 1)
                for b in range(2):
                    split_bank(4 + 2 * b, 1 + b)
                refill("w_out_2", l, 2)
                residual(1.0, lambda c: ("w_out_2", l, c))

            def cross(l):
                x_norm("cross_norm_2", l * DC, "cross_wq_2", l)
                refill("cross_wq_2", l, 1)
                if l == 0:
                    dve.wait_ge(sem("mem_rs"), W.next("mem_rs"))
                for c in range(DC):
                    stt(mem_n[:, c, :], memT[:, c, :], column("mem_norm_2", l * DC + c), rs_mem[:, :],
                        ALU.mult, ALU.mult).then_inc(sem("mem_normed"), 1)
                for c in range(4):
                    dve.wait_ge(sem("memH_ready"), W.next("memH_ready"))
                    v = slice(2 * c, 2 * c + 2)
                    tt(memL[:, v, :], mem_n[:, v, :], memH[:, v, :].bitcast(F32), ALU.subtract)\
                        .then_inc(sem("mem_split"), 1)
                refill("cross_wv_2", l, 3)

                def normalize(h):
                    dve.wait_ge(sem("score_free"), W.next("score_free"))
                    s = stat[:, h % 2, 0, :]
                    W.chain(dve.reciprocal(s[:, 2:4], s[:, 2:4]))
                    for t in range(TT):
                        p = prob[:, h % 2, 0, t * T:(t + 1) * T]
                        ins = ts(p, p, s[:, 2 + t:3 + t], None, ALU.mult)
                    ins.then_inc(sem("prob_ready"), 1)

                for h in range(4):
                    if h >= 1:
                        normalize(h - 1)
                    dve.wait_ge(sem("score_done"), W.next("score_done"))
                    dve.tensor_reduce(stat[:, h % 2, 0, 0:2], two(ps[:, 4 + h, :]), AX, ALU.max, negate=True)\
                        .then_inc(sem("max_ready"), 1)
                    if h >= 2:
                        split_bank(2 * (h - 2), h - 2)
                normalize(3)
                split_bank(4, 2)
                split_bank(6, 3)
                refill("cross_wo_2", l, 2)
                residual(1.0, lambda c: ("cross_wo_2", l, c))

            for c in range(4):
                dve.wait_ge(sem("x_turned"), W.next("x_turned"))
                dve.tensor_copy(xT[:, 2 * c:2 * c + 2, :], two(ps[:, 4 + c, :])).then_inc(sem("x_ready"), 1)
            for c in range(4):
                dve.wait_ge(sem("mem_turned"), W.next("mem_turned"))
                dve.tensor_copy(memT[:, 2 * c:2 * c + 2, :], two(ps[:, 4 + c, :])).then_inc(sem("mem_ready"), 1)
            dve.wait_ge(sem("vec_turned"), W.next("vec_turned"))
            dve.tensor_copy(vec[:, :], ps[:, 0, 0:NVEC])
            W.chain(dve.tensor_copy(bcast[:, 0:32], ps[:, 0, 256:288]))
            tt(lwork[:, 0:64], lrow[:, 0:64], lrow[:, 64:128], ALU.mult)
            W.chain(tt(lwork[:, 64:128], lrow[:, 128:192], lrow[:, 192:256], ALU.mult))
            dve.tensor_reduce(lwork[:, 128:130], lwork[:, 0:128].rearrange("p (a n) -> p a n", a=2), AX, ALU.add)\
                .then_inc(sem("lambda_sums"), 1)
            k = VCOL["hgrn_lb_2"]
            tt(lb[:, 0:4], vec[:, k:k + 4], vec[:, k + 4:k + 8], ALU.subtract).then_inc(sem("lb_diff"), 1)
            dve.wait_ge(sem("lambda_exp"), W.next("lambda_exp"))
            stt(lwork[:, 130:131], lwork[:, 130:131], LAMBDA_INIT, lwork[:, 131:132], ALU.add, ALU.subtract)\
                .then_inc(sem("lambda_ready"), 1)
            dve.wait_ge(sem("lb_log"), W.next("lb_log"))
            W.chain(ts(lb[:, 20:24], lb[:, 0:4], -1.0, None, ALU.mult))
            stt(lb[:, 12:16], lb[:, 20:24], 0.0, lb[:, 8:12], ALU.min, ALU.subtract)
            stt(lb[:, 16:20], lb[:, 0:4], 0.0, lb[:, 8:12], ALU.min, ALU.subtract).then_inc(sem("lb_ready"), 1)
            dve.wait_ge(sem("lambda_spread"), W.next("lambda_spread"))
            dve.tensor_copy(bcast[:, 32:33], ps[:, 1, 0:1])
            ts(bcast[:, 33:34], ps[:, 1, 0:1], -1.0, None, ALU.mult)
            dve.wait_ge(sem("lb_prob"), W.next("lb_prob"))
            ts(bcast[:, 34:35], column("diff_norm_g", 0), 1.0 - LAMBDA_INIT, None, ALU.mult)\
                .then_inc(sem("params_ready"), 1)
            split(1)
            for kind, i in parts:
                scope[0] = kind[:3] + "_"
                {"gdn": gdn, "mlstm": mlstm, "diff": diff, "mlp": mlp, "hybrid": hybrid, "cross": cross,
                 "ffn1": lambda l: ffn("ffn1", l), "ffn2": lambda l: ffn("ffn2", l)}[kind](i)
            x_norm("final_norm_2", 0)


_INS = ["x", "norm_g", "mlp_w1", "mlp_w2", "gdn_w_in", "gdn_conv", "gdn_a_log", "gdn_dt_bias", "gdn_norm_g",
        "gdn_w_out", "mlstm_w_in", "mlstm_gate_b", "mlstm_norm_g", "mlstm_w_out", "diff_w_in", "diff_lambda",
        "diff_norm_g", "diff_w_out", "mem_2", "ffn1_norm_2", "ffn1_w_gate_2", "ffn1_w_up_2", "ffn1_w_down_2",
        "mix_norm_2", "w_in_2", "hgrn_lb_2", "hgrn_out_norm_2", "fox_f_bias_2", "w_out_2", "cross_norm_2",
        "mem_norm_2", "cross_wq_2", "cross_wk_2", "cross_wv_2", "cross_wo_2", "ffn2_norm_2", "ffn2_w_gate_2",
        "ffn2_w_up_2", "ffn2_w_down_2", "final_norm_2"]


def kernel(**inputs):
    import concourse.bacc as _bacc
    from concourse.bass_utils import run_bass_kernel_spmd as _run

    nc = _bacc.Bacc("TRN2", target_bir_lowering=False, num_devices=1)
    arrays, io = {}, {}
    for name in _INS:
        a = np.ascontiguousarray(inputs[name])
        arrays[f"in_{name}"] = a
        io[name] = nc.dram_tensor(f"in_{name}", a.shape, F32, kind="ExternalInput").ap()
    arrays["shape_constants"] = shape_constants()
    io["shape_constants"] = nc.dram_tensor("shape_constants", (P, NCONST), F32, kind="ExternalInput").ap()
    out = nc.dram_tensor("out", (1, T, D), F32, kind="ExternalOutput").ap()
    program(nc, io, out)
    r = _run(nc, [arrays], core_ids=[0])
    return r.results[0]["out"]
```
